# Optimizing a Trainium2 kernel written in Bass

```python
import math
import jax, jax.numpy as jnp
from jax import lax
import numpy as np

D_MODEL = 1024
BATCH = 1
SEQ = 256
DEPTH = 2

N_MIXERS = 2
N_MLA = (DEPTH + 1) // 2
N_SSM = DEPTH // 2
MLA_HEADS = 8
QK_NOPE = 128
QK_ROPE = 64
V_DIM = 128
Q_LORA = 256
KV_LORA = 128
ROPE_THETA = 10000.0
Q_BLOCK = 128
SSM_WIDTH = D_MODEL
GROUP_CH = 16
N_GROUPS = SSM_WIDTH // GROUP_CH
STATE = 64
DT_MIN = 0.001
DT_MAX = 0.1
D_FF = 4 * D_MODEL
ALPHA = (2 * DEPTH) ** 0.25
BETA = (8 * DEPTH) ** -0.25
LN_EPS = 1e-5
RMS_EPS = 1e-6


def layer_norm(x, g, b):
    xf = x.astype(jnp.float32)
    mu = jnp.mean(xf, axis=-1, keepdims=True)
    var = jnp.mean(jnp.square(xf - mu), axis=-1, keepdims=True)
    y = (xf - mu) * lax.rsqrt(var + LN_EPS) * g.astype(jnp.float32) + b.astype(jnp.float32)
    return y.astype(x.dtype)

def rms_norm(x, g):
    xf = x.astype(jnp.float32)
    y = xf * lax.rsqrt(jnp.mean(jnp.square(xf), axis=-1, keepdims=True) + RMS_EPS) * g.astype(jnp.float32)
    return y.astype(x.dtype)

def rope_tables(positions):
    inv_freq = ROPE_THETA ** (-jnp.arange(0, QK_ROPE, 2, dtype=jnp.float32) / QK_ROPE)
    ang = positions.astype(jnp.float32)[..., None] * inv_freq
    return jnp.cos(ang), jnp.sin(ang)

def apply_rope(x, cos, sin):
    xf = x.astype(jnp.float32)
    x1, x2 = jnp.split(xf, 2, axis=-1)
    return jnp.concatenate([x1 * cos - x2 * sin, x1 * sin + x2 * cos], axis=-1).astype(x.dtype)

def mla_mixer(h, cos, sin, w_in, q_norm, w_qb, kv_norm, w_kvb, w_o):
    B, L, _ = h.shape
    z = h @ w_in
    cq = rms_norm(z[..., :Q_LORA], q_norm)
    ckv = rms_norm(z[..., Q_LORA:Q_LORA + KV_LORA], kv_norm)
    k_pe = apply_rope(z[..., Q_LORA + KV_LORA:], cos, sin)
    q = (cq @ w_qb).reshape(B, L, MLA_HEADS, QK_NOPE + QK_ROPE)
    q_nope = q[..., :QK_NOPE]
    q_pe = apply_rope(q[..., QK_NOPE:], cos[:, :, None, :], sin[:, :, None, :])
    kv = (ckv @ w_kvb).reshape(B, L, MLA_HEADS, QK_NOPE + V_DIM)
    k_nope = kv[..., :QK_NOPE]
    v = kv[..., QK_NOPE:]
    scale = 1.0 / math.sqrt(QK_NOPE + QK_ROPE)
    nb = L // Q_BLOCK
    qn_b = q_nope.reshape(B, nb, Q_BLOCK, MLA_HEADS, QK_NOPE).transpose(1, 0, 2, 3, 4)
    qp_b = q_pe.reshape(B, nb, Q_BLOCK, MLA_HEADS, QK_ROPE).transpose(1, 0, 2, 3, 4)
    k_idx = jnp.arange(L)

    def attend(args):
        qn, qp, start = args
        s = (jnp.einsum('bqhd,bkhd->bhqk', qn, k_nope)
             + jnp.einsum('bqhr,bkr->bhqk', qp, k_pe)).astype(jnp.float32) * scale
        q_idx = start + jnp.arange(Q_BLOCK)
        causal = k_idx[None, :] <= q_idx[:, None]
        s = jnp.where(causal, s, jnp.float32(-1e30))
        p = jax.nn.softmax(s, axis=-1).astype(v.dtype)
        return jnp.einsum('bhqk,bkhd->bqhd', p, v)

    o = lax.map(attend, (qn_b, qp_b, jnp.arange(nb) * Q_BLOCK))
    o = o.transpose(1, 0, 2, 3, 4).reshape(B, L, MLA_HEADS * V_DIM)
    return o @ w_o

def s5_mixer(h, w_in, log_dt, a_re, a_im, b_re, b_im, c_re, c_im, d_skip, w_glu, b_glu, w_out):
    B, L, _ = h.shape
    u = h @ w_in
    u32 = u.astype(jnp.float32).reshape(B, L, N_GROUPS, GROUP_CH)
    lr = a_re.astype(jnp.float32)
    li = a_im.astype(jnp.float32)
    dt = jnp.exp(log_dt.astype(jnp.float32))[:, None]
    mag = jnp.exp(lr * dt)
    ab_re = mag * jnp.cos(li * dt)
    ab_im = mag * jnp.sin(li * dt)
    den = lr * lr + li * li
    nr = ab_re - 1.0
    coef_re = ((nr * lr + ab_im * li) / den)[..., None]
    coef_im = ((ab_im * lr - nr * li) / den)[..., None]
    br = b_re.astype(jnp.float32)
    bi = b_im.astype(jnp.float32)
    bb_re = coef_re * br - coef_im * bi
    bb_im = coef_re * bi + coef_im * br
    bu_re = jnp.einsum('blgc,gpc->blgp', u32, bb_re)
    bu_im = jnp.einsum('blgc,gpc->blgp', u32, bb_im)
    a_re_t = jnp.broadcast_to(ab_re, (1, L, N_GROUPS, STATE))
    a_im_t = jnp.broadcast_to(ab_im, (1, L, N_GROUPS, STATE))

    def combine(e1, e2):
        a1r, a1i, b1r, b1i = e1
        a2r, a2i, b2r, b2i = e2
        return (a2r * a1r - a2i * a1i,
                a2r * a1i + a2i * a1r,
                a2r * b1r - a2i * b1i + b2r,
                a2r * b1i + a2i * b1r + b2i)

    _, _, xr, xi = lax.associative_scan(combine, (a_re_t, a_im_t, bu_re, bu_im), axis=1)
    y = (jnp.einsum('blgp,gcp->blgc', xr, c_re.astype(jnp.float32))
         - jnp.einsum('blgp,gcp->blgc', xi, c_im.astype(jnp.float32)))
    y = y + d_skip.astype(jnp.float32).reshape(N_GROUPS, GROUP_CH) * u32
    y = y.reshape(B, L, SSM_WIDTH).astype(h.dtype)
    g = jax.nn.gelu(y)
    z = g * jax.nn.sigmoid(g @ w_glu + b_glu)
    return z @ w_out

def sq_relu_mlp(h, w1, b1, w2, b2):
    a = jax.nn.relu(h @ w1 + b1)
    return (a * a) @ w2 + b2

def modulation(cs, w, b):
    m = cs @ w + b
    shift, scale, gate = jnp.split(m, 3, axis=-1)
    return shift[:, None, :], scale[:, None, :], gate[:, None, :]

def first_inputs(seed: int = 0) -> dict:
    key = jax.random.key(seed)
    ks = iter(jax.random.split(key, 40))
    f32 = jnp.float32
    nrm = lambda shape, s: jax.random.normal(next(ks), shape, f32) * s
    D = D_MODEL
    x = jax.random.normal(next(ks), (BATCH, SEQ, D), f32)
    c = jax.random.normal(next(ks), (BATCH, D), f32)
    offs = jax.random.randint(next(ks), (BATCH, 1), 0, 1024, dtype=jnp.int32)
    positions = offs + jnp.arange(SEQ, dtype=jnp.int32)[None, :]
    mla_w_in = nrm((N_MLA, D, Q_LORA + KV_LORA + QK_ROPE), D ** -0.5)
    mla_q_norm = 1.0 + nrm((N_MLA, Q_LORA), 0.02)
    mla_w_qb = nrm((N_MLA, Q_LORA, MLA_HEADS * (QK_NOPE + QK_ROPE)), Q_LORA ** -0.5)
    mla_kv_norm = 1.0 + nrm((N_MLA, KV_LORA), 0.02)
    mla_w_kvb = nrm((N_MLA, KV_LORA, MLA_HEADS * (QK_NOPE + V_DIM)), KV_LORA ** -0.5)
    mla_w_o = nrm((N_MLA, MLA_HEADS * V_DIM, D), BETA * (MLA_HEADS * V_DIM) ** -0.5)
    ssm_w_in = nrm((N_SSM, D, SSM_WIDTH), D ** -0.5)
    ssm_log_dt = jax.random.uniform(next(ks), (N_SSM, N_GROUPS), f32,
                                    math.log(DT_MIN), math.log(DT_MAX))
    n_idx = jnp.arange(STATE, dtype=f32)
    ssm_a_re = -0.5 + nrm((N_SSM, N_GROUPS, STATE), 0.01)
    ssm_a_im = math.pi * n_idx + nrm((N_SSM, N_GROUPS, STATE), 0.01)
    ssm_b_re = nrm((N_SSM, N_GROUPS, STATE, GROUP_CH), (2 * GROUP_CH) ** -0.5)
    ssm_b_im = nrm((N_SSM, N_GROUPS, STATE, GROUP_CH), (2 * GROUP_CH) ** -0.5)
    ssm_c_re = nrm((N_SSM, N_GROUPS, GROUP_CH, STATE), (2 * STATE) ** -0.5)
    ssm_c_im = nrm((N_SSM, N_GROUPS, GROUP_CH, STATE), (2 * STATE) ** -0.5)
    ssm_d = nrm((N_SSM, SSM_WIDTH), 1.0)
    ssm_w_glu = nrm((N_SSM, SSM_WIDTH, SSM_WIDTH), SSM_WIDTH ** -0.5)
    ssm_b_glu = nrm((N_SSM, SSM_WIDTH), 0.01)
    ssm_w_out = nrm((N_SSM, SSM_WIDTH, D), BETA * SSM_WIDTH ** -0.5)
    mlp_w1 = nrm((DEPTH, D, D_FF), D ** -0.5)
    mlp_b1 = nrm((DEPTH, D_FF), 0.01)
    mlp_w2 = nrm((DEPTH, D_FF, D), BETA * D_FF ** -0.5)
    mlp_b2 = nrm((DEPTH, D), 0.01)
    mod_mix_w = nrm((DEPTH, D, 3 * D), 0.2 * D ** -0.5)
    mod_mix_b = nrm((DEPTH, 3 * D), 0.01)
    mod_ffn_w = nrm((DEPTH, D, 3 * D), 0.2 * D ** -0.5)
    mod_ffn_b = nrm((DEPTH, 3 * D), 0.01)
    ln_mix_g = 1.0 + nrm((DEPTH, D), 0.02)
    ln_mix_b = nrm((DEPTH, D), 0.01)
    ln_ffn_g = 1.0 + nrm((DEPTH, D), 0.02)
    ln_ffn_b = nrm((DEPTH, D), 0.01)
    return {"x": x, "c": c, "positions": positions,
            "mla_w_in": mla_w_in, "mla_q_norm": mla_q_norm, "mla_w_qb": mla_w_qb,
            "mla_kv_norm": mla_kv_norm, "mla_w_kvb": mla_w_kvb, "mla_w_o": mla_w_o,
            "ssm_w_in": ssm_w_in, "ssm_log_dt": ssm_log_dt, "ssm_a_re": ssm_a_re,
            "ssm_a_im": ssm_a_im, "ssm_b_re": ssm_b_re, "ssm_b_im": ssm_b_im,
            "ssm_c_re": ssm_c_re, "ssm_c_im": ssm_c_im, "ssm_d": ssm_d,
            "ssm_w_glu": ssm_w_glu, "ssm_b_glu": ssm_b_glu, "ssm_w_out": ssm_w_out,
            "mlp_w1": mlp_w1, "mlp_b1": mlp_b1, "mlp_w2": mlp_w2, "mlp_b2": mlp_b2,
            "mod_mix_w": mod_mix_w, "mod_mix_b": mod_mix_b,
            "mod_ffn_w": mod_ffn_w, "mod_ffn_b": mod_ffn_b,
            "ln_mix_g": ln_mix_g, "ln_mix_b": ln_mix_b,
            "ln_ffn_g": ln_ffn_g, "ln_ffn_b": ln_ffn_b}

def first_block(x, c, positions,
              mla_w_in, mla_q_norm, mla_w_qb, mla_kv_norm, mla_w_kvb, mla_w_o,
              ssm_w_in, ssm_log_dt, ssm_a_re, ssm_a_im, ssm_b_re, ssm_b_im,
              ssm_c_re, ssm_c_im, ssm_d, ssm_w_glu, ssm_b_glu, ssm_w_out,
              mlp_w1, mlp_b1, mlp_w2, mlp_b2,
              mod_mix_w, mod_mix_b, mod_ffn_w, mod_ffn_b,
              ln_mix_g, ln_mix_b, ln_ffn_g, ln_ffn_b):
    cs = jax.nn.silu(c)
    cos, sin = rope_tables(positions)
    for i in range(DEPTH):
        shift, scale, gate = modulation(cs, mod_mix_w[i], mod_mix_b[i])
        h = x * (1.0 + scale) + shift
        j = i // N_MIXERS
        if i % N_MIXERS == 0:
            y = mla_mixer(h, cos, sin, mla_w_in[j], mla_q_norm[j], mla_w_qb[j],
                          mla_kv_norm[j], mla_w_kvb[j], mla_w_o[j])
        else:
            y = s5_mixer(h, ssm_w_in[j], ssm_log_dt[j], ssm_a_re[j], ssm_a_im[j],
                         ssm_b_re[j], ssm_b_im[j], ssm_c_re[j], ssm_c_im[j], ssm_d[j],
                         ssm_w_glu[j], ssm_b_glu[j], ssm_w_out[j])
        x = layer_norm(ALPHA * x + (1.0 + gate) * y, ln_mix_g[i], ln_mix_b[i])
        shift, scale, gate = modulation(cs, mod_ffn_w[i], mod_ffn_b[i])
        h = x * (1.0 + scale) + shift
        y = sq_relu_mlp(h, mlp_w1[i], mlp_b1[i], mlp_w2[i], mlp_b2[i])
        x = layer_norm(ALPHA * x + (1.0 + gate) * y, ln_ffn_g[i], ln_ffn_b[i])
    return x


N_A_LAYERS = DEPTH // 2
N_B_LAYERS = DEPTH - N_A_LAYERS
D_FF_2 = 2816
MACARON_WEIGHT = 0.5
D_RNN = D_MODEL
LRU_HEADS = 4
LRU_BLOCK = D_RNN // LRU_HEADS
CONV_WIDTH = 4
LRU_C = 8.0
N_HEADS = 8
HEAD_DIM = D_MODEL // N_HEADS
MOBA_BLOCK = 256
MOBA_TOPK = 3
Q_CHUNK = 16
N_BUCKETS = 32
MAX_DISTANCE = 128


def rms_norm_2(x, g):
    xf = x.astype(jnp.float32)
    y = xf * lax.rsqrt(jnp.mean(xf * xf, axis=-1, keepdims=True) + RMS_EPS)
    return (y * g.astype(jnp.float32)).astype(x.dtype)

def swiglu(x, w_gate, w_up, w_down):
    return (jax.nn.silu(x @ w_gate) * (x @ w_up)) @ w_down

def macaron_ffn(x, pre_g, post_g, w_gate, w_up, w_down):
    h = swiglu(rms_norm_2(x, pre_g), w_gate, w_up, w_down)
    return x + MACARON_WEIGHT * rms_norm_2(h, post_g)

def causal_dwconv(x, w, b):
    c = x.shape[-1]
    out = lax.conv_general_dilated(
        x, w[:, None, :].astype(x.dtype), window_strides=(1,),
        padding=[(CONV_WIDTH - 1, 0)], dimension_numbers=('NWC', 'WIO', 'NWC'),
        feature_group_count=c)
    return out + b

def rg_lru(x, w_r, b_r, w_i, b_i, lam):
    bn, s, c = x.shape
    xh = x.reshape(bn, s, LRU_HEADS, LRU_BLOCK)
    r = jax.nn.sigmoid(jnp.einsum('bshi,hij->bshj', xh, w_r).reshape(bn, s, c) + b_r)
    i = jax.nn.sigmoid(jnp.einsum('bshi,hij->bshj', xh, w_i).reshape(bn, s, c) + b_i)
    log_a = -LRU_C * r.astype(jnp.float32) * jax.nn.softplus(-lam.astype(jnp.float32))
    a = jnp.exp(log_a)
    mult = jnp.sqrt(-jnp.expm1(2.0 * log_a))
    u = mult * (i * x).astype(jnp.float32)

    def combine(left, right):
        a_l, b_l = left
        a_r, b_r2 = right
        return a_l * a_r, a_r * b_l + b_r2

    _, h = lax.associative_scan(combine, (a, u), axis=1)
    return h.astype(x.dtype)

def recurrent_block(xn, w_in, b_in, conv_w, conv_b, w_r, b_r, w_i, b_i, lam, w_out, b_out):
    proj = xn @ w_in + b_in
    xb, yb = jnp.split(proj, 2, axis=-1)
    xb = causal_dwconv(xb, conv_w, conv_b)
    h = rg_lru(xb, w_r, b_r, w_i, b_i, lam)
    return (h * jax.nn.gelu(yb)) @ w_out + b_out

def t5_bucket(dist):
    n = jnp.maximum(dist, 0)
    max_exact = N_BUCKETS // 2
    nf = jnp.maximum(n, 1).astype(jnp.float32)
    large = max_exact + (jnp.log(nf / max_exact) / math.log(MAX_DISTANCE / max_exact)
                         * (N_BUCKETS - max_exact)).astype(jnp.int32)
    large = jnp.minimum(large, N_BUCKETS - 1)
    return jnp.where(n < max_exact, n, large)

def shared_kv(x, kv_norm_g, w_kv):
    bn, s, _ = x.shape
    nblk = -(-s // MOBA_BLOCK)
    kv = rms_norm_2(x, kv_norm_g) @ w_kv
    k, v = jnp.split(kv, 2, axis=-1)
    pad = nblk * MOBA_BLOCK - s
    k = jnp.pad(k, ((0, 0), (0, pad), (0, 0)))
    v = jnp.pad(v, ((0, 0), (0, pad), (0, 0)))
    k_blk = k.reshape(bn, nblk, MOBA_BLOCK, N_HEADS, HEAD_DIM).transpose(0, 3, 1, 2, 4)
    v_blk = v.reshape(bn, nblk, MOBA_BLOCK, N_HEADS, HEAD_DIM).transpose(0, 3, 1, 2, 4)
    k_mean = jnp.mean(k_blk, axis=3)
    return k_blk, v_blk, k_mean

def moba_attention(q, k_blk, v_blk, k_mean, rel_bias):
    bn, s = q.shape[0], q.shape[1]
    nblk = k_blk.shape[2]
    topk = min(MOBA_TOPK, max(nblk - 1, 1))
    pos = jnp.arange(s)
    cur = pos // MOBA_BLOCK
    gate = jnp.einsum('bshd,bhnd->bhsn', q, k_mean).astype(jnp.float32)
    past = jnp.arange(nblk)[None, :] < cur[:, None]
    gate = jnp.where(past, gate, -jnp.inf)
    _, idx = lax.top_k(gate, topk)
    valid = idx < cur[None, None, :, None]

    nc = s // Q_CHUNK
    q_c = q.transpose(0, 2, 1, 3).reshape(bn, N_HEADS, nc, Q_CHUNK, HEAD_DIM).transpose(2, 0, 1, 3, 4)
    idx_c = idx.reshape(bn, N_HEADS, nc, Q_CHUNK, topk).transpose(2, 0, 1, 3, 4)
    valid_c = valid.reshape(bn, N_HEADS, nc, Q_CHUNK, topk).transpose(2, 0, 1, 3, 4)
    starts = jnp.arange(nc) * Q_CHUNK
    b_ix = jnp.arange(bn)[:, None, None, None]
    h_ix = jnp.arange(N_HEADS)[None, :, None, None]
    offs = jnp.arange(MOBA_BLOCK)
    scale = HEAD_DIM ** -0.5
    n_sel = topk * MOBA_BLOCK

    def chunk(args):
        qc, ic, vc, start = args
        t = start + jnp.arange(Q_CHUNK)
        ks = k_blk[b_ix, h_ix, ic]
        vs = v_blk[b_ix, h_ix, ic]
        kpos = ic[..., None] * MOBA_BLOCK + offs
        bias_s = rel_bias[h_ix[..., None], t5_bucket(t[:, None, None] - kpos)]
        s_sel = jnp.einsum('bhqd,bhqkjd->bhqkj', qc, ks).astype(jnp.float32) * scale + bias_s
        s_sel = jnp.where(vc[..., None], s_sel, -jnp.inf)
        cb = start // MOBA_BLOCK
        k_own = lax.dynamic_index_in_dim(k_blk, cb, axis=2, keepdims=False)
        v_own = lax.dynamic_index_in_dim(v_blk, cb, axis=2, keepdims=False)
        d_own = t[:, None] - (cb * MOBA_BLOCK + offs)[None, :]
        bias_o = rel_bias[:, t5_bucket(d_own)]
        s_own = jnp.einsum('bhqd,bhjd->bhqj', qc, k_own).astype(jnp.float32) * scale + bias_o
        s_own = jnp.where(d_own >= 0, s_own, -jnp.inf)
        logits = jnp.concatenate([s_sel.reshape(bn, N_HEADS, Q_CHUNK, n_sel), s_own], axis=-1)
        p = jax.nn.softmax(logits, axis=-1)
        p_sel = p[..., :n_sel].reshape(bn, N_HEADS, Q_CHUNK, topk, MOBA_BLOCK).astype(vs.dtype)
        p_own = p[..., n_sel:].astype(v_own.dtype)
        return (jnp.einsum('bhqkj,bhqkjd->bhqd', p_sel, vs)
                + jnp.einsum('bhqj,bhjd->bhqd', p_own, v_own))

    out = lax.map(chunk, (q_c, idx_c, valid_c, starts))
    return out.transpose(1, 0, 3, 2, 4).reshape(bn, s, N_HEADS * HEAD_DIM)

def second_inputs(seed: int = 0) -> dict:
    key = jax.random.key(seed)
    ks = iter(jax.random.split(key, 64))

    def nrm(shape, scale):
        return jax.random.normal(next(ks), shape, jnp.float32) * scale

    def gain(shape):
        return 1.0 + nrm(shape, 0.05)

    d, f = D_MODEL, D_FF_2
    u = jax.random.uniform(next(ks), (N_A_LAYERS, D_RNN), jnp.float32, 0.9, 0.999)
    return {
        "x": nrm((BATCH, SEQ, d), 1.0),
        "ffn1_pre_g": gain((DEPTH, d)),
        "ffn1_post_g": gain((DEPTH, d)),
        "ffn1_w_gate": nrm((DEPTH, d, f), d ** -0.5),
        "ffn1_w_up": nrm((DEPTH, d, f), d ** -0.5),
        "ffn1_w_down": nrm((DEPTH, f, d), f ** -0.5),
        "ffn2_pre_g": gain((DEPTH, d)),
        "ffn2_post_g": gain((DEPTH, d)),
        "ffn2_w_gate": nrm((DEPTH, d, f), d ** -0.5),
        "ffn2_w_up": nrm((DEPTH, d, f), d ** -0.5),
        "ffn2_w_down": nrm((DEPTH, f, d), f ** -0.5),
        "mix_pre_g": gain((DEPTH, d)),
        "mix_post_g": gain((DEPTH, d)),
        "lru_w_in": nrm((N_A_LAYERS, d, 2 * D_RNN), d ** -0.5),
        "lru_b_in": nrm((N_A_LAYERS, 2 * D_RNN), 0.02),
        "lru_conv_w": nrm((N_A_LAYERS, CONV_WIDTH, D_RNN), CONV_WIDTH ** -0.5),
        "lru_conv_b": nrm((N_A_LAYERS, D_RNN), 0.02),
        "lru_w_r": nrm((N_A_LAYERS, LRU_HEADS, LRU_BLOCK, LRU_BLOCK), LRU_BLOCK ** -0.5),
        "lru_b_r": nrm((N_A_LAYERS, D_RNN), 0.02),
        "lru_w_i": nrm((N_A_LAYERS, LRU_HEADS, LRU_BLOCK, LRU_BLOCK), LRU_BLOCK ** -0.5),
        "lru_b_i": nrm((N_A_LAYERS, D_RNN), 0.02),
        "lru_lambda": jnp.log(u / (1.0 - u)),
        "lru_w_out": nrm((N_A_LAYERS, D_RNN, d), D_RNN ** -0.5),
        "lru_b_out": nrm((N_A_LAYERS, d), 0.02),
        "kv_norm_g": gain((d,)),
        "w_kv": nrm((d, 2 * N_HEADS * HEAD_DIM), d ** -0.5),
        "attn_w_q": nrm((N_B_LAYERS, d, N_HEADS * HEAD_DIM), d ** -0.5),
        "attn_w_o": nrm((N_B_LAYERS, N_HEADS * HEAD_DIM, d), (N_HEADS * HEAD_DIM) ** -0.5),
        "rel_bias": nrm((N_HEADS, N_BUCKETS), 0.5),
    }

def second_block(x, ffn1_pre_g, ffn1_post_g, ffn1_w_gate, ffn1_w_up, ffn1_w_down,
              ffn2_pre_g, ffn2_post_g, ffn2_w_gate, ffn2_w_up, ffn2_w_down,
              mix_pre_g, mix_post_g,
              lru_w_in, lru_b_in, lru_conv_w, lru_conv_b, lru_w_r, lru_b_r, lru_w_i, lru_b_i,
              lru_lambda, lru_w_out, lru_b_out,
              kv_norm_g, w_kv, attn_w_q, attn_w_o, rel_bias):
    bn, s, _ = x.shape
    k_blk = v_blk = k_mean = None
    for l in range(DEPTH):
        x = macaron_ffn(x, ffn1_pre_g[l], ffn1_post_g[l], ffn1_w_gate[l], ffn1_w_up[l], ffn1_w_down[l])
        xn = rms_norm_2(x, mix_pre_g[l])
        if l < N_A_LAYERS:
            m = recurrent_block(xn, lru_w_in[l], lru_b_in[l], lru_conv_w[l], lru_conv_b[l],
                                lru_w_r[l], lru_b_r[l], lru_w_i[l], lru_b_i[l], lru_lambda[l],
                                lru_w_out[l], lru_b_out[l])
        else:
            j = l - N_A_LAYERS
            q = (xn @ attn_w_q[j]).reshape(bn, s, N_HEADS, HEAD_DIM)
            m = moba_attention(q, k_blk, v_blk, k_mean, rel_bias) @ attn_w_o[j]
        x = x + rms_norm_2(m, mix_post_g[l])
        x = macaron_ffn(x, ffn2_pre_g[l], ffn2_post_g[l], ffn2_w_gate[l], ffn2_w_up[l], ffn2_w_down[l])
        if l == N_A_LAYERS - 1:
            k_blk, v_blk, k_mean = shared_kv(x, kv_norm_g, w_kv)
    return x


def setup_inputs(seed=0):
    out = dict(first_inputs(seed))
    for name, value in second_inputs(seed + 1).items():
        if name != "x":
            out[name + "_2"] = value
    return out


def reference(
    x, c, positions, mla_w_in, mla_q_norm, mla_w_qb, mla_kv_norm, mla_w_kvb, mla_w_o, ssm_w_in,
    ssm_log_dt, ssm_a_re, ssm_a_im, ssm_b_re, ssm_b_im, ssm_c_re, ssm_c_im, ssm_d, ssm_w_glu,
    ssm_b_glu, ssm_w_out, mlp_w1, mlp_b1, mlp_w2, mlp_b2, mod_mix_w, mod_mix_b, mod_ffn_w,
    mod_ffn_b, ln_mix_g, ln_mix_b, ln_ffn_g, ln_ffn_b, ffn1_pre_g_2, ffn1_post_g_2,
    ffn1_w_gate_2, ffn1_w_up_2, ffn1_w_down_2, ffn2_pre_g_2, ffn2_post_g_2, ffn2_w_gate_2,
    ffn2_w_up_2, ffn2_w_down_2, mix_pre_g_2, mix_post_g_2, lru_w_in_2, lru_b_in_2, lru_conv_w_2,
    lru_conv_b_2, lru_w_r_2, lru_b_r_2, lru_w_i_2, lru_b_i_2, lru_lambda_2, lru_w_out_2,
    lru_b_out_2, kv_norm_g_2, w_kv_2, attn_w_q_2, attn_w_o_2, rel_bias_2,
):
    x = first_block(
        x, c, positions, mla_w_in, mla_q_norm, mla_w_qb, mla_kv_norm, mla_w_kvb, mla_w_o,
        ssm_w_in, ssm_log_dt, ssm_a_re, ssm_a_im, ssm_b_re, ssm_b_im, ssm_c_re, ssm_c_im, ssm_d,
        ssm_w_glu, ssm_b_glu, ssm_w_out, mlp_w1, mlp_b1, mlp_w2, mlp_b2, mod_mix_w, mod_mix_b,
        mod_ffn_w, mod_ffn_b, ln_mix_g, ln_mix_b, ln_ffn_g, ln_ffn_b,
    )
    return second_block(
        x, ffn1_pre_g_2, ffn1_post_g_2, ffn1_w_gate_2, ffn1_w_up_2, ffn1_w_down_2, ffn2_pre_g_2,
        ffn2_post_g_2, ffn2_w_gate_2, ffn2_w_up_2, ffn2_w_down_2, mix_pre_g_2, mix_post_g_2,
        lru_w_in_2, lru_b_in_2, lru_conv_w_2, lru_conv_b_2, lru_w_r_2, lru_b_r_2, lru_w_i_2,
        lru_b_i_2, lru_lambda_2, lru_w_out_2, lru_b_out_2, kv_norm_g_2, w_kv_2, attn_w_q_2,
        attn_w_o_2, rel_bias_2,
    )


_drawn_inputs = setup_inputs


def setup_inputs(seed=0):
    import zlib

    import numpy as np

    out = dict(_drawn_inputs(seed))
    spreads = {}
    factors = {'mla_q_norm': 8.0,
     'mla_kv_norm': 8.0,
     'ssm_log_dt': 44.224,
     'ssm_a_re': 64.0,
     'ssm_a_im': 38.08,
     'ssm_b_re': 53.776,
     'ssm_b_im': 53.936,
     'ssm_c_re': 54.44,
     'ssm_c_im': 53.16,
     'ssm_b_glu': 60.66,
     'mlp_b1': 4.431,
     'mod_mix_b': 5.391,
     'mod_ffn_b': 3.03,
     'lru_b_r_2': 8.0,
     'lru_b_i_2': 8.0,
     'ffn2_post_g_2': 2.678}
    for name, (base, spread) in spreads.items():
        noise = np.random.default_rng([zlib.crc32(name.encode()), seed]).standard_normal(out[name].shape)
        drawn = base * np.exp(spread * noise) if base else spread * noise
        out[name] = __import__('jax').numpy.asarray(drawn.astype(out[name].dtype))
    for name, factor in factors.items():
        out[name] = (out[name] * factor).astype(out[name].dtype)
    return out
```

```python
from contextlib import ExitStack
import math

import numpy as np
import concourse.bass as bass
from concourse import mybir

F32 = mybir.dt.float32
F32R = mybir.dt.float32r
I32 = mybir.dt.int32
ALU = mybir.AluOpType
ACT = mybir.ActivationFunctionType

P = 128
L = 256
T = L // P
D = 1024
KT = D // P
CH = 2048
RAW, SPL = 3, 3
HEADS = 8
F1, F2 = 4096, 2816
ALPHA = 4 ** 0.25
QL, KVL, ROPE, NOPE = 256, 128, 64, 128
ZW = QL + KVL + ROPE
NEG = -1e30
TWO_PI = 2 * math.pi
MAGIC = 1.5 * 2 ** 23
PAIRS = 32
CONV = 4


def bits12(x):
    m, e = math.frexp(x)
    return math.ldexp(math.floor(m * 4096) / 4096, e)


PI_A = 6.28125
PI_B = bits12(TWO_PI - PI_A)
PI_C = TWO_PI - PI_A - PI_B


class Steps:

    def __init__(self, eng, sem):
        self.eng, self.sem, self.n, self.base = eng, sem, 0, None

    def did(self, ins):
        self.n += 1
        return ins.then_inc(self.sem, 1)

    def settle(self):
        self.eng.wait_ge(self.sem, self.n if self.base is None else self.base + self.n)

    def loop(self, i, start, per):
        self.before, self.per = self.n, per
        self.base = i * per - start * per

    def end(self, trips):
        assert self.n - self.before == self.per, (self.n - self.before, self.per)
        self.n = self.before + self.per * trips
        self.base = None


PHASES = [("mla", 9), ("mlp0", 32), ("s5", 12), ("mlp1", 32), ("ffn10", 33), ("lru", 14), ("ffn20", 33),
          ("kv", 8), ("ffn11", 33), ("att", 8), ("ffn21", 33)]
FIRST = {}
_n = 0
for _name, _k in PHASES:
    FIRST[_name] = _n
    _n += _k
TOTAL = _n
MLPS, FFNS = ["mlp0", "mlp1"], ["ffn10", "ffn20", "ffn11", "ffn21"]
ITERS = {"mlp0": F1 // 256, "mlp1": F1 // 256, "ffn10": 11, "ffn20": 11, "ffn11": 11, "ffn21": 11}
HID0 = {}
_n = 0
for _name in ["mlp0", "mlp1", "ffn10", "ffn20", "ffn11", "ffn21"]:
    HID0[_name] = _n
    _n += ITERS[_name]
ACC = {n: i for i, n in enumerate(["mla", "mlp0", "s5", "mlp1", "ffn10", "lru", "ffn20", "kv", "ffn11", "att", "ffn21"])}
XTS = {n: i for i, n in enumerate(["mla", "mlp0", "s5", "mlp1", "ffn10", "lru", "ffn20", "kv", "ffn11", "att", "ffn21"])}


def buckets():
    d = np.arange(L)
    nf = np.maximum(d, 1).astype(np.float32)
    large = 16 + (np.log(nf / np.float32(16)) / np.float32(math.log(8)) * np.float32(16)).astype(np.int32)
    return np.where(d < 16, d, np.minimum(large, 31))



ROWS = [("lg1", 0), ("lb1", 1), ("lg2", 0), ("lb2", 1), ("lg3", 0), ("lb3", 1), ("lg4", 3), ("lb4", 4),
        ("pre_ffn10", 0), ("post_ffn10", 1), ("pre_lru", 2), ("post_lru", 3), ("pre_ffn20", 4), ("post_ffn20", 5),
        ("pre_kv", 0), ("pre_ffn11", 1), ("post_ffn11", 2), ("pre_att", 3), ("post_att", 4), ("pre_ffn21", 5),
        ("post_ffn21", 0)]
ROW_FIRST = 8
ROW_SLOT = dict(ROWS)
ROW_COUNT = {n: sum(1 for m, s in ROWS[:i + 1] if s == ROWS[i][1]) for i, (n, _) in enumerate(ROWS)}
ROW_INDEX = {n: i for i, (n, _) in enumerate(ROWS)}
BIASED = ["mlp0", "mlp1", "lru"]


S5P_ANGLE = 2


def build_program(nc, t, out, until="ffn21"):
    order = [n for n, _ in PHASES]
    phases = order[:order.index(until) + 1]
    total = FIRST[phases[-1]] + dict(PHASES)[phases[-1]]
    ctx = ExitStack()
    with ctx:
        def sb(name, shape, dt=F32):
            return ctx.enter_context(nc.sbuf_tensor(name, shape, dt))

        def sem(name):
            return ctx.enter_context(nc.semaphore(name))

        raw = sb("raw", [P, RAW, CH])
        whi = sb("whi", [P, SPL, CH], F32R)
        wlo = sb("wlo", [P, SPL, CH], F32R)
        xhi = sb("xhi", [P, KT, L], F32R)
        xlo = sb("xlo", [P, KT, L], F32R)
        hhi = sb("hhi", [P, KT, L], F32R)
        hlo = sb("hlo", [P, KT, L], F32R)
        X = sb("X", [P, T, D])
        work = sb("work", [P, 8960])
        Y = work[:, 0:2048].rearrange("p (t d) -> p t d", t=T)
        H = work[:, 2048:4096].rearrange("p (t d) -> p t d", t=T)
        TMP = work[:, 4096:6144]
        AR = work[:, 6144:8960]
        mod = sb("mod", [P, 7168])
        modw = mod[:, 0:4096].rearrange("p (s n) -> p s n", s=2)
        modacc = mod[:, 4096:7168]
        G = sb("G", [P, 2, D])
        A = sb("A", [P, D])
        B = sb("B", [P, D])
        GA = sb("GA", [P, D])
        BA = sb("BA", [P, D])
        row_slots = [GA[:, :], BA[:, :], G[:, 0, :], A[:, :], B[:, :], G[:, 1, :]]
        brow = sb("brow", [1, D])
        ident = sb("ident", [P, P])
        ones = sb("ones", [P, P])
        mask = sb("mask", [P, L])
        zeros = mask[0:1, 0:P].bitcast(mybir.dt.bfloat16)
        small = sb("small", [P, 512])
        rope = sb("rope", [P, 2, T, 32])
        ps = ctx.enter_context(nc.psum_tensor("ps", [P, 8, 512], F32))
        s5_store = nc.dram_tensor("s5_store", (2, P, 2048), F32, kind="Internal").ap()
        bias_store = nc.dram_tensor("bias_store", (HEADS, P * 386), F32, kind="Internal").ap()

        used = [0]

        def col(n):
            used[0] += n
            assert used[0] < 512
            return small[:, used[0] - n:used[0]]

        craw, csil = col(8), col(8)
        stats, mv, nmr = col(24), col(4), col(2)
        ssq, rsq = col(8), col(8)
        newton = col(24)
        posi, posf = col(2), col(2)
        invf = col(32)
        rho, th, th_hi, th_lo = col(PAIRS), col(PAIRS), col(PAIRS), col(PAIRS)
        dskip, bglu, b1c = col(8), col(8), col(64)
        lru_bin, lru_conv, lru_cb = col(16), col(32), col(8)
        lru_br, lru_bi, lru_lam, lam_n, lam_p = col(8), col(8), col(8), col(8), col(8)
        attm, atts = col(8), col(8)

        raw_in = [sem(f"raw_in{i}") for i in range(RAW)]
        hi_done = sem("hi_done")
        lo_done = sem("lo_done")
        w_used = sem("w_used")
        x_in, c_in, small_in, small2_in, s5_in = sem("x_in"), sem("c_in"), sem("small_in"), sem("small2_in"), sem("s5_in")
        m0_in = [sem(f"m0_in{i}") for i in range(4)]
        m0_used = sem("m0_used")
        modw_in = [sem(f"modw_in{i}") for i in range(2)]
        modb_in, modb0_in = sem("modb_in"), sem("modb0_in")
        acc0_clear = sem("acc0_clear")
        mod_sum, mod0_sum = sem("mod_sum"), sem("mod0_sum")
        modb_ps, modb_out = sem("modb_ps"), sem("modb_out")
        row_in = [sem(f"row_in{i}") for i in range(6)]
        row_used = sem("row_used")
        vec_done = sem("vec_done")
        glue_done = sem("glue_done")
        x_scaled = sem("x_scaled")
        const_ok, csil_ok = sem("const_ok"), sem("csil_ok")
        dve_step, act_step, pool_step, pe_step = sem("dve_step"), sem("act_step"), sem("pool_step"), sem("pe_step")
        acc_half, acc_free = sem("acc_half"), sem("acc_free")
        ln_stats, res_ok, sq_done, x_new, h_ready = sem("ln_stats"), sem("res_ok"), sem("sq_done"), sem("x_new"), sem("h_ready")
        xt_ps, xhi_ok, xt_ok = sem("xt_ps"), sem("xhi_ok"), sem("xt_ok")
        act1, prod, hid_hi, hid_ok = sem("act1"), sem("prod"), sem("hid_hi"), sem("hid_ok")
        brow_in, acc_open = sem("brow_in"), sem("acc_open")
        rope_r, rope_sin, rope_tab = sem("rope_r"), sem("rope_sin"), sem("rope_tab")
        z_full, z_sq, zn_ok, zt_ps, zhi_ok, zx_ok = sem("z_full"), sem("z_sq"), sem("zn_ok"), sem("zt_ps"), sem("zhi_ok"), sem("zx_ok")
        k_ps, k_ok, v_ps, v_ok = sem("k_ps"), sem("k_ok"), sem("v_ps"), sem("v_ok")
        q_ps, q_ok, qp_ps, qp_ok, qt_ps, qt_ok = sem("q_ps"), sem("q_ok"), sem("qp_ps"), sem("qp_ok"), sem("qt_ps"), sem("qt_ok")
        s_ps, sm_ok, mx_ok, exp_ok, p_ok = sem("s_ps"), sem("sm_ok"), sem("mx_ok"), sem("exp_ok"), sem("p_ok")
        pt_ps, pt_ok, o_ps, o_hi, o_ok = sem("pt_ps"), sem("pt_ok"), sem("o_ps"), sem("o_hi"), sem("o_ok")
        s5t_ok, s5p_ps, s5p_act, s5p_pool, s5p_dve = sem("s5t_ok"), sem("s5p_ps"), sem("s5p_act"), sem("s5p_pool"), sem("s5p_dve")
        s5_stored, s5_loaded = sem("s5_stored"), sem("s5_loaded")
        u_ok, bu_ps, bu_rot = sem("u_ok"), sem("bu_ps"), sem("bu_rot")
        phase_r, table_ok, x_rot, x_used, y_ok = sem("phase_r"), sem("table_ok"), sem("x_rot"), sem("x_used"), sem("y_ok")
        g_act, g_hi, g_ok, sig_ok, zz_ok, zz_hi, zz_lo = (sem(n) for n in ("g_act", "g_hi", "g_ok", "sig_ok", "zz_ok", "zz_hi", "zz_lo"))
        lp_ok, conv_ok, xc_hi, xc_ok = sem("lp_ok"), sem("conv_ok"), sem("xc_hi"), sem("xc_ok")
        lg_ps, lg_ok, la_ok, m2_ok, mult_ok, hg_ok, hg_hi, hg_lo = (
            sem(n) for n in ("lg_ps", "lg_ok", "la_ok", "m2_ok", "mult_ok", "hg_ok", "hg_hi", "hg_lo"))
        lam_exp, lam_ok = sem("lam_exp"), sem("lam_ok")
        vrev_ok, bias_stored, bias_in, rel_in = sem("vrev_ok"), sem("bias_stored"), sem("bias_in"), sem("rel_in")
        final_ok, out_done = sem("final_ok"), sem("out_done")

        block = ctx.enter_context(nc.Block())

        kT = Y.rearrange("p t d -> p (t d)").rearrange("p (h l) -> p h l", h=HEADS)
        V = H
        qT = TMP.rearrange("p (h l) -> p h l", h=HEADS)
        qpT = AR[:, 0:1024].rearrange("p (r l) -> p r l", r=4)
        kpT = AR[:, 1024:1280]
        sm = AR[:, 1280:2048].rearrange("p (s n) -> p s n", s=2)
        pt = AR[:, 2048:2816].rearrange("p (s n) -> p s n", s=2)
        zn = Y
        qp_tok = AR[:, 1280:1792].rearrange("p (t n) -> p t n", t=T)
        rt = AR[:, 1792:2304].rearrange("p (s n) -> p s n", s=4)
        kT2 = mod[:, 0:2048].rearrange("p (h l) -> p h l", h=HEADS)
        V2 = mod[:, 2048:4096].rearrange("p (t d) -> p t d", t=T)
        relb = mod[:, 4096:6144].rearrange("p (h l) -> p h l", h=HEADS)
        qT2 = kT
        sm2 = TMP[:, 0:768].rearrange("p (s n) -> p s n", s=2)
        pt2 = TMP[:, 768:1536].rearrange("p (s n) -> p s n", s=2)
        b_in = mod[:, 0:1024].rearrange("p (r q c) -> p r q c", r=2, q=PAIRS)
        b_dg = mod[:, 1024:3072].rearrange("p (m r i c) -> p m r i c", m=KT, r=2, i=4)
        c_pad = mod[:, 3072:5120].rearrange("p (m r n) -> p m r n", m=KT, r=2)
        s5_stage = mod[:, 5120:7168].rearrange("p (m r n) -> p m r n", m=KT, r=2)
        a_rows = work[0:PAIRS, 8192:8576].rearrange("p (k n) -> p k n", k=3)
        g0v = G[:, 0, :].rearrange("p (k n) -> p k n", n=PAIRS)
        straight_phases = ("s5", "lru", "kv", "att")
        bu1 = mod[:, 5120:5632].rearrange("p (q c) -> p q c", q=PAIRS)
        bu2 = mod[:, 5632:6144].rearrange("p (q c) -> p q c", q=PAIRS)
        ldt_rows = work[0:PAIRS, 8576:8578]
        s5B = mod[:, 0:2048].rearrange("p (m r n) -> p m r n", m=KT, r=2)
        s5C = mod[:, 2048:4096].rearrange("p (m r n) -> p m r n", m=KT, r=2)
        uT = H.rearrange("p t d -> p (t d)").rearrange("p (m l) -> p m l", m=KT)
        yT = Y.rearrange("p t d -> p (t d)").rearrange("p (m l) -> p m l", m=KT)
        tabs = mod[:, 4096:5120].rearrange("p (s k l) -> p s k l", s=2, k=2)
        ph = mod[:, 5120:6144].rearrange("p (s k l) -> p s k l", s=2, k=2)
        half = mod[:, 6144:6656].rearrange("p (k l) -> p k l", k=2)
        iotaf = mod[:, 6656:6912]
        rot_a = TMP[:, 0:1024].rearrange("p (s n) -> p s n", s=2)
        rot_b = TMP[:, 1024:2048].rearrange("p (s n) -> p s n", s=2)
        zst = AR[:, 0:512]
        xa = AR[:, 512:1536].rearrange("p (s n) -> p s n", s=2)
        xb = AR[:, 1536:2560].rearrange("p (s n) -> p s n", s=2)
        sig = TMP[:, 0:1024].rearrange("p (s n) -> p s n", s=2)
        zz = TMP[:, 1024:2048].rearrange("p (s n) -> p s n", s=2)
        rel = mod[0:HEADS, 6144:6144 + 32]
        vrev = mod[0:HEADS, 6656:6656 + 384]
        xbp = work[:, 4096:6168].rearrange("p (m l) -> p m l", m=KT)
        xcT = Y.rearrange("p t d -> p (t d)").rearrange("p (m l) -> p m l", m=KT)
        gyT = H.rearrange("p t d -> p (t d)").rearrange("p (m l) -> p m l", m=KT)
        rT = mod[:, 0:2048].rearrange("p (m l) -> p m l", m=KT)
        iT = mod[:, 2048:4096].rearrange("p (m l) -> p m l", m=KT)
        aT = mod[:, 4096:6144].rearrange("p (m l) -> p m l", m=KT)
        tT = work[:, 6400:8448].rearrange("p (m l) -> p m l", m=KT)

        def ws_src(w, j):
            return w.rearrange("(k p) f -> p k f", p=P)[:, :, j * 256:(j + 1) * 256]

        def xs_src(w, j):
            return w[2 * j * P:(2 * j + 2) * P, :].rearrange("(k p) n -> p k n", p=P)

        straight = {}
        w_in = t["mla_w_in"][0].rearrange("(k p) f -> p k f", p=P)
        w_qb = t["mla_w_qb"][0].rearrange("(k p) f -> p k f", p=P)
        for i in range(2):
            straight[i] = (w_in[:, 4 * i:4 * i + 4, :], (4, ZW))
            straight[3 + i] = (w_qb[:, :, 768 * i:768 * i + 768], (2, 768))
        straight[2] = (t["mla_w_kvb"][0].rearrange("p (a n) -> p a n", a=2), (2, 1024))
        c0 = FIRST["s5"]
        for i in range(4):
            straight[5 + i] = (xs_src(t["mla_w_o"][0], i), (2, D))
            straight[c0 + i] = (ws_src(t["ssm_w_in"][0], i), (8, 256))
            straight[c0 + 4 + i] = (ws_src(t["ssm_w_glu"][0], i), (8, 256))
            straight[c0 + 8 + i] = (xs_src(t["ssm_w_out"][0], i), (2, D))
        c0 = FIRST["lru"]
        for i in range(8):
            straight[c0 + i] = (ws_src(t["lru_w_in_2"][0], i), (8, 256))
        straight[c0 + 8] = (t["lru_w_r_2"][0].rearrange("h (k p) j -> p (h k) j", p=P), (8, 256))
        straight[c0 + 9] = (t["lru_w_i_2"][0].rearrange("h (k p) j -> p (h k) j", p=P), (8, 256))
        for i in range(4):
            straight[c0 + 10 + i] = (xs_src(t["lru_w_out_2"][0], i), (2, D))
            straight[FIRST["kv"] + i] = (ws_src(t["w_kv_2"], i), (8, 256))
            straight[FIRST["kv"] + 4 + i] = (xs_src(t["w_kv_2"][:, D:2 * D], i), (2, D))
            straight[FIRST["att"] + i] = (ws_src(t["attn_w_q_2"][0], i), (8, 256))
            straight[FIRST["att"] + 4 + i] = (xs_src(t["attn_w_o_2"][0], i), (2, D))
        width = {c: int(np.prod(s)) for c, (_, s) in straight.items()}
        ffn_w = {"mlp0": (t["mlp_w1"][0], None, t["mlp_w2"][0]), "mlp1": (t["mlp_w1"][1], None, t["mlp_w2"][1])}
        for name, k, l in (("ffn10", 1, 0), ("ffn20", 2, 0), ("ffn11", 1, 1), ("ffn21", 2, 1)):
            ffn_w[name] = tuple(t[f"ffn{k}_w_{x}_2"][l] for x in ("gate", "up", "down"))
        row_src = {"lg1": t["ln_mix_g"][0], "lb1": t["ln_mix_b"][0], "lg2": t["ln_ffn_g"][0], "lb2": t["ln_ffn_b"][0],
                   "lg3": t["ln_mix_g"][1], "lb3": t["ln_mix_b"][1], "lg4": t["ln_ffn_g"][1], "lb4": t["ln_ffn_b"][1],
                   "pre_ffn10": t["ffn1_pre_g_2"][0], "post_ffn10": t["ffn1_post_g_2"][0],
                   "pre_lru": t["mix_pre_g_2"][0], "post_lru": t["mix_post_g_2"][0],
                   "pre_ffn20": t["ffn2_pre_g_2"][0], "post_ffn20": t["ffn2_post_g_2"][0],
                   "pre_kv": t["kv_norm_g_2"], "pre_ffn11": t["ffn1_pre_g_2"][1], "post_ffn11": t["ffn1_post_g_2"][1],
                   "pre_att": t["mix_pre_g_2"][1], "post_att": t["mix_post_g_2"][1],
                   "pre_ffn21": t["ffn2_pre_g_2"][1], "post_ffn21": t["ffn2_post_g_2"][1]}
        bias_src = {"mlp0": t["mlp_b2"][0], "mlp1": t["mlp_b2"][1], "lru": t["lru_b_out_2"][0]}
        mod_w = [t["mod_mix_w"][0], t["mod_ffn_w"][0], t["mod_mix_w"][1], t["mod_ffn_w"][1]]
        mod_b = [t["mod_mix_b"][0], t["mod_ffn_b"][0], t["mod_mix_b"][1], t["mod_ffn_b"][1]]

        def shaped(ap, shape):
            return ap[:, 0:shape[0] * shape[1]].rearrange("p (a b) -> p a b", a=shape[0])

        def row(name):
            return row_slots[ROW_SLOT[name]]

        def row_wait(eng, name):
            eng.wait_ge(row_in[ROW_SLOT[name]], 16 * ROW_COUNT[name])

        def mlp_runs(name):
            return [(0, 3), (3, 5)]

        @block.sync
        def _(sp):
            def chunk(c, src, shape, i=None):
                if c >= RAW:
                    need = c - RAW + 1
                    sp.wait_ge(lo_done, need if i is None else i * 6 + need)
                sp.dma_start(shaped(raw[:, c % RAW, :], shape), src).then_inc(raw_in[c % RAW], 16)

            def line(c):
                if c < total:
                    chunk(c, *straight[c])

            def up_src(w, j):
                return w.rearrange("(k p) f -> p k f", p=P)[:, :, bass.ds(j * 256, 256)]

            def down_src(w, j):
                return w[bass.ds(j * 256, 256), :].rearrange("(k p) n -> p k n", p=P)

            def load_row(name):
                sp.dma_start(row(name), row_src[name].rearrange("(o n) -> o n", o=1).to_broadcast([P, D])).then_inc(
                    row_in[ROW_SLOT[name]], 16)

            def reload_row(name):
                if ROW_INDEX[name] - ROW_FIRST >= 6:
                    sp.wait_ge(row_used, ROW_INDEX[name] - ROW_FIRST - 5)
                load_row(name)

            def cols(dst, src, s):
                with nc.allow_non_contiguous_dma(reason="short vectors"):
                    sp.dma_start(dst, src.rearrange("(k p) -> p k", p=P)).then_inc(s, 16)

            def bias_row(name):
                if BIASED.index(name):
                    sp.wait_ge(acc_open, BIASED.index(name))
                sp.dma_start(brow[0:1, :], bias_src[name].rearrange("(o n) -> o n", o=1)).then_inc(brow_in, 16)

            def mlp(name):
                up, _, down = ffn_w[name]
                c = FIRST[name]
                chunk(c, ws_src(up, 0), (8, 256))
                for a, b in mlp_runs(name):
                    with sp.Fori(a, b) as i:
                        for k in range(3):
                            chunk(c + 1 + 2 * k, up_src(up, i * 3 + (k + 1)), (8, 256), i)
                            chunk(c + 2 + 2 * k, down_src(down, i * 3 + k), (2, D), i)
                    if a == 0 and name == "mlp0":
                        sp.wait_ge(res_ok, 2)
                        load_row("lg2")
                        load_row("lb2")
                    if a == 0 and name == "mlp1":
                        sp.wait_ge(res_ok, 6)
                        load_row("pre_ffn10")
                        load_row("post_ffn10")
                        sp.wait_ge(glue_done, 4)
                        load_row("lg4")
                        load_row("lb4")
                        load_row("pre_lru")
                chunk(c + 31, xs_src(down, 15), (2, D))

            def ffn(name):
                gate, up, down = ffn_w[name]
                c = FIRST[name]
                chunk(c, ws_src(gate, 0), (8, 256))
                chunk(c + 1, ws_src(up, 0), (8, 256))
                with sp.Fori(0, 5) as i:
                    for k in range(2):
                        chunk(c + 2 + 3 * k, up_src(gate, i * 2 + (k + 1)), (8, 256), i)
                        chunk(c + 3 + 3 * k, up_src(up, i * 2 + (k + 1)), (8, 256), i)
                        chunk(c + 4 + 3 * k, down_src(down, i * 2 + k), (2, D), i)
                chunk(c + 32, xs_src(down, 10), (2, D))

            cols(craw, t["c"][0], c_in)
            w0 = mod_w[0].rearrange("(k p) n -> p k n", p=P)
            m0 = [work[:, 2048 * s:2048 * (s + 1)].rearrange("p (k n) -> p k n", k=2) for s in range(4)]
            for n in range(8):
                third, kk = n // 4, n % 4
                if n >= 4:
                    sp.wait_ge(m0_used, n - 3)
                sp.dma_start(m0[n % 4], w0[:, 2 * kk:2 * kk + 2, D * third:D * (third + 1)]).then_inc(m0_in[n % 4], 16)
                if n < 2:
                    if n == 0:
                        sp.wait_ge(acc0_clear, 1)
                    sp.dma_start([GA, BA][n][0:1, :], mod_b[0][D * n:D * (n + 1)].rearrange("(o n) -> o n", o=1)).then_inc(modb0_in, 16)
            sp.dma_start(X[:, :, :], t["x"][0].rearrange("(t p) d -> p t d", p=P)).then_inc(x_in, 16)
            with nc.allow_non_contiguous_dma(reason="short vectors"):
                sp.dma_start(posi.bitcast(I32), t["positions"][0].rearrange("(t p) -> p t", p=P)).then_inc(small_in, 16)
            sp.dma_start(invf, t["inv_freq"].rearrange("(o n) -> o n", o=1).to_broadcast([P, 32])).then_inc(small_in, 16)
            sp.dma_start(G[:, 1, 0:QL], t["mla_q_norm"].to_broadcast([P, QL])).then_inc(small_in, 16)
            sp.dma_start(G[:, 1, QL:QL + KVL], t["mla_kv_norm"].to_broadcast([P, KVL])).then_inc(small_in, 16)
            for c in range(3):
                line(c)
            for dst, src in ((dskip, t["ssm_d"][0]), (bglu, t["ssm_b_glu"][0]), (b1c[:, 0:32], t["mlp_b1"][0]),
                             (b1c[:, 32:64], t["mlp_b1"][1]), (lru_bin, t["lru_b_in_2"][0]), (lru_cb, t["lru_conv_b_2"][0]),
                             (lru_br, t["lru_b_r_2"][0]), (lru_bi, t["lru_b_i_2"][0]), (lru_lam, t["lru_lambda_2"][0]),
                             *((lru_conv[:, 8 * j:8 * j + 8], t["lru_conv_w_2"][0, j]) for j in range(CONV))):
                cols(dst, src, small2_in)
            bias_row("mlp0")
            line(3)
            sp.wait_ge(glue_done, 1)
            load_row("lg1")
            load_row("lb1")
            for c in range(4, 9):
                line(c)
            for name in phases[1:]:
                if name in MLPS:
                    mlp(name)
                if name in FFNS:
                    ffn(name)
                if name == "ffn10":
                    bias_row("lru")
                    sp.wait_ge(glue_done, 5)
                    for r in ("post_lru", "pre_ffn20", "post_ffn20"):
                        load_row(r)
                if name in straight_phases:
                    for k in range(dict(PHASES)[name]):
                        line(FIRST[name] + k)
                        if name == "s5" and k == 3:
                            bias_row("mlp1")
                            sp.wait_ge(res_ok, 4)
                            load_row("lg3")
                            load_row("lb3")
                        if name == "s5" and k == 6:
                            sp.wait_ge(modb_out, 24)
                            sp.wait_ge(s5_stored, 32)
                            sp.dma_start(mod[:, 0:2048], s5_store[0]).then_inc(s5_loaded, 16)
                            sp.dma_start(mod[:, 2048:4096], s5_store[1]).then_inc(s5_loaded, 16)
                        if name != "s5" and k == 1:
                            for r in {"lru": ("pre_kv", "pre_ffn11", "post_ffn11"), "kv": ("pre_att", "post_att"),
                                      "att": ("pre_ffn21", "post_ffn21")}[name]:
                                reload_row(r)
            if until in MLPS:
                chunk(total, ws_src(t["mlp_w1"][0], 0), (8, 256))
            sp.wait_ge(final_ok, 1)
            sp.dma_start(out[0].rearrange("(t p) d -> p t d", p=P), X[:, :, :]).then_inc(out_done, 16)
            sp.wait_ge(out_done, 16)

        @block.tensor
        def _(pe):
            spread = [0]

            def mm3(o, lh, ll, rh, rl, start, stop):
                pe.matmul(o, lh, rh, start=start, stop=False)
                pe.matmul(o, lh, rl, start=False, stop=False)
                return pe.matmul(o, ll, rh, start=False, stop=stop)

            def chunk_ready(c, i=None):
                pe.wait_ge(lo_done, c + 1 if i is None else i * 6 + (c + 1))

            def parts(c, shape):
                return shaped(whi[:, c % SPL, :], shape), shaped(wlo[:, c % SPL, :], shape)

            def columns(c, bank, i=None, src=(xhi, xlo)):
                chunk_ready(c, i)
                wh, wl = parts(c, (8, 256))
                for m in range(2):
                    for k in range(KT):
                        last = mm3(ps[:, bank, m * L:(m + 1) * L], wh[:, k, m * P:(m + 1) * P], wl[:, k, m * P:(m + 1) * P],
                                   src[0][:, k, :], src[1][:, k, :], k == 0, k == KT - 1)
                last.then_inc(w_used, 1)

            def rows_of(c, tile, i=None, first=False, final=False, src=(hhi, hlo)):
                chunk_ready(c, i)
                wh, wl = parts(c, (2, D))
                for tt in range(T):
                    for k in range(2):
                        for n in range(2):
                            last = mm3(ps[:, 2 * tt + n, :], src[0][:, tile + k, tt * P:(tt + 1) * P],
                                       src[1][:, tile + k, tt * P:(tt + 1) * P], wh[:, k, n * 512:(n + 1) * 512],
                                       wl[:, k, n * 512:(n + 1) * 512], first and k == 0, final and k == 1)
                    if final and tt == 0:
                        last.then_inc(acc_half, 1)
                last.then_inc(w_used, 1)

            def project(c, bias=False, src=(hhi, hlo)):
                for j in range(4):
                    rows_of(c + j, 2 * j, first=(j == 0 and not bias), final=(j == 3), src=src)

            def open_acc(name):
                pe.wait_ge(acc_free, 2 * ACC[name])
                if name in BIASED:
                    pe.wait_ge(brow_in, 16 * (BIASED.index(name) + 1))
                for b in range(4):
                    if name in BIASED:
                        last = pe.matmul(ps[:, b, :], ones[0:1, :], brow[0:1, (b % 2) * 512:(b % 2 + 1) * 512], start=True, stop=False)
                    else:
                        pe.matmul(ps[:, b, 0:L], zeros[:, 0:P], zeros, start=True, stop=False)
                        pe.matmul(ps[:, b, L:], zeros[:, 0:P], zeros, start=False, stop=False)
                if name in BIASED:
                    last.then_inc(acc_open, 1)

            def turn(name):
                if name == "mlp0":
                    pe.wait_ge(modb_out, 12)
                for tt in range(T):
                    pe.wait_ge(h_ready, 2 * XTS[name] + tt + 1)
                    for hf in range(2):
                        for j in range(4):
                            k = 4 * hf + j
                            last = pe.transpose(ps[:, 4 + 2 * tt + hf, j * P:(j + 1) * P], H[:, tt, k * P:(k + 1) * P], ident[:, :])
                        last.then_inc(xt_ps, 1)

            def input_ready(name):
                pe.wait_ge(xt_ok, 4 * (XTS[name] + 1))

            def spread_mod(acc, banks, third_count=None, s=mod_sum):
                if third_count is not None:
                    pe.wait_ge(s, third_count)
                for b, half_row in zip(banks, acc):
                    pe.matmul(ps[:, b, :], ones[:, :], half_row, start=True, stop=True).then_inc(modb_ps, 1)
                    spread[0] += 1

            def halves(ap, n):
                return [ap[:, 512 * q:512 * (q + 1)] for q in range(n)]

            def mlp(name):
                h, c = HID0[name], FIRST[name]
                turn(name)
                open_acc(name)
                input_ready(name)
                columns(c, 4)
                for a, b in mlp_runs(name):
                    with pe.Fori(a, b) as i:
                        for k in range(3):
                            columns(c + 1 + 2 * k, 4 + (k + 1) % 3, i)
                            pe.wait_ge(hid_ok, i * 3 + (h + k + 1))
                            rows_of(c + 2 + 2 * k, 2 * k, i)
                    if a == 0 and name == "mlp0":
                        spread_mod(halves(modacc, 3), (5, 6, 7), 7)
                        pe.wait_ge(modb_out, 15)
                        spread_mod(halves(modacc, 6)[3:], (5, 6, 7))
                        pe.wait_ge(modb_out, 18)
                pe.wait_ge(hid_ok, h + 16)
                rows_of(c + 31, 0, final=True)

            def ffn(name):
                h, c = HID0[name], FIRST[name]
                turn(name)
                open_acc(name)
                input_ready(name)
                columns(c, 4)
                columns(c + 1, 6)
                with pe.Fori(0, 5) as i:
                    for k in range(2):
                        columns(c + 2 + 3 * k, 4 + (k + 1) % 2, i)
                        columns(c + 3 + 3 * k, 6 + (k + 1) % 2, i)
                        pe.wait_ge(hid_ok, i * 2 + (h + k + 1))
                        rows_of(c + 4 + 3 * k, 2 * k, i)
                pe.wait_ge(hid_ok, h + 11)
                rows_of(c + 32, 0, final=True)


            def mla():
                turn("mla")
                pe.wait_ge(s5t_ok, 8)
                input_ready("mla")
                for c in range(2):
                    chunk_ready(c)
                    wh, wl = parts(c, (4, ZW))
                    for tt in range(T):
                        for k in range(4):
                            kt = 4 * c + k
                            last = mm3(ps[:, tt, 0:ZW], xhi[:, kt, tt * P:(tt + 1) * P], xlo[:, kt, tt * P:(tt + 1) * P],
                                       wh[:, k, :], wl[:, k, :], kt == 0, kt == KT - 1)
                    last.then_inc(w_used, 1)
                for tt in range(T):
                    pe.wait_ge(zn_ok, tt + 1)
                    for j in range(4):
                        last = pe.transpose(ps[:, 4 + j // 2, (j % 2) * L + tt * P:(j % 2) * L + (tt + 1) * P],
                                            zn[:, tt, j * P:(j + 1) * P], ident[:, :])
                last.then_inc(zt_ps, 1)
                chunk_ready(2)
                pe.wait_ge(zx_ok, 1)
                wh, wl = (w[:, 2 % SPL, :].rearrange("p (h n) -> p h n", h=HEADS) for w in (whi, wlo))
                for h in range(HEADS):
                    last = mm3(ps[:, h // 2, (h % 2) * L:(h % 2 + 1) * L], wh[:, h, 0:P], wl[:, h, 0:P], xhi[:, 2, :], xlo[:, 2, :],
                               True, True)
                    if h % 2:
                        last.then_inc(k_ps, 1)
                pe.wait_ge(zx_ok, 2)
                for tt in range(T):
                    for n in range(2):
                        last = mm3(ps[:, 4 + 2 * tt + n, :], xhi[:, 2, tt * P:(tt + 1) * P], xlo[:, 2, tt * P:(tt + 1) * P],
                                   wh[:, 4 * n:4 * n + 4, P:2 * P], wl[:, 4 * n:4 * n + 4, P:2 * P], True, True)
                    if tt == 0:
                        last.then_inc(v_ps, 1)
                last.then_inc(w_used, 1)
                for g in range(2):
                    chunk_ready(3 + g)
                    pe.wait_ge(k_ok, 4)
                    if g:
                        pe.wait_ge(q_ok, 2)
                        pe.wait_ge(qp_ok, 1)
                    wh, wl = (w[:, (3 + g) % SPL, 0:1536].rearrange("p (k h n) -> p k h n", k=2, h=4) for w in (whi, wlo))
                    for h in range(4):
                        for k in range(2):
                            last = mm3(ps[:, h // 2, (h % 2) * L:(h % 2 + 1) * L], wh[:, k, h, 0:P], wl[:, k, h, 0:P],
                                       xhi[:, k, :], xlo[:, k, :], k == 0, k == 1)
                        if h % 2:
                            last.then_inc(q_ps, 1)
                    for tt in range(T):
                        for k in range(2):
                            last = mm3(ps[:, 2, tt * L:(tt + 1) * L], xhi[:, k, tt * P:(tt + 1) * P], xlo[:, k, tt * P:(tt + 1) * P],
                                       wh[:, k, :, P:P + ROPE], wl[:, k, :, P:P + ROPE], k == 0, k == 1)
                    last.then_inc(w_used, 1)
                    pe.wait_ge(qp_ok, g + 1)
                    if g:
                        pe.wait_ge(qt_ok, 1)
                    for r in range(2):
                        for tt in range(T):
                            last = pe.transpose(ps[:, 3, r * L + tt * P:r * L + (tt + 1) * P], qp_tok[:, tt, r * P:(r + 1) * P], ident[:, :])
                    last.then_inc(qt_ps, 1)
                pe.wait_ge(q_ok, 4)
                pe.wait_ge(qt_ok, 2)
                pe.wait_ge(v_ok, 2)
                attention(0, qT, kT, V, True)
                spread_mod(halves(G[:, 0, :], 2), (6, 7), 1)
                rows_of(5, 0, first=True)
                rows_of(6, 2)
                pe.wait_ge(modb_out, 6)
                pe.wait_ge(mod_sum, 4)
                spread_mod(halves(modacc, 4), (4, 5, 6, 7))
                rows_of(7, 4)
                pe.wait_ge(modb_out, 8)
                spread_mod(halves(modacc, 6)[4:], (4, 5))
                rows_of(8, 6, final=True)

            def attention(n, q, k, v, rotary):
                for i in range(HEADS + 2):
                    if i < HEADS:
                        h, e = i, HEADS * n + i
                        if e >= 2:
                            pe.wait_ge(sm_ok, e - 1)
                        for lo, hi, tt, keys in ((0, P, 0, P), (P, 3 * P, 1, L)):
                            last = pe.matmul(ps[:, h % 2, lo:hi], q[:, h, tt * P:(tt + 1) * P], k[:, h, 0:keys], start=True, stop=not rotary)
                            if rotary:
                                a = 64 * (h % 2)
                                last = pe.matmul(ps[:, h % 2, lo:hi], qpT[a:a + 64, h // 2, tt * P:(tt + 1) * P], kpT[a:a + 64, 0:keys],
                                                 start=False, stop=True)
                        last.then_inc(s_ps, 1)
                    if 1 <= i <= HEADS:
                        h, e = i - 1, HEADS * n + i - 1
                        pe.wait_ge(p_ok, e + 1)
                        if e >= 2:
                            pe.wait_ge(pt_ok, e - 1)
                        for j in range(3):
                            last = pe.transpose(ps[:, 2 + h % 2, j * P:(j + 1) * P], (sm, sm2)[n][:, h % 2, j * P:(j + 1) * P], ident[:, :])
                        last.then_inc(pt_ps, 1)
                    if i >= 2:
                        h, e = i - 2, HEADS * n + i - 2
                        pe.wait_ge(pt_ok, e + 1)
                        if e >= 2:
                            pe.wait_ge(o_ok, e - 1)
                        pp = (pt, pt2)[n][:, h % 2, :]
                        pe.matmul(ps[:, 4 + h % 2, 0:L], v[:, 0, h * P:(h + 1) * P], pp[:, 0:L], start=True, stop=False)
                        pe.matmul(ps[:, 4 + h % 2, P:L], v[:, 1, h * P:(h + 1) * P], pp[:, L:3 * P], start=False, stop=True).then_inc(o_ps, 1)
                pe.wait_ge(o_ok, HEADS * (n + 1))

            def s5():
                c = FIRST["s5"]
                turn("s5")
                pe.wait_ge(acc_free, 2 * ACC["s5"])
                pe.wait_ge(mod_sum, 9)
                spread_mod(halves(modacc, 4), (0, 1, 2, 3))
                input_ready("s5")
                for j in range(4):
                    columns(c + j, 4 + j)
                pe.wait_ge(modb_out, 22)
                pe.wait_ge(mod_sum, 10)
                spread_mod(halves(modacc, 6)[4:], (0, 1))
                pe.wait_ge(modb_out, 24)
                pe.wait_ge(u_ok, 4)
                pe.wait_ge(s5_loaded, 32)
                for i in range(PAIRS + 1):
                    if i < PAIRS:
                        m, a = i // 4, 32 * (i % 4)
                        if i >= 2:
                            pe.wait_ge(bu_rot, i - 1)
                        for r in range(2):
                            last = pe.matmul(ps[:, i % 2, r * L:(r + 1) * L], s5B[a:a + 32, m, r, :], uT[a:a + 32, m, :], start=True, stop=True)
                        last.then_inc(bu_ps, 1)
                    if i >= 1:
                        e = i - 1
                        m, a = e // 4, 32 * (e % 4)
                        pe.wait_ge(x_rot, e + 1)
                        if e % 4 == 0 and m >= 2:
                            pe.wait_ge(y_ok, m - 1)
                        s = e % 2
                        for q, (r, x) in enumerate(((0, xa[:, s, 0:L]), (0, xb[:, s, 0:L]), (1, xa[:, s, L:]), (1, xb[:, s, L:]))):
                            last = pe.matmul(ps[a:a + 32, 2 + m % 2, 0:L], s5C[:, m, r, a:a + 32], x, start=(q == 0), stop=(q == 3))
                        last.then_inc(x_used, 1)
                pe.wait_ge(g_ok, 2)
                for j in range(4):
                    columns(c + 4 + j, 4 + j)
                for j in range(4):
                    if j == 0:
                        pe.wait_ge(y_ok, KT)
                    pe.wait_ge(zz_lo, j + 1)
                    rows_of(c + 8 + j, 2 * j, first=(j == 0), final=(j == 3))

            def lru():
                c = FIRST["lru"]
                turn("lru")
                open_acc("lru")
                input_ready("lru")
                for j in range(8):
                    if j >= 4:
                        pe.wait_ge(lp_ok, j - 3)
                    columns(c + j, 4 + j % 4)
                chunk_ready(c + 9)
                rh, rl = parts(c + 8, (8, L))
                ih, il = parts(c + 9, (8, L))
                pe.wait_ge(xc_ok, 2)
                for m in range(KT):
                    h, j = m // 2, m % 2
                    pe.wait_ge(lp_ok, 5 + min(m, 3)) if m < 4 else pe.wait_ge(lg_ok, m - 3)
                    for g, (wh, wl) in enumerate(((rh, rl), (ih, il))):
                        for k in range(2):
                            last = mm3(ps[:, 4 + m % 4, g * L:(g + 1) * L], wh[:, 2 * h + k, j * P:(j + 1) * P],
                                       wl[:, 2 * h + k, j * P:(j + 1) * P], xhi[:, 2 * h + k, :], xlo[:, 2 * h + k, :], k == 0, k == 1)
                    if m < KT - 1:
                        last.then_inc(lg_ps, 1)
                last.then_inc(w_used, 2)
                for j in range(4):
                    pe.wait_ge(hg_lo, j // 2 + 1)
                    rows_of(c + 10 + j, 2 * j, final=(j == 3))

            def kv():
                c = FIRST["kv"]
                turn("kv")
                pe.wait_ge(acc_free, 2 * ACC["kv"])
                input_ready("kv")
                for j in range(4):
                    columns(c + j, 4 + j)
                project(c + 4, src=(xhi, xlo))

            def att():
                c = FIRST["att"]
                turn("att")
                pe.wait_ge(acc_free, 2 * ACC["att"])
                input_ready("att")
                for j in range(4):
                    columns(c + j, 4 + j)
                pe.wait_ge(q_ok, 8)
                attention(1, qT2, kT2, V2, False)
                project(c + 4)

            pe.wait_ge(const_ok, 1)
            pe.wait_ge(s5_in, 16 * 21)
            pe.wait_ge(s5p_pool, 1)
            for k in range(3):
                last = pe.transpose(ps[:, k, 0:PAIRS], a_rows[:, k, :], ident[0:PAIRS, 0:PAIRS])
            last.then_inc(s5p_ps, 1)
            pe.wait_ge(s5p_pool, 3)
            for r, src in enumerate((b_dg, c_pad)):
                if r:
                    pe.wait_ge(s5t_ok, 4)
                for q in range(4):
                    for j in range(4):
                        m, ri = (4 * q + j) // 2, j % 2
                        blk = b_dg[:, m, ri, :, :] if r == 0 else c_pad[:, m, ri, :]
                        last = pe.transpose(ps[:, q, j * P:(j + 1) * P], blk, ident[:, :])
                    last.then_inc(s5p_ps, 1)
            pe.wait_ge(mod0_sum, 1)
            spread_mod(halves(GA[:, :], 2) + halves(BA[:, :], 2), (4, 5, 6, 7))
            pe.wait_ge(modb_out, 4)
            run = {"mla": mla, "s5": s5, "lru": lru, "kv": kv, "att": att}
            for name in phases:
                run[name]() if name in run else (mlp if name in MLPS else ffn)(name)

        @block.scalar
        def _(act):
            steps = Steps(act, act_step)
            spread = [0]

            def hi(c, i=None, extra=0):
                if i is None and c >= total + extra:
                    return
                act.wait_ge(raw_in[c % RAW], 16 * (c // RAW + 1) if i is None else i * 32 + 16 * (c // RAW + 1))
                if c >= SPL:
                    act.wait_ge(w_used, c - SPL + 1 if i is None else i * 6 + (c - SPL + 1))
                n = width.get(c, CH) if i is None else CH
                act.activation(whi[:, c % SPL, 0:n], raw[:, c % RAW, 0:n], ACT.Copy).then_inc(hi_done, 1)

            def acc_wait(name, tt):
                if tt == 0:
                    act.wait_ge(acc_half, ACC[name] + 1)
                else:
                    act.wait_ge(w_used, FIRST[name] + dict(PHASES)[name])

            def turned(name):
                for tt in range(T):
                    for hf in range(2):
                        act.wait_ge(xt_ps, 4 * XTS[name] + 2 * tt + hf + 1)
                        act.activation(xhi[:, 4 * hf:4 * hf + 4, tt * P:(tt + 1) * P],
                                       ps[:, 4 + 2 * tt + hf, :].rearrange("p (k n) -> p k n", k=4), ACT.Copy).then_inc(xhi_ok, 1)

            def despread(dsts):
                for dst, b, add in dsts:
                    spread[0] += 1
                    act.wait_ge(modb_ps, spread[0])
                    act.activation(dst, ps[:, b, :], ACT.Copy, bias=add).then_inc(modb_out, 1)

            def half_rows(ap, banks, add):
                return [(ap[:, 512 * q:512 * (q + 1)], b, add) for q, b in enumerate(banks)]

            def squares(name, tt):
                acc_wait(name, tt)
                for n in range(2):
                    last = act.activation(H[:, tt, n * 512:(n + 1) * 512], ps[:, 2 * tt + n, :], ACT.Square,
                                          accum_out=ssq[:, 2 * tt + n:2 * tt + n + 1])
                last.then_inc(sq_done, 1)

            glues = [0]

            def rms_glue(name, norm=True):
                for tt in range(T):
                    squares(name, tt)
                if norm:
                    norm_squares()
                glues[0] += 1

            def norm_squares():
                for tt in range(T):
                    xs[0] += 1
                    act.wait_ge(x_new, xs[0])
                    act.activation(Y[:, tt, :], X[:, tt, :], ACT.Square, accum_out=ssq[:, 4 + tt:5 + tt]).then_inc(sq_done, 1)

            xs = [0]

            def mlp(name):
                l, h, c = MLPS.index(name), HID0[name], FIRST[name]
                turned(name)
                if l == 0:
                    act.wait_ge(small2_in, 16 * 13)

                def hidden(k, i=None):
                    act.wait_ge(w_used, c + 2 * k + 1 if i is None else i * 6 + (c + 2 * k + 1))
                    s = k % 3
                    for m in range(2):
                        b = b1c[:, 32 * l + 2 * k + m:32 * l + 2 * k + m + 1] if i is None else b1c[:, bass.ds(i * 6 + (32 * l + 2 * k + m), 1)]
                        steps.did(act.activation(TMP[:, 512 * s + m * L:512 * s + (m + 1) * L], ps[:, 4 + s, m * L:(m + 1) * L],
                                                 ACT.Relu, bias=b))
                    steps.settle()
                    act.activation(hhi[:, 2 * s:2 * s + 2, :].rearrange("p k l -> p (k l)"), TMP[:, 512 * s:512 * (s + 1)],
                                   ACT.Square).then_inc(hid_hi, 1)

                for a, b in mlp_runs(name):
                    with act.Fori(a, b) as i:
                        steps.loop(i, a, 6)
                        for k in range(3):
                            hidden(k, i)
                            hi(c + 3 + 2 * k, i)
                            hi(c + 4 + 2 * k, i)
                    steps.end(b - a)
                    if a == 0 and name == "mlp0":
                        despread(half_rows(B[:, :], (5, 6), 0.0) + half_rows(A[:, :], (7,), 1.0))
                        despread([(A[:, 512:1024], 5, 1.0)] + half_rows(G[:, 0, :], (6, 7), 1.0))
                hidden(15)
                hi(c + 33)
                hi(c + 34)

            def ffn(name):
                h, c = HID0[name], FIRST[name]
                s0 = h - HID0["ffn10"]
                turned(name)

                def gate(k, i=None):
                    act.wait_ge(w_used, c + 3 * k + 1 if i is None else i * 6 + (c + 3 * k + 1))
                    act.activation(TMP[:, 512 * (k % 2):512 * (k % 2 + 1)], ps[:, 4 + k % 2, :], ACT.Silu).then_inc(act1, 1)

                def hidden(k, i=None):
                    act.wait_ge(prod, s0 + k + 1 if i is None else i * 2 + (s0 + k + 1))
                    s = k % 2
                    act.activation(hhi[:, 2 * s:2 * s + 2, :].rearrange("p k l -> p (k l)"), TMP[:, 1024 + 512 * s:1536 + 512 * s],
                                   ACT.Copy).then_inc(hid_hi, 1)

                with act.Fori(0, 5) as i:
                    for k in range(2):
                        gate(k, i)
                        hi(c + 3 + 3 * k, i)
                        hidden(k, i)
                        hi(c + 4 + 3 * k, i)
                        hi(c + 5 + 3 * k, i)
                gate(10)
                hidden(10)
                hi(c + 33)
                hi(c + 34)

            def rope_table():
                act.wait_ge(rope_r, 1)
                rr = AR[:, 0:64].rearrange("p (t n) -> p t n", t=T)
                hh = AR[:, 64:128].rearrange("p (t n) -> p t n", t=T)
                act.activation(rope[:, 1, :, :], rr, ACT.Sin)
                steps.did(act.activation(hh, rr, ACT.Sin, scale=0.5))
                steps.settle()
                steps.did(act.activation(hh, hh, ACT.Square))
                steps.settle()
                act.activation(rope[:, 0, :, :], hh, ACT.Copy, scale=-2.0, bias=1.0).then_inc(rope_tab, 1)

            def mla():
                turned("mla")
                hi(3)
                for tt in range(T):
                    act.wait_ge(w_used, 2)
                    act.activation(qpT[:, tt, 0:QL], ps[:, tt, 0:QL], ACT.Square, accum_out=ssq[:, 2 * tt:2 * tt + 1])
                    act.activation(qpT[:, 2 + tt, 0:KVL], ps[:, tt, QL:QL + KVL], ACT.Square, accum_out=ssq[:, 2 * tt + 1:2 * tt + 2]).then_inc(z_sq, 1)
                hi(4)
                act.wait_ge(zt_ps, 1)
                act.activation(xhi[:, 2, :], ps[:, 5, 0:L], ACT.Copy)
                act.activation(kpT, ps[:, 5, L:2 * L], ACT.Copy).then_inc(zhi_ok, 1)
                act.activation(xhi[:, 0:2, :].rearrange("p k l -> p (k l)"), ps[:, 4, :], ACT.Copy).then_inc(zhi_ok, 1)
                for b in range(4):
                    act.wait_ge(k_ps, b + 1)
                    act.activation(kT[:, 2 * b:2 * b + 2, :].rearrange("p h l -> p (h l)"), ps[:, b, :], ACT.Copy).then_inc(k_ok, 1)
                hi(5)
                for g in range(2):
                    for b in range(2):
                        act.wait_ge(q_ps, 2 * g + b + 1)
                        act.activation(qT[:, 4 * g + 2 * b:4 * g + 2 * b + 2, :].rearrange("p h l -> p (h l)"), ps[:, b, :], ACT.Copy).then_inc(q_ok, 1)
                    hi(6 + g)
                    act.wait_ge(qt_ps, g + 1)
                    act.activation(qpT[:, 2 * g:2 * g + 2, :].rearrange("p r l -> p (r l)"), ps[:, 3, :], ACT.Copy).then_inc(qt_ok, 1)
                attention(0)
                despread(half_rows(G[:, 0, :], (6, 7), 1.0))
                hi(8)
                hi(9)
                despread(half_rows(B[:, :], (4, 5), 0.0) + half_rows(A[:, :], (6, 7), 1.0))
                hi(10)
                despread(half_rows(G[:, 1, :], (4, 5), 1.0))
                hi(11)
                softplus()

            def attention(n):
                sms, pts = (sm, sm2)[n], (pt, pt2)[n]
                for i in range(HEADS + 2):
                    if i < HEADS:
                        h, e = i, HEADS * n + i
                        act.wait_ge(mx_ok, e + 1)
                        for tt, (lo, up) in enumerate(((0, P), (P, 3 * P))):
                            last = act.activation(sms[:, h % 2, lo:up], sms[:, h % 2, lo:up], ACT.Exp, bias=attm[:, 2 * (h % 2) + tt:2 * (h % 2) + tt + 1],
                                                  accum_out=atts[:, 2 * (h % 2) + tt:2 * (h % 2) + tt + 1])
                        last.then_inc(exp_ok, 1)
                    if 1 <= i <= HEADS:
                        h, e = i - 1, HEADS * n + i - 1
                        act.wait_ge(pt_ps, e + 1)
                        if e >= 2:
                            act.wait_ge(o_ps, e - 1)
                        act.activation(pts[:, h % 2, :], ps[:, 2 + h % 2, 0:3 * P], ACT.Copy).then_inc(pt_ok, 1)
                    if i >= 2:
                        h, e = i - 2, HEADS * n + i - 2
                        act.wait_ge(o_ps, e + 1)
                        act.activation(hhi[:, h, :], ps[:, 4 + h % 2, 0:L], ACT.Copy).then_inc(o_hi, 1)

            def s5():
                c = FIRST["s5"]
                turned("s5")
                despread(half_rows(B[:, :], (0, 1), 0.0) + half_rows(A[:, :], (2, 3), 1.0))
                for j in range(4):
                    act.wait_ge(w_used, c + j + 1)
                    act.activation(uT[:, 2 * j:2 * j + 2, :].rearrange("p k l -> p (k l)"), ps[:, 4 + j, :], ACT.Copy).then_inc(u_ok, 1)
                    hi(c + 3 + j)
                despread(half_rows(G[:, 1, :], (0, 1), 1.0))
                for i in range(PAIRS):
                    s = i % 2
                    act.wait_ge(phase_r, i + 1)
                    if i >= 2:
                        act.wait_ge(x_rot, i - 1)
                    act.activation(tabs[:, s, 1, :], ph[:, s, 0, :], ACT.Sin, scale=TWO_PI * (1 - 2.0 ** -22))
                    steps.did(act.activation(half[:, 0, :], ph[:, s, 0, :], ACT.Sin, scale=math.pi))
                    steps.settle()
                    steps.did(act.activation(half[:, 1, :], half[:, 0, :], ACT.Square))
                    steps.settle()
                    act.activation(tabs[:, s, 0, :], half[:, 1, :], ACT.Copy, scale=-2.0, bias=1.0).then_inc(table_ok, 1)
                yf = Y.rearrange("p t d -> p (t d)")
                gx = xhi[:, :, :].rearrange("p k l -> p (k l)")
                for q in range(2):
                    act.wait_ge(y_ok, 4 * q + 4)
                    act.activation(yf[:, 1024 * q:1024 * (q + 1)], yf[:, 1024 * q:1024 * (q + 1)], ACT.Gelu_apprx_tanh).then_inc(g_act, 1)
                    act.wait_ge(g_act, q + 1)
                    act.activation(gx[:, 1024 * q:1024 * (q + 1)], yf[:, 1024 * q:1024 * (q + 1)], ACT.Copy).then_inc(g_hi, 1)
                for j in range(4):
                    act.wait_ge(w_used, c + 4 + j + 1)
                    if j >= 2:
                        act.wait_ge(zz_ok, j - 1)
                    for m in range(2):
                        last = act.activation(sig[:, j % 2, m * L:(m + 1) * L], ps[:, 4 + j, m * L:(m + 1) * L], ACT.Sigmoid,
                                              bias=bglu[:, 2 * j + m:2 * j + m + 1])
                    last.then_inc(sig_ok, 1)
                    hi(c + 7 + j)
                    act.wait_ge(zz_ok, j + 1)
                    act.activation(hhi[:, 2 * j:2 * j + 2, :].rearrange("p k l -> p (k l)"), zz[:, j % 2, :], ACT.Copy).then_inc(zz_hi, 1)
                for j in range(4):
                    hi(c + 11 + j)

            def lru():
                c = FIRST["lru"]
                turned("lru")
                for j in range(4):
                    act.wait_ge(w_used, c + j + 1)
                    for m in range(2):
                        last = act.activation(xbp[:, 2 * j + m, 3:], ps[:, 4 + j, m * L:(m + 1) * L], ACT.Identity,
                                              bias=lru_bin[:, 2 * j + m:2 * j + m + 1])
                    last.then_inc(lp_ok, 1)
                    hi(c + 3 + j)
                for j in range(4, 8):
                    act.wait_ge(w_used, c + j + 1)
                    for m in range(2):
                        last = act.activation(gyT[:, 2 * (j - 4) + m, :], ps[:, j, m * L:(m + 1) * L], ACT.Gelu_apprx_tanh,
                                              bias=lru_bin[:, 2 * j + m:2 * j + m + 1])
                    last.then_inc(lp_ok, 1)
                    hi(c + 3 + j)
                for q in range(2):
                    act.wait_ge(conv_ok, q + 1)
                    act.activation(xhi[:, 4 * q:4 * q + 4, :], xcT[:, 4 * q:4 * q + 4, :], ACT.Copy).then_inc(xc_hi, 1)
                for m in range(KT):
                    if m < KT - 1:
                        act.wait_ge(lg_ps, m + 1)
                    else:
                        act.wait_ge(w_used, c + 10)
                    act.activation(rT[:, m, :], ps[:, 4 + m % 4, 0:L], ACT.Sigmoid, bias=lru_br[:, m:m + 1])
                    act.activation(iT[:, m, :], ps[:, 4 + m % 4, L:2 * L], ACT.Sigmoid, bias=lru_bi[:, m:m + 1]).then_inc(lg_ok, 1)
                for q in range(2):
                    act.wait_ge(lg_ok, 4 * q + 4)
                    for m in range(4 * q, 4 * q + 4):
                        act.activation(aT[:, m, :], rT[:, m, :], ACT.Exp, scale=lam_n[:, m:m + 1])
                        last = act.activation(tT[:, m, :], rT[:, m, :], ACT.Tanh, scale=lam_p[:, m:m + 1])
                    last.then_inc(la_ok, 1)
                hi(c + 11)
                for q in range(2):
                    act.wait_ge(m2_ok, q + 1)
                    act.activation(tT[:, 4 * q:4 * q + 4, :], tT[:, 4 * q:4 * q + 4, :], ACT.Sqrt, scale=2.0).then_inc(mult_ok, 1)
                hi(c + 12)
                for q in range(2):
                    act.wait_ge(hg_ok, q + 1)
                    act.activation(hhi[:, 4 * q:4 * q + 4, :], aT[:, 4 * q:4 * q + 4, :], ACT.Copy).then_inc(hg_hi, 1)
                for j in range(4):
                    hi(c + 13 + j)

            def softplus():
                act.wait_ge(lam_ok, 1)
                steps.did(act.activation(lam_p, lam_n, ACT.Exp, scale=-1.0))
                steps.settle()
                act.activation(lam_p, lam_p, ACT.Ln, bias=1.0).then_inc(lam_exp, 1)

            def kv():
                c = FIRST["kv"]
                turned("kv")
                for j in range(4):
                    act.wait_ge(w_used, c + j + 1)
                    act.activation(kT2[:, 2 * j:2 * j + 2, :].rearrange("p k l -> p (k l)"), ps[:, 4 + j, :], ACT.Copy).then_inc(k_ok, 1)
                    hi(c + 3 + j)
                for j in range(4):
                    hi(c + 7 + j)

            def att():
                c = FIRST["att"]
                turned("att")
                for j in range(4):
                    act.wait_ge(w_used, c + j + 1)
                    act.activation(qT2[:, 2 * j:2 * j + 2, :].rearrange("p k l -> p (k l)"), ps[:, 4 + j, :], ACT.Copy).then_inc(q_ok, 1)
                    hi(c + 3 + j)
                attention(1)
                for j in range(4):
                    hi(c + 7 + j)

            act.wait_ge(c_in, 16)
            act.activation(csil, craw, ACT.Silu).then_inc(csil_ok, 1)
            for k, src in enumerate((t["ssm_a_re"][0], t["ssm_a_im"][0])):
                act.dma_start(a_rows[:, k, :], src.rearrange("(q g) p -> q (g p)", g=2)).then_inc(s5_in, 16)
            act.dma_start(ldt_rows, t["ssm_log_dt"][0].rearrange("(q g) -> q g", g=2)).then_inc(s5_in, 16)
            for r, src in enumerate((t["ssm_b_re"][0], t["ssm_b_im"][0])):
                act.dma_start(b_in[:, r, :, :], src.rearrange("(q g) p c -> (g p) q c", g=2)).then_inc(s5_in, 16)
            act.wait_ge(const_ok, 1)
            for r, src in enumerate((t["ssm_c_re"][0], t["ssm_c_im"][0])):
                v = src.rearrange("(m i g) c p -> i g c m p", m=KT, i=4)
                for i in range(4):
                    for g in range(2):
                        a = 32 * i + 16 * g
                        act.dma_start(c_pad[a:a + 16, :, r, 64 * g:64 * g + 64], v[i, g]).then_inc(s5_in, 16)
            act.wait_ge(s5p_ps, 1)
            for k in range(3):
                last = act.activation(g0v[:, k, :], ps[:, k, 0:PAIRS], ACT.Copy)
            last.then_inc(s5p_act, 1)
            act.wait_ge(s5p_act, 1)
            act.activation(g0v[:, 2, :], g0v[:, 2, :], ACT.Exp).then_inc(s5p_act, 1)
            act.wait_ge(s5p_pool, S5P_ANGLE)
            act.activation(rho, g0v[:, 3, :], ACT.Exp).then_inc(s5p_act, 1)
            act.activation(g0v[:, 6, :], g0v[:, 5, :], ACT.Sin)
            act.activation(g0v[:, 7, :], g0v[:, 5, :], ACT.Sin, scale=0.5).then_inc(s5p_act, 1)
            act.wait_ge(s5p_act, 4)
            act.activation(g0v[:, 7, :], g0v[:, 7, :], ACT.Square).then_inc(s5p_act, 1)
            act.wait_ge(s5p_act, 5)
            act.activation(g0v[:, 7, :], g0v[:, 7, :], ACT.Copy, scale=-2.0, bias=1.0).then_inc(s5p_act, 1)
            for q in range(8):
                act.wait_ge(s5p_ps, q + 2)
                if q == 4:
                    act.wait_ge(s5_stored, 16)
                st = s5_stage.rearrange("p m r n -> p (m r n)")[:, (q % 4) * 512:(q % 4 + 1) * 512]
                act.activation(st, ps[:, q % 4, :], ACT.Copy).then_inc(s5t_ok, 1)
                if q >= 4:
                    act.wait_ge(s5t_ok, q + 1)
                    si = st.rearrange("p (m r n) -> p m r n", m=2, r=2)[:, :, 1, :]
                    steps.did(act.activation(si, si, ACT.Copy, scale=-1.0))
                if q % 4 == 3:
                    steps.settle() if q == 7 else act.wait_ge(s5t_ok, 4)
                    act.dma_start(s5_store[q // 4], s5_stage.rearrange("p m r n -> p (m r n)")).then_inc(s5_stored, 16)
            for c in range(3):
                hi(c)
            despread(half_rows(B[:, :], (4, 5), 0.0) + half_rows(A[:, :], (6, 7), 1.0))
            rope_table()
            for name in phases:
                {"mla": mla, "s5": s5, "lru": lru, "kv": kv, "att": att}.get(name, None)() if name in ("mla", "s5", "lru", "kv", "att") else \
                    (mlp if name in MLPS else ffn)(name)
                if name in ("ffn10", "lru", "ffn20", "ffn11", "att", "ffn21"):
                    rms_glue(name, name != "ffn21")
                if name == "mlp1":
                    norm_squares()
                if name in FFNS:
                    hi(FIRST[name] + 35)
            act.wait_ge(s5_stored, 32)


        @block.vector
        def _(dve):
            steps = Steps(dve, dve_step)
            spare = small[0:1, 511:512]
            sq, xn = [0], [0]

            def do(ins):
                steps.did(ins)
                steps.settle()

            def lo(c, i=None):
                if i is None and c >= total:
                    return
                dve.wait_ge(hi_done, c + 1 if i is None else i * 6 + (c + 1))
                n = width.get(c, CH) if i is None else CH
                dve.tensor_tensor(wlo[:, c % SPL, 0:n], raw[:, c % RAW, 0:n], whi[:, c % SPL, 0:n].bitcast(F32),
                                  ALU.subtract).then_inc(lo_done, 1)

            def rest(dst, src, hi_part):
                return dve.tensor_tensor(dst, src, hi_part.bitcast(F32), ALU.subtract)

            def rsqrt(dst, src, n):
                y, tmp = newton[:, 0:n], newton[:, 8:8 + n]
                do(dve.tensor_scalar(tmp.bitcast(I32), src.bitcast(I32), 1, None, ALU.logical_shift_right))
                do(dve.tensor_scalar(y.bitcast(I32), tmp.bitcast(I32), -1, 0x5F3759DF, ALU.mult, ALU.add))
                for it in range(3):
                    do(dve.tensor_tensor(tmp, y, y, ALU.mult))
                    do(dve.scalar_tensor_tensor(tmp, tmp, -0.5, src, ALU.mult, ALU.mult))
                    do(dve.scalar_tensor_tensor(dst if it == 2 else y, tmp, 1.5, y, ALU.add, ALU.mult))

            def acc_wait(name, tt):
                if tt == 0:
                    dve.wait_ge(acc_half, ACC[name] + 1)
                else:
                    dve.wait_ge(w_used, FIRST[name] + dict(PHASES)[name])

            def acc_tile(tt):
                return ps[:, 2 * tt:2 * tt + 2, :].rearrange("p b n -> p (b n)")

            def turned(name):
                for tt in range(T):
                    for hf in range(2):
                        dve.wait_ge(xhi_ok, 4 * XTS[name] + 2 * tt + hf + 1)
                        rest(xlo[:, 4 * hf:4 * hf + 4, tt * P:(tt + 1) * P],
                             ps[:, 4 + 2 * tt + hf, :].rearrange("p (k n) -> p k n", k=4),
                             xhi[:, 4 * hf:4 * hf + 4, tt * P:(tt + 1) * P]).then_inc(xt_ok, 1)

            def row_read(name, s, n):
                dve.wait_ge(s, n)
                dve.memset(spare, 0.0).then_inc(row_used, 1)
                dve.wait_ge(row_used, ROW_INDEX[name] - ROW_FIRST + 1)

            def normed(name, nxt):
                pre = "pre_" + nxt
                for tt in range(T):
                    if name is not None:
                        sq[0] += 1
                        dve.wait_ge(sq_done, sq[0])
                        do(dve.tensor_scalar(mv[:, tt:tt + 1], ssq[:, 4 + tt:5 + tt], 1.0 / D, 1e-6, ALU.mult, ALU.add))
                        rsqrt(rsq[:, 2 + tt:3 + tt], mv[:, tt:tt + 1], 1)
                    if tt == 0:
                        row_wait(dve, pre)
                    dve.scalar_tensor_tensor(H[:, tt, :], X[:, tt, :], rsq[:, 2 + tt:3 + tt], row(pre), ALU.mult, ALU.mult).then_inc(h_ready, 1)
                row_read(pre, h_ready, 2 * XTS[nxt] + 2)

            def ln_glue(name):
                k = {"mla": 1, "mlp0": 2, "s5": 3, "mlp1": 4}[name]
                for tt in range(T):
                    acc_wait(name, tt)
                    if tt == 0:
                        dve.wait_ge(modb_out, (6, 12, 18, 24)[k - 1])
                        if k == 1:
                            dve.wait_ge(x_scaled, 1)
                        else:
                            dve.wait_ge(res_ok, 2 * (k - 1))
                    dve.tensor_tensor(Y[:, tt, :], acc_tile(tt), G[:, (k - 1) % 2, :], ALU.mult).then_inc(acc_free, 1)
                    dve.wait_ge(acc_free, 2 * ACC[name] + tt + 1)
                    do(dve.tensor_tensor(Y[:, tt, :], Y[:, tt, :], X[:, tt, :], ALU.add))
                    for n in range(2):
                        steps.did(dve.bn_stats(stats[:, 12 * tt + 6 * n:12 * tt + 6 * n + 6], Y[:, tt, n * 512:(n + 1) * 512]))
                    steps.settle()
                    do(dve.bn_aggr(mv[:, 2 * tt:2 * tt + 2], stats[:, 12 * tt:12 * tt + 12]))
                    do(dve.tensor_scalar(ssq[:, 6 + tt:7 + tt], mv[:, 2 * tt + 1:2 * tt + 2], 1e-5, None, ALU.add))
                    rsqrt(rsq[:, tt:tt + 1], ssq[:, 6 + tt:7 + tt], 1)
                    dve.scalar_tensor_tensor(nmr[:, tt:tt + 1], mv[:, 2 * tt:2 * tt + 1], -1.0, rsq[:, tt:tt + 1], ALU.mult, ALU.mult).then_inc(ln_stats, 1)
                    if tt == 0:
                        if k < 4:
                            dve.wait_ge(vec_done, k)
                        else:
                            row_wait(dve, "lg4")
                            row_wait(dve, "lb4")
                    do(dve.scalar_tensor_tensor(H[:, tt, :], Y[:, tt, :], mv[:, 2 * tt:2 * tt + 1], A[:, :], ALU.subtract, ALU.mult))
                    dst, s = (H, h_ready) if k < 4 else (X, x_new)
                    dve.scalar_tensor_tensor(dst[:, tt, :], H[:, tt, :], rsq[:, tt:tt + 1], B[:, :], ALU.mult, ALU.add).then_inc(s, 1)
                if k < 4:
                    dve.wait_ge(h_ready, 2 * XTS[name] + 4)
                else:
                    xn[0] += 2
                    dve.wait_ge(x_new, xn[0])
                dve.memset(spare, 0.0).then_inc(glue_done, 1)
                dve.wait_ge(glue_done, k + 1)
                if k == 4:
                    normed(name, "ffn10")

            def rms_glue(name, nxt):
                w = 4.0 if name in FFNS else 1.0
                post = "post_" + name
                for tt in range(T):
                    sq[0] += 1
                    dve.wait_ge(sq_done, sq[0])
                    do(dve.tensor_tensor(mv[:, tt:tt + 1], ssq[:, 2 * tt:2 * tt + 1], ssq[:, 2 * tt + 1:2 * tt + 2], ALU.add))
                    do(dve.tensor_scalar(mv[:, tt:tt + 1], mv[:, tt:tt + 1], w / D, w * 1e-6, ALU.mult, ALU.add))
                    rsqrt(rsq[:, tt:tt + 1], mv[:, tt:tt + 1], 1)
                    if tt == 0:
                        row_wait(dve, post)
                    dve.scalar_tensor_tensor(Y[:, tt, :], acc_tile(tt), rsq[:, tt:tt + 1], row(post), ALU.mult, ALU.mult).then_inc(acc_free, 1)
                    dve.wait_ge(acc_free, 2 * ACC[name] + tt + 1)
                    dve.tensor_tensor(X[:, tt, :], X[:, tt, :], Y[:, tt, :], ALU.add).then_inc(x_new, 1)
                row_read(post, acc_free, 2 * ACC[name] + 2)
                xn[0] += 2
                dve.wait_ge(x_new, xn[0])
                if nxt is not None:
                    normed(name, nxt)

            def mlp(name):
                h, c = HID0[name], FIRST[name]
                turned(name)

                def hidden(k, i=None):
                    dve.wait_ge(hid_hi, h + k + 1 if i is None else i * 3 + (h + k + 1))
                    s = k % 3
                    r = TMP[:, 512 * s:512 * (s + 1)]
                    do(dve.tensor_tensor(TMP[:, 1536:2048], r, r, ALU.mult))
                    rest(hlo[:, 2 * s:2 * s + 2, :].rearrange("p k l -> p (k l)"), TMP[:, 1536:2048],
                         hhi[:, 2 * s:2 * s + 2, :].rearrange("p k l -> p (k l)")).then_inc(hid_ok, 1)

                for a, b in mlp_runs(name):
                    with dve.Fori(a, b) as i:
                        steps.loop(i, a, 3)
                        for k in range(3):
                            hidden(k, i)
                            lo(c + 3 + 2 * k, i)
                            lo(c + 4 + 2 * k, i)
                    steps.end(b - a)
                hidden(15)
                lo(c + 33)
                lo(c + 34)

            def ffn(name):
                h, c = HID0[name], FIRST[name]
                s0 = h - HID0["ffn10"]
                turned(name)

                def product(k, i=None):
                    dve.wait_ge(act1, s0 + k + 1 if i is None else i * 2 + (s0 + k + 1))
                    dve.wait_ge(w_used, c + 3 * k + 2 if i is None else i * 6 + (c + 3 * k + 2))
                    s = k % 2
                    dve.tensor_tensor(TMP[:, 1024 + 512 * s:1536 + 512 * s], TMP[:, 512 * s:512 * (s + 1)], ps[:, 6 + s, :],
                                      ALU.mult).then_inc(prod, 1)

                def hidden(k, i=None):
                    dve.wait_ge(hid_hi, h + k + 1 if i is None else i * 2 + (h + k + 1))
                    s = k % 2
                    rest(hlo[:, 2 * s:2 * s + 2, :].rearrange("p k l -> p (k l)"), TMP[:, 1024 + 512 * s:1536 + 512 * s],
                         hhi[:, 2 * s:2 * s + 2, :].rearrange("p k l -> p (k l)")).then_inc(hid_ok, 1)

                with dve.Fori(0, 5) as i:
                    for k in range(2):
                        lo(c + 3 + 3 * k, i)
                        product(k, i)
                        hidden(k, i)
                        lo(c + 4 + 3 * k, i)
                        lo(c + 5 + 3 * k, i)
                product(10)
                hidden(10)
                lo(c + 33)
                lo(c + 34)

            def table(k, tt, heads):
                return rope[:, k, tt, :].rearrange("p (h x n) -> p h x n", h=1, x=1).to_broadcast([P, heads, 2, 32])

            def rotate(dsts, src, tt, heads):
                n = heads * ROPE
                a, b = (rt.rearrange("p s n -> p (s n)")[:, q * 256:q * 256 + n].rearrange("p (h x n) -> p h x n", h=heads, x=2) for q in range(2))
                x = src.rearrange("p (h x n) -> p h x n", h=heads, x=2)
                steps.did(dve.tensor_tensor(a, x, table(0, tt, heads), ALU.mult))
                do(dve.tensor_tensor(b, x, table(1, tt, heads), ALU.mult))
                for dst in dsts:
                    d = dst.rearrange("p (h x n) -> p h x n", h=heads, x=2)
                    dve.tensor_tensor(d[:, :, 0, :], a[:, :, 0, :], b[:, :, 1, :], ALU.subtract)
                    last = dve.tensor_tensor(d[:, :, 1, :], b[:, :, 0, :], a[:, :, 1, :], ALU.add)
                return last

            def mla():
                turned("mla")
                lo(3)
                for tt in range(T):
                    dve.wait_ge(z_sq, tt + 1)
                    do(dve.tensor_scalar(mv[:, 0:1], ssq[:, 2 * tt:2 * tt + 1], 1.0 / QL, 1e-6, ALU.mult, ALU.add))
                    do(dve.tensor_scalar(mv[:, 1:2], ssq[:, 2 * tt + 1:2 * tt + 2], 1.0 / KVL, 1e-6, ALU.mult, ALU.add))
                    rsqrt(rsq[:, 2 * tt:2 * tt + 2], mv[:, 0:2], 2)
                    dve.scalar_tensor_tensor(zn[:, tt, 0:QL], ps[:, tt, 0:QL], rsq[:, 2 * tt:2 * tt + 1], G[:, 1, 0:QL], ALU.mult, ALU.mult)
                    dve.scalar_tensor_tensor(zn[:, tt, QL:QL + KVL], ps[:, tt, QL:QL + KVL], rsq[:, 2 * tt + 1:2 * tt + 2],
                                             G[:, 1, QL:QL + KVL], ALU.mult, ALU.mult)
                    if tt == 0:
                        dve.wait_ge(rope_tab, 1)
                    rotate([zn[:, tt, 384:448], zn[:, tt, 448:512]], ps[:, tt, QL + KVL:ZW], tt, 1).then_inc(zn_ok, 1)
                    dve.wait_ge(zn_ok, tt + 1)
                lo(4)
                dve.wait_ge(zhi_ok, 1)
                rest(xlo[:, 2, :], ps[:, 5, 0:L], xhi[:, 2, :]).then_inc(zx_ok, 1)
                dve.wait_ge(zhi_ok, 2)
                rest(xlo[:, 0:2, :].rearrange("p k l -> p (k l)"), ps[:, 4, :], xhi[:, 0:2, :].rearrange("p k l -> p (k l)")).then_inc(zx_ok, 1)
                for tt in range(T):
                    dve.wait_ge(v_ps, 1) if tt == 0 else dve.wait_ge(w_used, 3)
                    dve.tensor_copy(V[:, tt, :], ps[:, 4 + 2 * tt:6 + 2 * tt, :].rearrange("p b n -> p (b n)")).then_inc(v_ok, 1)
                lo(5)
                for g in range(2):
                    dve.wait_ge(w_used, 4 + g)
                    if g:
                        dve.wait_ge(qt_ps, 1)
                    for tt in range(T):
                        last = rotate([qp_tok[:, tt, :]], ps[:, 2, tt * L:(tt + 1) * L], tt, 4)
                        if tt == 0:
                            do(last)
                    last.then_inc(qp_ok, 1)
                    dve.wait_ge(qp_ok, g + 1)
                    lo(6 + g)
                attention(0)
                for c in range(8, 12):
                    lo(c)
                dve.wait_ge(small2_in, 16 * 13)
                do(dve.tensor_scalar(lam_p, lru_lam, -1.0, None, ALU.mult))
                dve.tensor_tensor(lam_n, lam_p, lru_lam, ALU.max).then_inc(lam_ok, 1)

            def softplus():
                dve.wait_ge(lam_exp, 1)
                do(dve.tensor_scalar(lam_n, lru_lam, -1.0, 0.0, ALU.mult, ALU.max))
                do(dve.tensor_tensor(lam_n, lam_n, lam_p, ALU.add))
                do(dve.tensor_scalar(lam_p, lam_n, 8.0, None, ALU.mult))
                do(dve.tensor_scalar(lam_n, lam_n, -8.0, None, ALU.mult))

            def attention(n):
                sms = (sm, sm2)[n]
                scale = ((NOPE + ROPE) ** -0.5, 128 ** -0.5)[n]
                if n:
                    dve.wait_ge(bias_in, 16)
                for i in range(HEADS + 2):
                    if i < HEADS:
                        h, e = i, HEADS * n + i
                        dve.wait_ge(s_ps, e + 1)
                        if e >= 2:
                            dve.wait_ge(pt_ps, e - 1)
                        s = h % 2
                        bias = relb[:, h, :] if n else mask
                        dve.scalar_tensor_tensor(sms[:, s, 0:P], ps[:, s, 0:P], scale, bias[:, P:2 * P], ALU.mult, ALU.add)
                        dve.scalar_tensor_tensor(sms[:, s, P:3 * P], ps[:, s, P:3 * P], scale, bias[:, 0:L], ALU.mult, ALU.add).then_inc(sm_ok, 1)
                        dve.wait_ge(sm_ok, e + 1)
                        for tt, (a, b) in enumerate(((0, P), (P, 3 * P))):
                            last = dve.tensor_reduce(attm[:, 2 * s + tt:2 * s + tt + 1], sms[:, s, a:b], mybir.AxisListType.X, ALU.max, negate=True)
                        last.then_inc(mx_ok, 1)
                    if 1 <= i <= HEADS:
                        h, e = i - 1, HEADS * n + i - 1
                        s = h % 2
                        dve.wait_ge(exp_ok, e + 1)
                        do(dve.reciprocal(newton[:, 0:2], atts[:, 2 * s:2 * s + 2]))
                        dve.tensor_scalar(sms[:, s, 0:P], sms[:, s, 0:P], newton[:, 0:1], None, ALU.mult)
                        dve.tensor_scalar(sms[:, s, P:3 * P], sms[:, s, P:3 * P], newton[:, 1:2], None, ALU.mult).then_inc(p_ok, 1)
                        dve.wait_ge(p_ok, e + 1)
                    if i >= 2:
                        h, e = i - 2, HEADS * n + i - 2
                        dve.wait_ge(o_hi, e + 1)
                        rest(hlo[:, h, :], ps[:, 4 + h % 2, 0:L], hhi[:, h, :]).then_inc(o_ok, 1)

            def s5():
                c = FIRST["s5"]
                turned("s5")
                for j in range(4):
                    lo(c + 3 + j)
                dve.wait_ge(res_ok, 4)
                dve.wait_ge(u_ok, 4)

                def both(ap):
                    return ap.rearrange("p (k l) -> p k l", k=1).to_broadcast([P, 2, L])

                def out_tile(m):
                    dve.wait_ge(x_used, 4 * m + 4)
                    dve.scalar_tensor_tensor(yT[:, m, :], uT[:, m, :], dskip[:, m:m + 1], ps[:, 2 + m % 2, 0:L], ALU.mult, ALU.add).then_inc(y_ok, 1)

                for i in range(PAIRS + 1):
                    if i < PAIRS:
                        s = i % 2
                        dve.wait_ge(bu_ps, i + 1)
                        dve.wait_ge(table_ok, i + 1)
                        cos, sin = tabs[:, s, 0, :], tabs[:, s, 1, :]
                        dve.tensor_tensor(rot_a[:, s, :].rearrange("p (k l) -> p k l", k=2), ps[:, s, :].rearrange("p (k l) -> p k l", k=2), both(cos), ALU.mult)
                        dve.tensor_tensor(rot_b[:, s, 0:L], ps[:, s, L:2 * L], sin, ALU.mult)
                        dve.scalar_tensor_tensor(rot_b[:, s, L:], ps[:, s, 0:L], -1.0, sin, ALU.mult, ALU.mult).then_inc(bu_rot, 1)
                        dve.wait_ge(bu_rot, i + 1)
                        do(dve.tensor_tensor(rot_a[:, s, :], rot_a[:, s, :], rot_b[:, s, :], ALU.add))
                    if i >= 1:
                        e = i - 1
                        s = e % 2
                        cos, sin = tabs[:, s, 0, :], tabs[:, s, 1, :]
                        for r in range(2):
                            steps.did(dve.tensor_tensor_scan(zst[:, r * L:(r + 1) * L], rho[:, e:e + 1].to_broadcast([P, L]),
                                                             rot_a[:, s, r * L:(r + 1) * L], 0.0, ALU.mult, ALU.add))
                        steps.settle()
                        if e >= 2:
                            dve.wait_ge(x_used, e - 1)
                        dve.tensor_tensor(xa[:, s, :].rearrange("p (k l) -> p k l", k=2), zst.rearrange("p (k l) -> p k l", k=2), both(cos), ALU.mult)
                        dve.scalar_tensor_tensor(xb[:, s, 0:L], zst[:, L:], -1.0, sin, ALU.mult, ALU.mult)
                        dve.tensor_tensor(xb[:, s, L:], zst[:, 0:L], sin, ALU.mult).then_inc(x_rot, 1)
                        dve.wait_ge(x_rot, e + 1)
                        if e % 4 == 0 and e:
                            out_tile(e // 4 - 1)
                out_tile(KT - 1)
                for q in range(2):
                    dve.wait_ge(g_hi, q + 1)
                    rest(xlo[:, 4 * q:4 * q + 4, :], yT[:, 4 * q:4 * q + 4, :], xhi[:, 4 * q:4 * q + 4, :]).then_inc(g_ok, 1)
                for j in range(4):
                    dve.wait_ge(sig_ok, j + 1)
                    if j >= 2:
                        dve.wait_ge(zz_lo, j - 1)
                    dve.tensor_tensor(zz[:, j % 2, :], yT[:, 2 * j:2 * j + 2, :].rearrange("p k l -> p (k l)"), sig[:, j % 2, :], ALU.mult).then_inc(zz_ok, 1)
                    lo(c + 7 + j)
                    dve.wait_ge(zz_hi, j + 1)
                    rest(hlo[:, 2 * j:2 * j + 2, :].rearrange("p k l -> p (k l)"), zz[:, j % 2, :],
                         hhi[:, 2 * j:2 * j + 2, :].rearrange("p k l -> p (k l)")).then_inc(zz_lo, 1)
                for j in range(4):
                    lo(c + 11 + j)

            def lru():
                c = FIRST["lru"]
                turned("lru")
                do(dve.memset(xbp[:, :, 0:3], 0.0))
                for j in range(4):
                    dve.wait_ge(lp_ok, j + 1)
                    tiles = (2 * j, 2 * j + 1)
                    for m in tiles:
                        steps.did(dve.tensor_scalar(xcT[:, m, :], xbp[:, m, 3:3 + L], lru_conv[:, 24 + m:25 + m], lru_cb[:, m:m + 1], ALU.mult, ALU.add))
                    for tap in range(3):
                        steps.settle()
                        for m in tiles:
                            ins = dve.scalar_tensor_tensor(xcT[:, m, :], xbp[:, m, tap:tap + L], lru_conv[:, 8 * tap + m:8 * tap + m + 1],
                                                           xcT[:, m, :], ALU.mult, ALU.add)
                            if tap == 2 and m % 4 == 3:
                                ins.then_inc(conv_ok, 1)
                            else:
                                steps.did(ins)
                    lo(c + 3 + j)
                for j in range(4, 8):
                    lo(c + 3 + j)
                for q in range(2):
                    dve.wait_ge(xc_hi, q + 1)
                    rest(xlo[:, 4 * q:4 * q + 4, :], xcT[:, 4 * q:4 * q + 4, :], xhi[:, 4 * q:4 * q + 4, :]).then_inc(xc_ok, 1)
                hf = lambda ap, q: ap[:, 4 * q:4 * q + 4, :]
                den = work[:, 4096:6144].rearrange("p (m l) -> p m l", m=KT)
                for q in range(2):
                    dve.wait_ge(la_ok, q + 1)
                    do(dve.tensor_scalar(hf(den, q), hf(tT, q), 1.0, None, ALU.add))
                    do(dve.reciprocal(hf(den, q), hf(den, q)))
                    dve.tensor_tensor(hf(tT, q), hf(tT, q), hf(den, q), ALU.mult).then_inc(m2_ok, 1)
                    do(dve.tensor_tensor(hf(iT, q), hf(iT, q), hf(xcT, q), ALU.mult))
                lo(c + 11)
                for q in range(2):
                    dve.wait_ge(mult_ok, q + 1)
                    do(dve.tensor_tensor(hf(tT, q), hf(tT, q), hf(iT, q), ALU.mult))
                    for m in range(4 * q, 4 * q + 4):
                        steps.did(dve.tensor_tensor_scan(rT[:, m, :], aT[:, m, :], tT[:, m, :], 0.0, ALU.mult, ALU.add))
                    steps.settle()
                    dve.tensor_tensor(hf(aT, q), hf(rT, q), hf(gyT, q), ALU.mult).then_inc(hg_ok, 1)
                lo(c + 12)
                for q in range(2):
                    dve.wait_ge(hg_hi, q + 1)
                    rest(hf(hlo, q), hf(aT, q), hf(hhi, q)).then_inc(hg_lo, 1)
                for j in range(4):
                    lo(c + 13 + j)

            def kv():
                c = FIRST["kv"]
                turned("kv")
                if "ffn11" in phases:
                    normed(None, "ffn11")
                for j in range(8):
                    lo(c + 3 + j)
                for tt in range(T):
                    acc_wait("kv", tt)
                    dve.tensor_copy(V2[:, tt, :], acc_tile(tt)).then_inc(acc_free, 1)

            def att():
                c = FIRST["att"]
                turned("att")
                for j in range(4):
                    lo(c + 3 + j)
                attention(1)
                for j in range(4):
                    lo(c + 7 + j)

            acc0 = (GA, BA)
            m0 = [work[:, 2048 * s:2048 * (s + 1)].rearrange("p (k n) -> p k n", k=2) for s in range(4)]
            dve.memset(GA[:, :], 0.0)
            dve.memset(BA[:, :], 0.0).then_inc(acc0_clear, 1)
            dve.wait_ge(csil_ok, 1)
            dve.wait_ge(modb0_in, 32)
            for n in range(8):
                dve.wait_ge(m0_in[n % 4], 16 * (n // 4 + 1))
                a = acc0[n // 4][:, :]
                for kk in range(2):
                    k = 2 * (n % 4) + kk
                    last = dve.scalar_tensor_tensor(a, m0[n % 4][:, kk, :], csil[:, k:k + 1], a, ALU.mult, ALU.add)
                    if kk == 0:
                        do(last)
                if n < 7:
                    last.then_inc(m0_used, 1)
                    dve.wait_ge(m0_used, n + 1)
                else:
                    last.then_inc(mod0_sum, 1)
                    dve.wait_ge(mod0_sum, 1)
            dve.wait_ge(s5p_pool, S5P_ANGLE)
            dve.reciprocal(g0v[:, 8, :], g0v[:, 8, :]).then_inc(s5p_dve, 1)
            for c in range(3):
                lo(c)
            dve.wait_ge(small_in, 64)
            do(dve.tensor_copy(posf, posi.bitcast(I32)))
            ang, turns, red = AR[:, 128:192], AR[:, 192:256], AR[:, 0:64]
            for tt in range(T):
                steps.did(dve.tensor_scalar(ang[:, 32 * tt:32 * tt + 32], invf, posf[:, tt:tt + 1], None, ALU.mult))
            steps.settle()
            do(dve.tensor_scalar(turns, ang, 1 / TWO_PI, MAGIC, ALU.mult, ALU.add))
            do(dve.tensor_scalar(turns, turns, -MAGIC, None, ALU.add))
            do(dve.scalar_tensor_tensor(red, turns, -PI_A, ang, ALU.mult, ALU.add))
            do(dve.scalar_tensor_tensor(red, turns, -PI_B, red, ALU.mult, ALU.add))
            do(dve.scalar_tensor_tensor(red, turns, -PI_C, red, ALU.mult, ALU.add))
            dve.tensor_scalar(red, red, 3.1415925, -3.1415925, ALU.min, ALU.max).then_inc(rope_r, 1)
            dve.wait_ge(x_in, 16)
            dve.wait_ge(modb_out, 4)
            for tt in range(T):
                do(dve.tensor_tensor(H[:, tt, :], X[:, tt, :], A[:, :], ALU.mult))
                dve.tensor_tensor(H[:, tt, :], H[:, tt, :], B[:, :], ALU.add).then_inc(h_ready, 1)
            dve.wait_ge(h_ready, 2)
            dve.memset(spare, 0.0).then_inc(glue_done, 1)
            dve.wait_ge(glue_done, 1)

            following = {"ffn10": "lru", "lru": "ffn20", "ffn20": "kv", "ffn11": "att", "att": "ffn21", "ffn21": None}
            run = {"mla": mla, "s5": s5, "lru": lru, "kv": kv, "att": att}
            for name in phases:
                if name in run:
                    run[name]()
                else:
                    (mlp if name in MLPS else ffn)(name)
                if name in ("mla", "mlp0", "s5", "mlp1"):
                    ln_glue(name)
                if name == "mla":
                    softplus()
                if name in following:
                    rms_glue(name, following[name])
                if name in FFNS:
                    lo(FIRST[name] + 35)
            if until in ("mla", "mlp0", "s5"):
                dve.wait_ge(res_ok, {"mla": 2, "mlp0": 4, "s5": 6}[until])
            dve.memset(spare, 0.0).then_inc(final_ok, 1)

        @block.gpsimd
        def _(pool):
            steps = Steps(pool, pool_step)
            TT, TS = pool.tensor_tensor, pool.tensor_scalar

            def do(ins):
                steps.did(ins)
                steps.settle()

            def axpy(x, a, y, tmp, op=ALU.add):
                do(TS(tmp, x, a, None, ALU.mult))
                return lambda dst: TT(dst, tmp, y, op)

            steps.did(pool.memset(ones[:, :], 1.0))
            steps.did(pool.memset(ident[:, :], 0.0))
            steps.did(pool.memset(mask[:, :], 0.0))
            steps.did(pool.memset(mod[:, 1024:5120], 0.0))
            steps.settle()
            steps.did(pool.affine_select(out=ident[:, :], in_=ident[:, :], compare_op=ALU.not_equal, fill=1.0, base=0,
                                         pattern=[[-1, P]], channel_multiplier=1))
            pool.affine_select(out=mask[:, P:], in_=mask[:, P:], compare_op=ALU.is_ge, fill=NEG, base=0,
                               pattern=[[-1, P]], channel_multiplier=1).then_inc(const_ok, 1)

            v = lambda k: g0v[:, k, :]
            pool.wait_ge(s5_in, 16 * 21)
            pool.tensor_copy(a_rows[:, 2, :].rearrange("q (g p) -> q g p", g=2),
                             ldt_rows.rearrange("q (g o) -> q g o", o=1).to_broadcast([PAIRS, 2, 64])).then_inc(s5p_pool, 1)
            pool.wait_ge(s5p_act, 2)
            steps.did(TT(v(3), v(0), v(2), ALU.mult))
            steps.did(TT(v(4), v(1), v(2), ALU.mult))
            steps.did(TT(v(8), v(0), v(0), ALU.mult))
            do(TT(v(9), v(1), v(1), ALU.mult))
            steps.did(TT(v(8), v(8), v(9), ALU.add))
            do(TS(v(10), v(4), 1 / TWO_PI, MAGIC, ALU.mult, ALU.add))
            do(TS(v(10), v(10), -MAGIC, None, ALU.add))
            do(axpy(v(10), -PI_A, v(4), v(11))(v(5)))
            do(axpy(v(10), -PI_B, v(5), v(11))(v(5)))
            do(axpy(v(10), -PI_C, v(5), v(11))(v(5)))
            TS(v(5), v(5), 3.1415925, -3.1415925, ALU.min, ALU.max).then_inc(s5p_pool, 1)
            pool.wait_ge(s5p_pool, S5P_ANGLE)
            do(TS(th, v(5), 1 / TWO_PI, None, ALU.mult))
            do(TS(th_hi, th, 192.0, None, ALU.add))
            do(TS(th_hi, th_hi, -192.0, None, ALU.add))
            do(axpy(th_hi, -PI_A, v(5), v(11))(th_lo))
            do(axpy(th_hi, -(PI_B + PI_C), th_lo, v(11))(th_lo))
            do(TS(th_lo, th_lo, 1 / TWO_PI, None, ALU.mult))
            pool.wait_ge(s5p_act, 6)
            pool.wait_ge(s5p_dve, 1)
            steps.did(TT(v(9), rho, v(7), ALU.mult))
            do(TT(v(10), rho, v(6), ALU.mult))
            do(TS(v(9), v(9), -1.0, None, ALU.add))
            steps.did(TT(v(11), v(9), v(0), ALU.mult))
            steps.did(TT(v(12), v(10), v(1), ALU.mult))
            steps.did(TT(v(13), v(10), v(0), ALU.mult))
            do(TT(v(14), v(9), v(1), ALU.mult))
            steps.did(TT(v(11), v(11), v(12), ALU.add))
            do(TT(v(13), v(13), v(14), ALU.subtract))
            steps.did(TT(v(11), v(11), v(8), ALU.mult))
            do(TT(v(13), v(13), v(8), ALU.mult))
            wide = lambda k: v(k).rearrange("p (q o) -> p q o", o=1).to_broadcast([P, PAIRS, 16])
            for r, (c0, c1, op) in enumerate(((11, 13, ALU.subtract), (13, 11, ALU.add))):
                steps.did(TT(bu1, b_in[:, 0], wide(c0), ALU.mult))
                do(TT(bu2, b_in[:, 1], wide(c1), ALU.mult))
                for g in range(2):
                    q = slice(64 * g, 64 * g + 64)
                    last = TT(b_dg[q, :, r, :, 16 * g:16 * g + 16], bu1[q].rearrange("p (m i) c -> p m i c", i=4),
                              bu2[q].rearrange("p (m i) c -> p m i c", i=4), op)
                    if r and g:
                        last.then_inc(s5p_pool, 1)
                    else:
                        do(last)

            pieces = [(0, 2, kk) for kk in range(4)]
            for m in range(1, 4):
                pieces += [(m, q, kk) for q in range(3) for kk in range(4)]
            index = {p: n for n, p in enumerate(pieces)}

            def fetch(n):
                m, q, kk = pieces[n]
                pool.dma_start(modw[:, n % 2, :].rearrange("p (k n) -> p k n", k=2),
                               mod_w[m].rearrange("(k p) n -> p k n", p=P)[:, 2 * kk:2 * kk + 2, D * q:D * (q + 1)]).then_inc(modw_in[n % 2], 16)

            def third(m, q, ahead):
                acc = G[:, 0, :] if m == 0 else modacc[:, D * q:D * (q + 1)]
                do(pool.memset(acc, 0.0))
                pool.dma_start(acc[0:1, :], mod_b[m][D * q:D * (q + 1)].rearrange("(o n) -> o n", o=1)).then_inc(modb_in, 16)
                thirds[0] += 1
                pool.wait_ge(modb_in, 16 * thirds[0])
                for kk in range(4):
                    n = index[(m, q, kk)]
                    if n + 1 < len(pieces) and (kk < 3 or ahead):
                        fetch(n + 1)
                    pool.wait_ge(modw_in[n % 2], 16 * (n // 2 + 1))
                    for k in range(2):
                        w = modw[:, n % 2, D * k:D * (k + 1)]
                        last = axpy(w, csil[:, 2 * kk + k:2 * kk + k + 1], acc, w)(acc)
                        if kk == 3 and k == 1:
                            last.then_inc(mod_sum, 1)
                            pool.wait_ge(mod_sum, thirds[0])
                        else:
                            do(last)

            thirds = [0]

            def vectors(k):
                pool.wait_ge(modb_out, (10, 18, 24)[k - 1])
                row_wait(pool, f"lg{k}")
                row_wait(pool, f"lb{k}")
                if k == 3:
                    pool.wait_ge(x_rot, PAIRS)
                tmp = modacc[:, 0:D]
                steps.did(TT(tmp, BA[:, :], A[:, :], ALU.mult))
                steps.settle()
                steps.did(TT(B[:, :], B[:, :], tmp, ALU.add))
                steps.did(TT(A[:, :], A[:, :], GA[:, :], ALU.mult))
                steps.settle()
                steps.did(TS(GA[:, :], GA[:, :], ALPHA, None, ALU.mult))
                steps.settle()
                TS(BA[:, :], BA[:, :], ALPHA, None, ALU.mult).then_inc(vec_done, 1)
                pool.wait_ge(vec_done, k)

            def residual(k):
                for tt in range(T):
                    pool.wait_ge(ln_stats, 2 * (k - 1) + tt + 1)
                    do(TS(X[:, tt, :], Y[:, tt, :], rsq[:, tt:tt + 1], nmr[:, tt:tt + 1], ALU.mult, ALU.add))
                    do(TT(X[:, tt, :], X[:, tt, :], GA[:, :], ALU.mult))
                    TT(X[:, tt, :], X[:, tt, :], BA[:, :], ALU.add).then_inc(res_ok, 1)

            def s5_phases():
                pool.wait_ge(modb_out, 24)
                count = ph[:, 0, 0, :].bitcast(I32)
                do(pool.iota(count, pattern=[[1, L]], base=0, channel_multiplier=0))
                do(pool.tensor_copy(iotaf, count))
                for i in range(PAIRS):
                    s = i % 2
                    if i >= 2:
                        pool.wait_ge(table_ok, i - 1)
                    r, k = ph[:, s, 0, :], ph[:, s, 1, :]
                    do(TS(k, iotaf, th[:, i:i + 1], MAGIC, ALU.mult, ALU.add))
                    do(TS(k, k, -MAGIC, None, ALU.add))
                    do(axpy(iotaf, th_hi[:, i:i + 1], k, r, ALU.subtract)(r))
                    do(axpy(iotaf, th_lo[:, i:i + 1], r, k)(r))
                    TS(r, r, 0.5, -0.5, ALU.min, ALU.max).then_inc(phase_r, 1)

            def relative_bias():
                pool.wait_ge(x_rot, PAIRS)
                pool.dma_start(rel, t["rel_bias_2"]).then_inc(rel_in, 16)
                pool.wait_ge(rel_in, 16)
                b = buckets()[::-1]
                cuts = [0] + [m for m in range(1, L) if b[m] != b[m - 1]] + [L]
                for m0, m1 in zip(cuts, cuts[1:]):
                    steps.did(pool.tensor_copy(vrev[:, m0:m1], rel[:, int(b[m0]):int(b[m0]) + 1].to_broadcast([HEADS, m1 - m0])))
                steps.settle()
                pool.memset(vrev[:, L:], NEG).then_inc(vrev_ok, 1)
                pool.wait_ge(vrev_ok, 1)
                pool.dma_start(bias_store[:, 0:P * 385].rearrange("h (q m) -> h q m", m=385)[:, :, 0:384],
                               vrev.rearrange("h (o m) -> h o m", o=1).to_broadcast([HEADS, P, 384])).then_inc(bias_stored, 16)
                pool.wait_ge(bias_stored, 16)

            def load_bias():
                pool.wait_ge(hg_lo, 2)
                src = bias_store[:, P - 1:P - 1 + P * 384].rearrange("h (q m) -> q h m", m=384)[:, :, 0:L]
                pool.dma_start(relb, src).then_inc(bias_in, 16)

            pool.wait_ge(s5t_ok, 8)
            pool.wait_ge(s5_stored, 32)
            pool.wait_ge(csil_ok, 1)
            fetch(0)
            third(0, 2, True)
            for q in range(3):
                third(1, q, True)
            pool.wait_ge(glue_done, 1)
            TS(X[:, :, :].rearrange("p t d -> p (t d)"), X[:, :, :].rearrange("p t d -> p (t d)"), ALPHA, None, ALU.mult).then_inc(x_scaled, 1)
            vectors(1)
            if "mlp0" in phases:
                pool.wait_ge(modb_out, 12)
                third(2, 0, True)
            residual(1)
            if "mlp0" in phases:
                third(2, 1, True)
                third(2, 2, True)
                vectors(2)
            if "s5" in phases:
                for q in range(3):
                    third(3, q, q < 2)
            if "mlp0" in phases:
                residual(2)
            if "s5" in phases:
                s5_phases()
                vectors(3)
                residual(3)
            if "lru" in phases:
                relative_bias()
            if "att" in phases:
                load_bias()


def kernel(**inputs):
    import concourse.bacc as bacc
    from concourse.bass_utils import run_bass_kernel_spmd

    nc = bacc.Bacc("TRN2", target_bir_lowering=False, num_devices=1)
    arrays = {name: np.ascontiguousarray(a) for name, a in inputs.items()}
    arrays["inv_freq"] = (10000.0 ** (-np.arange(0, ROPE, 2, dtype=np.float32) / ROPE)).astype(np.float32)
    arrays = {f"in_{name}": a for name, a in arrays.items()}
    t = {name[3:]: nc.dram_tensor(name, a.shape, mybir.dt.from_np(a.dtype), kind="ExternalInput").ap() for name, a in arrays.items()}
    out = nc.dram_tensor("out", (1, L, D), F32, kind="ExternalOutput").ap()
    build_program(nc, t, out)
    return run_bass_kernel_spmd(nc, [arrays], core_ids=[0]).results[0]["out"]
```

```python
from contextlib import ExitStack
import math

import numpy as np
import concourse.bass as bass
from concourse import mybir

F32 = mybir.dt.float32
F32R = mybir.dt.float32r
I32 = mybir.dt.int32
ALU = mybir.AluOpType
ACT = mybir.ActivationFunctionType

P = 128
L = 256
T = L // P
D = 1024
KT = D // P
CH = 2048
RAW, SPL = 3, 3
HEADS = 8
F1, F2 = 4096, 2816
ALPHA = 4 ** 0.25
QL, KVL, ROPE, NOPE = 256, 128, 64, 128
ZW = QL + KVL + ROPE
NEG = -1e30
TWO_PI = 2 * math.pi
MAGIC = 1.5 * 2 ** 23
PAIRS = 32
CONV = 4


def bits12(x):
    m, e = math.frexp(x)
    return math.ldexp(math.floor(m * 4096) / 4096, e)


PI_A = 6.28125
PI_B = bits12(TWO_PI - PI_A)
PI_C = TWO_PI - PI_A - PI_B


class Steps:

    def __init__(self, eng, sem):
        self.eng, self.sem, self.n, self.base = eng, sem, 0, None

    def did(self, ins):
        self.n += 1
        return ins.then_inc(self.sem, 1)

    def settle(self):
        self.eng.wait_ge(self.sem, self.n if self.base is None else self.base + self.n)

    def loop(self, i, start, per):
        self.before, self.per = self.n, per
        self.base = i * per - start * per

    def end(self, trips):
        assert self.n - self.before == self.per, (self.n - self.before, self.per)
        self.n = self.before + self.per * trips
        self.base = None


PHASES = [("mla", 9), ("mlp0", 32), ("s5", 12), ("mlp1", 32), ("ffn10", 33), ("lru", 14), ("ffn20", 33),
          ("kv", 8), ("ffn11", 33), ("att", 8), ("ffn21", 33)]
FIRST = {}
_n = 0
for _name, _k in PHASES:
    FIRST[_name] = _n
    _n += _k
TOTAL = _n
MLPS, FFNS = ["mlp0", "mlp1"], ["ffn10", "ffn20", "ffn11", "ffn21"]
ITERS = {"mlp0": F1 // 256, "mlp1": F1 // 256, "ffn10": 11, "ffn20": 11, "ffn11": 11, "ffn21": 11}
HID0 = {}
_n = 0
for _name in ["mlp0", "mlp1", "ffn10", "ffn20", "ffn11", "ffn21"]:
    HID0[_name] = _n
    _n += ITERS[_name]
ACC = {n: i for i, n in enumerate(["mla", "mlp0", "s5", "mlp1", "ffn10", "lru", "ffn20", "kv", "ffn11", "att", "ffn21"])}
XTS = {n: i for i, n in enumerate(["mla", "mlp0", "s5", "mlp1", "ffn10", "lru", "ffn20", "kv", "ffn11", "att", "ffn21"])}


def buckets():
    d = np.arange(L)
    nf = np.maximum(d, 1).astype(np.float32)
    large = 16 + (np.log(nf / np.float32(16)) / np.float32(math.log(8)) * np.float32(16)).astype(np.int32)
    return np.where(d < 16, d, np.minimum(large, 31))



ROWS = [("lg1", 0), ("lb1", 1), ("lg2", 0), ("lb2", 1), ("lg3", 0), ("lb3", 1), ("lg4", 3), ("lb4", 4),
        ("pre_ffn10", 0), ("post_ffn10", 1), ("pre_lru", 2), ("post_lru", 3), ("pre_ffn20", 4), ("post_ffn20", 5),
        ("pre_kv", 0), ("pre_ffn11", 1), ("post_ffn11", 2), ("pre_att", 3), ("post_att", 4), ("pre_ffn21", 5),
        ("post_ffn21", 0)]
ROW_FIRST = 8
ROW_SLOT = dict(ROWS)
ROW_COUNT = {n: sum(1 for m, s in ROWS[:i + 1] if s == ROWS[i][1]) for i, (n, _) in enumerate(ROWS)}
ROW_INDEX = {n: i for i, (n, _) in enumerate(ROWS)}
BIASED = ["mlp0", "mlp1", "lru"]


S5P_ANGLE = 2


def build_program(nc, t, out):
    phases = [n for n, _ in PHASES]
    ctx = ExitStack()
    with ctx:
        def sb(name, shape, dt=F32):
            return ctx.enter_context(nc.sbuf_tensor(name, shape, dt))

        def sem(name):
            return ctx.enter_context(nc.semaphore(name))

        raw = sb("raw", [P, RAW, CH])
        whi = sb("whi", [P, SPL, CH], F32R)
        wlo = sb("wlo", [P, SPL, CH], F32R)
        xhi = sb("xhi", [P, KT, L], F32R)
        xlo = sb("xlo", [P, KT, L], F32R)
        hhi = sb("hhi", [P, KT, L], F32R)
        hlo = sb("hlo", [P, KT, L], F32R)
        X = sb("X", [P, T, D])
        work = sb("work", [P, 8960])
        Y = work[:, 0:2048].rearrange("p (t d) -> p t d", t=T)
        H = work[:, 2048:4096].rearrange("p (t d) -> p t d", t=T)
        TMP = work[:, 4096:6144]
        AR = work[:, 6144:8960]
        mod = sb("mod", [P, 7168])
        modw = mod[:, 0:4096].rearrange("p (s n) -> p s n", s=2)
        modacc = mod[:, 4096:7168]
        G = sb("G", [P, 2, D])
        A = sb("A", [P, D])
        B = sb("B", [P, D])
        GA = sb("GA", [P, D])
        BA = sb("BA", [P, D])
        row_slots = [GA[:, :], BA[:, :], G[:, 0, :], A[:, :], B[:, :], G[:, 1, :]]
        brow = sb("brow", [1, D])
        ident = sb("ident", [P, P])
        ones = sb("ones", [P, P])
        mask = sb("mask", [P, L])
        zeros = mask[0:1, 0:P].bitcast(mybir.dt.bfloat16)
        small = sb("small", [P, 512])
        rope = sb("rope", [P, 2, T, 32])
        ps = ctx.enter_context(nc.psum_tensor("ps", [P, 8, 512], F32))
        s5_store = nc.dram_tensor("s5_store", (2, P, 2048), F32, kind="Internal").ap()
        bias_store = nc.dram_tensor("bias_store", (HEADS, P * 386), F32, kind="Internal").ap()

        used = [0]

        def col(n):
            used[0] += n
            assert used[0] < 512
            return small[:, used[0] - n:used[0]]

        craw, csil = col(8), col(8)
        stats, mv, nmr = col(24), col(4), col(2)
        ssq, rsq, root, val = col(8), col(8), col(8), col(8)
        eps_ln, eps_rms, eps_rms4 = col(1), col(1), col(1)
        newton, recip = col(2), col(2)
        posi, posf = col(2), col(2)
        invf = col(32)
        rho, th, th_hi, th_lo = col(PAIRS), col(PAIRS), col(PAIRS), col(PAIRS)
        dskip, bglu, b1c = col(8), col(8), col(64)
        lru_bin, lru_conv, lru_cb = col(16), col(32), col(8)
        lru_br, lru_bi, lru_lam, lam_n, lam_p = col(8), col(8), col(8), col(8), col(8)
        attm, atts = col(8), col(8)

        raw_in = [sem(f"raw_in{i}") for i in range(RAW)]
        hi_done = sem("hi_done")
        lo_done = sem("lo_done")
        w_used = sem("w_used")
        x_in, c_in, small_in, small2_in, s5_in = sem("x_in"), sem("c_in"), sem("small_in"), sem("small2_in"), sem("s5_in")
        m0_in = [sem(f"m0_in{i}") for i in range(4)]
        m0_gate = sem("m0_gate")
        m0_used = sem("m0_used")
        modw_in = [sem(f"modw_in{i}") for i in range(2)]
        modb_in, modb0_in = sem("modb_in"), sem("modb0_in")
        m1_used, m1_clear, m1_bias, m1_sum = sem("m1_used"), sem("m1_clear"), sem("m1_bias"), sem("m1_sum")
        acc0_clear = sem("acc0_clear")
        mod_sum, mod0_sum = sem("mod_sum"), sem("mod0_sum")
        modb_ps, modb_out = sem("modb_ps"), sem("modb_out")
        row_in = [sem(f"row_in{i}") for i in range(6)]
        row_used = sem("row_used")
        vec_done = sem("vec_done")
        glue_done = sem("glue_done")
        x_scaled = sem("x_scaled")
        const_ok, csil_ok = sem("const_ok"), sem("csil_ok")
        dve_step, act_step, pool_step = sem("dve_step"), sem("act_step"), sem("pool_step")
        acc_half, acc_free = sem("acc_half"), sem("acc_free")
        var_ok, root_ok = sem("var_ok"), sem("root_ok")
        ln_stats, res_ok, sq_done, x_new, h_ready = sem("ln_stats"), sem("res_ok"), sem("sq_done"), sem("x_new"), sem("h_ready")
        xt_ps, xhi_ok, xt_ok = sem("xt_ps"), sem("xhi_ok"), sem("xt_ok")
        act1, prod, hid_hi, hid_ok = sem("act1"), sem("prod"), sem("hid_hi"), sem("hid_ok")
        brow_in, acc_open = sem("brow_in"), sem("acc_open")
        rope_r, rope_tab = sem("rope_r"), sem("rope_tab")
        z_sq, zn_ok, zt_ps, zhi_ok, zx_ok = sem("z_sq"), sem("zn_ok"), sem("zt_ps"), sem("zhi_ok"), sem("zx_ok")
        k_ps, k_ok, v_ps, v_ok = sem("k_ps"), sem("k_ok"), sem("v_ps"), sem("v_ok")
        q_ps, q_ok, qp_ok, qt_ps, qt_ok = sem("q_ps"), sem("q_ok"), sem("qp_ok"), sem("qt_ps"), sem("qt_ok")
        s_ps, sm_ok, mx_ok, exp_ok, p_ok = sem("s_ps"), sem("sm_ok"), sem("mx_ok"), sem("exp_ok"), sem("p_ok")
        pt_ps, pt_ok, o_ps, o_hi, o_ok = sem("pt_ps"), sem("pt_ok"), sem("o_ps"), sem("o_hi"), sem("o_ok")
        s5t_ok, s5p_ps, s5p_act, s5p_pool, s5p_dve = sem("s5t_ok"), sem("s5p_ps"), sem("s5p_act"), sem("s5p_pool"), sem("s5p_dve")
        s5_stored, s5_loaded = sem("s5_stored"), sem("s5_loaded")
        u_ok, bu_ps, bu_rot, w_ps = sem("u_ok"), sem("bu_ps"), sem("bu_rot"), sem("w_ps")
        turn_r = sem("turn_r")
        phase_r, table_ok, x_rot, x_used, y_ok = sem("phase_r"), sem("table_ok"), sem("x_rot"), sem("x_used"), sem("y_ok")
        g_act, g_hi, g_ok, sig_ok, zz_ok, zz_hi, zz_lo = (sem(n) for n in ("g_act", "g_hi", "g_ok", "sig_ok", "zz_ok", "zz_hi", "zz_lo"))
        lp_ok, conv_ok, xc_hi, xc_ok = sem("lp_ok"), sem("conv_ok"), sem("xc_hi"), sem("xc_ok")
        lg_ps, lg_ok, la_ok, m2_ok, mult_ok, hg_ok, hg_hi, hg_lo = (
            sem(n) for n in ("lg_ps", "lg_ok", "la_ok", "m2_ok", "mult_ok", "hg_ok", "hg_hi", "hg_lo"))
        lam_exp, lam_ok = sem("lam_exp"), sem("lam_ok")
        vrev_ok, bias_stored, bias_in, rel_in = sem("vrev_ok"), sem("bias_stored"), sem("bias_in"), sem("rel_in")
        final_ok, out_done = sem("final_ok"), sem("out_done")

        block = ctx.enter_context(nc.Block())

        kT = Y.rearrange("p t d -> p (t d)").rearrange("p (h l) -> p h l", h=HEADS)
        V = H
        qT = TMP.rearrange("p (h l) -> p h l", h=HEADS)
        qpT = AR[:, 0:1024].rearrange("p (r l) -> p r l", r=4)
        kpT = AR[:, 1024:1280]
        sm = AR[:, 1280:2048].rearrange("p (s n) -> p s n", s=2)
        pt = AR[:, 2048:2816].rearrange("p (s n) -> p s n", s=2)
        zn = Y
        qp_tok = AR[:, 1280:1792].rearrange("p (t n) -> p t n", t=T)
        rt = AR[:, 1792:2304].rearrange("p (s n) -> p s n", s=4)
        kT2 = mod[:, 0:2048].rearrange("p (h l) -> p h l", h=HEADS)
        V2 = mod[:, 2048:4096].rearrange("p (t d) -> p t d", t=T)
        relb = mod[:, 4096:6144].rearrange("p (h l) -> p h l", h=HEADS)
        qT2 = kT
        sm2 = TMP[:, 0:768].rearrange("p (s n) -> p s n", s=2)
        pt2 = TMP[:, 768:1536].rearrange("p (s n) -> p s n", s=2)
        b_in = mod[:, 0:1024].rearrange("p (r q c) -> p r q c", r=2, q=PAIRS)
        b_dg = mod[:, 1024:3072].rearrange("p (m r i c) -> p m r i c", m=KT, r=2, i=4)
        c_pad = mod[:, 3072:5120].rearrange("p (m r n) -> p m r n", m=KT, r=2)
        s5_stage = mod[:, 5120:7168].rearrange("p (m r n) -> p m r n", m=KT, r=2)
        a_rows = work[0:PAIRS, 8192:8576].rearrange("p (k n) -> p k n", k=3)
        g0v = G[:, 1, 384:864].rearrange("p (k n) -> p k n", n=PAIRS)
        m0 = [work[:, 2048 * s:2048 * (s + 1)].rearrange("p (k n) -> p k n", k=2) for s in range(4)]
        late = [(1, 2), (2, 0)]
        straight_phases = ("s5", "lru", "kv", "att")
        bu1 = mod[:, 5120:5632].rearrange("p (q c) -> p q c", q=PAIRS)
        bu2 = mod[:, 5632:6144].rearrange("p (q c) -> p q c", q=PAIRS)
        ldt_rows = work[0:PAIRS, 8576:8578]
        s5B = mod[:, 0:2048].rearrange("p (m r n) -> p m r n", m=KT, r=2)
        s5C = mod[:, 2048:4096].rearrange("p (m r n) -> p m r n", m=KT, r=2)
        uT = H.rearrange("p t d -> p (t d)").rearrange("p (m l) -> p m l", m=KT)
        yT = Y.rearrange("p t d -> p (t d)").rearrange("p (m l) -> p m l", m=KT)
        tabs = mod[:, 4096:5632].rearrange("p (s k l) -> p s k l", s=3, k=2)
        ph = mod[:, 5632:6656].rearrange("p (s k l) -> p s k l", s=2, k=2)
        half = mod[:, 6656:6912]
        iotaf = mod[:, 6912:7168]
        rot_a = TMP[:, 0:1024].rearrange("p (s n) -> p s n", s=2)
        rot_b = TMP[:, 1024:2048].rearrange("p (s n) -> p s n", s=2)
        zst = AR[:, 0:512]
        xa = AR[:, 512:1536].rearrange("p (s n) -> p s n", s=2)
        xb = AR[:, 1536:2560].rearrange("p (s n) -> p s n", s=2)
        sig = TMP[:, 0:1024].rearrange("p (s n) -> p s n", s=2)
        zz = TMP[:, 1024:2048].rearrange("p (s n) -> p s n", s=2)
        rel = mod[0:HEADS, 6144:6144 + 32]
        vrev = mod[0:HEADS, 6656:6656 + 384]
        xbp = work[:, 4096:6168].rearrange("p (m l) -> p m l", m=KT)
        xcT = Y.rearrange("p t d -> p (t d)").rearrange("p (m l) -> p m l", m=KT)
        gyT = H.rearrange("p t d -> p (t d)").rearrange("p (m l) -> p m l", m=KT)
        rT = mod[:, 0:2048].rearrange("p (m l) -> p m l", m=KT)
        iT = mod[:, 2048:4096].rearrange("p (m l) -> p m l", m=KT)
        aT = mod[:, 4096:6144].rearrange("p (m l) -> p m l", m=KT)
        tT = work[:, 6400:8448].rearrange("p (m l) -> p m l", m=KT)

        def ws_src(w, j):
            return w.rearrange("(k p) f -> p k f", p=P)[:, :, j * 256:(j + 1) * 256]

        def xs_src(w, j):
            return w[2 * j * P:(2 * j + 2) * P, :].rearrange("(k p) n -> p k n", p=P)

        straight = {}
        w_in = t["mla_w_in"][0].rearrange("(k p) f -> p k f", p=P)
        w_qb = t["mla_w_qb"][0].rearrange("(k p) f -> p k f", p=P)
        for i in range(2):
            straight[i] = (w_in[:, 4 * i:4 * i + 4, :], (4, ZW))
            straight[3 + i] = (w_qb[:, :, 768 * i:768 * i + 768], (2, 768))
        straight[2] = (t["mla_w_kvb"][0].rearrange("p (a n) -> p a n", a=2), (2, 1024))
        c0 = FIRST["s5"]
        for i in range(4):
            straight[5 + i] = (xs_src(t["mla_w_o"][0], i), (2, D))
            straight[c0 + i] = (ws_src(t["ssm_w_in"][0], i), (8, 256))
            straight[c0 + 4 + i] = (ws_src(t["ssm_w_glu"][0], i), (8, 256))
            straight[c0 + 8 + i] = (xs_src(t["ssm_w_out"][0], i), (2, D))
        c0 = FIRST["lru"]
        for i in range(8):
            straight[c0 + i] = (ws_src(t["lru_w_in_2"][0], i), (8, 256))
        straight[c0 + 8] = (t["lru_w_r_2"][0].rearrange("h (k p) j -> p (h k) j", p=P), (8, 256))
        straight[c0 + 9] = (t["lru_w_i_2"][0].rearrange("h (k p) j -> p (h k) j", p=P), (8, 256))
        for i in range(4):
            straight[c0 + 10 + i] = (xs_src(t["lru_w_out_2"][0], i), (2, D))
            straight[FIRST["kv"] + i] = (ws_src(t["w_kv_2"], i), (8, 256))
            straight[FIRST["kv"] + 4 + i] = (xs_src(t["w_kv_2"][:, D:2 * D], i), (2, D))
            straight[FIRST["att"] + i] = (ws_src(t["attn_w_q_2"][0], i), (8, 256))
            straight[FIRST["att"] + 4 + i] = (xs_src(t["attn_w_o_2"][0], i), (2, D))
        width = {c: int(np.prod(s)) for c, (_, s) in straight.items()}
        ffn_w = {"mlp0": (t["mlp_w1"][0], None, t["mlp_w2"][0]), "mlp1": (t["mlp_w1"][1], None, t["mlp_w2"][1])}
        for name, k, l in (("ffn10", 1, 0), ("ffn20", 2, 0), ("ffn11", 1, 1), ("ffn21", 2, 1)):
            ffn_w[name] = tuple(t[f"ffn{k}_w_{x}_2"][l] for x in ("gate", "up", "down"))
        row_src = {"lg1": t["ln_mix_g"][0], "lb1": t["ln_mix_b"][0], "lg2": t["ln_ffn_g"][0], "lb2": t["ln_ffn_b"][0],
                   "lg3": t["ln_mix_g"][1], "lb3": t["ln_mix_b"][1], "lg4": t["ln_ffn_g"][1], "lb4": t["ln_ffn_b"][1],
                   "pre_ffn10": t["ffn1_pre_g_2"][0], "post_ffn10": t["ffn1_post_g_2"][0],
                   "pre_lru": t["mix_pre_g_2"][0], "post_lru": t["mix_post_g_2"][0],
                   "pre_ffn20": t["ffn2_pre_g_2"][0], "post_ffn20": t["ffn2_post_g_2"][0],
                   "pre_kv": t["kv_norm_g_2"], "pre_ffn11": t["ffn1_pre_g_2"][1], "post_ffn11": t["ffn1_post_g_2"][1],
                   "pre_att": t["mix_pre_g_2"][1], "post_att": t["mix_post_g_2"][1],
                   "pre_ffn21": t["ffn2_pre_g_2"][1], "post_ffn21": t["ffn2_post_g_2"][1]}
        bias_src = {"mlp0": t["mlp_b2"][0], "mlp1": t["mlp_b2"][1], "lru": t["lru_b_out_2"][0]}
        mod_w = [t["mod_mix_w"][0], t["mod_ffn_w"][0], t["mod_mix_w"][1], t["mod_ffn_w"][1]]
        mod_b = [t["mod_mix_b"][0], t["mod_ffn_b"][0], t["mod_mix_b"][1], t["mod_ffn_b"][1]]

        def shaped(ap, shape):
            return ap[:, 0:shape[0] * shape[1]].rearrange("p (a b) -> p a b", a=shape[0])

        def row(name):
            return row_slots[ROW_SLOT[name]]

        def row_wait(eng, name):
            eng.wait_ge(row_in[ROW_SLOT[name]], 16 * ROW_COUNT[name])

        def mlp_runs(name):
            return [(0, 2), (2, 5)]

        @block.sync
        def _(sp):
            def chunk(c, src, shape, i=None):
                if c >= RAW:
                    need = c - RAW + 1
                    sp.wait_ge(lo_done, need if i is None else i * 6 + need)
                sp.dma_start(shaped(raw[:, c % RAW, :], shape), src).then_inc(raw_in[c % RAW], 16)

            def line(c):
                chunk(c, *straight[c])

            def up_src(w, j):
                return w.rearrange("(k p) f -> p k f", p=P)[:, :, bass.ds(j * 256, 256)]

            def down_src(w, j):
                return w[bass.ds(j * 256, 256), :].rearrange("(k p) n -> p k n", p=P)

            def load_row(name):
                sp.dma_start(row(name), row_src[name].rearrange("(o n) -> o n", o=1).to_broadcast([P, D])).then_inc(
                    row_in[ROW_SLOT[name]], 16)

            def reload_row(name):
                if ROW_INDEX[name] - ROW_FIRST >= 6:
                    sp.wait_ge(row_used, ROW_INDEX[name] - ROW_FIRST - 5)
                load_row(name)

            def cols(dst, src, s):
                with nc.allow_non_contiguous_dma(reason="short vectors"):
                    sp.dma_start(dst, src.rearrange("(k p) -> p k", p=P)).then_inc(s, 16)

            def bias_row(name):
                if BIASED.index(name):
                    sp.wait_ge(acc_open, BIASED.index(name))
                sp.dma_start(brow[0:1, :], bias_src[name].rearrange("(o n) -> o n", o=1)).then_inc(brow_in, 16)

            def mlp(name):
                up, _, down = ffn_w[name]
                c = FIRST[name]
                chunk(c, ws_src(up, 0), (8, 256))
                for a, b in mlp_runs(name):
                    with sp.Fori(a, b) as i:
                        for k in range(3):
                            chunk(c + 1 + 2 * k, up_src(up, i * 3 + (k + 1)), (8, 256), i)
                            chunk(c + 2 + 2 * k, down_src(down, i * 3 + k), (2, D), i)
                    if a == 0 and name == "mlp0":
                        sp.wait_ge(res_ok, 2)
                        load_row("lg2")
                        load_row("lb2")
                    if a == 0 and name == "mlp1":
                        sp.wait_ge(res_ok, 6)
                        load_row("pre_ffn10")
                        load_row("post_ffn10")
                        sp.wait_ge(glue_done, 4)
                        load_row("lg4")
                        load_row("lb4")
                        load_row("pre_lru")
                chunk(c + 31, xs_src(down, 15), (2, D))

            def ffn(name):
                gate, up, down = ffn_w[name]
                c = FIRST[name]
                chunk(c, ws_src(gate, 0), (8, 256))
                chunk(c + 1, ws_src(up, 0), (8, 256))
                with sp.Fori(0, 5) as i:
                    for k in range(2):
                        chunk(c + 2 + 3 * k, up_src(gate, i * 2 + (k + 1)), (8, 256), i)
                        chunk(c + 3 + 3 * k, up_src(up, i * 2 + (k + 1)), (8, 256), i)
                        chunk(c + 4 + 3 * k, down_src(down, i * 2 + k), (2, D), i)
                chunk(c + 32, xs_src(down, 10), (2, D))

            cols(craw, t["c"][0], c_in)
            w0 = mod_w[0].rearrange("(k p) n -> p k n", p=P)
            for n in range(8):
                third, kk = n // 4, n % 4
                if n >= 4:
                    sp.wait_ge(m0_used, n - 3)
                sp.dma_start(m0[n % 4], w0[:, 2 * kk:2 * kk + 2, D * third:D * (third + 1)]).then_inc(m0_in[n % 4], 16)
                if n < 3:
                    if n == 0:
                        sp.wait_ge(acc0_clear, 1)
                    sp.dma_start([GA[0:1, :], BA[0:1, :], G[0:1, 0, :]][n], mod_b[0][D * n:D * (n + 1)].rearrange("(o n) -> o n", o=1)).then_inc(modb0_in, 16)
            sp.dma_start(X[:, :, :], t["x"][0].rearrange("(t p) d -> p t d", p=P)).then_inc(x_in, 16)
            with nc.allow_non_contiguous_dma(reason="short vectors"):
                sp.dma_start(posi.bitcast(I32), t["positions"][0].rearrange("(t p) -> p t", p=P)).then_inc(small_in, 16)
            sp.dma_start(invf, t["inv_freq"].rearrange("(o n) -> o n", o=1).to_broadcast([P, 32])).then_inc(small_in, 16)
            sp.dma_start(G[:, 1, 0:QL], t["mla_q_norm"].to_broadcast([P, QL])).then_inc(small_in, 16)
            sp.dma_start(G[:, 1, QL:QL + KVL], t["mla_kv_norm"].to_broadcast([P, KVL])).then_inc(small_in, 16)
            for c in range(3):
                line(c)
            def gate_piece(n):
                sp.wait_ge(m0_used, (7, 7, 8, 10)[n])
                sp.dma_start(m0[0 if n == 1 else 2], w0[:, 2 * n:2 * n + 2, 2 * D:3 * D]).then_inc(m0_gate, 16)

            gate_piece(0)
            gate_piece(1)
            for dst, src in ((dskip, t["ssm_d"][0]), (bglu, t["ssm_b_glu"][0]), (b1c[:, 0:32], t["mlp_b1"][0]),
                             (b1c[:, 32:64], t["mlp_b1"][1]), (lru_bin, t["lru_b_in_2"][0]), (lru_cb, t["lru_conv_b_2"][0]),
                             (lru_br, t["lru_b_r_2"][0]), (lru_bi, t["lru_b_i_2"][0]), (lru_lam, t["lru_lambda_2"][0]),
                             *((lru_conv[:, 8 * j:8 * j + 8], t["lru_conv_w_2"][0, j]) for j in range(CONV))):
                cols(dst, src, small2_in)
            bias_row("mlp0")
            line(3)
            gate_piece(2)
            sp.wait_ge(glue_done, 1)
            load_row("lg1")
            load_row("lb1")
            line(4)
            line(5)
            gate_piece(3)
            for c in range(6, 9):
                line(c)
            for name in phases[1:]:
                if name in MLPS:
                    mlp(name)
                if name in FFNS:
                    ffn(name)
                if name == "ffn10":
                    bias_row("lru")
                    sp.wait_ge(glue_done, 5)
                    for r in ("post_lru", "pre_ffn20", "post_ffn20"):
                        load_row(r)
                if name in straight_phases:
                    for k in range(dict(PHASES)[name]):
                        line(FIRST[name] + k)
                        if name == "s5" and k == 3:
                            bias_row("mlp1")
                            sp.wait_ge(res_ok, 4)
                            load_row("lg3")
                            load_row("lb3")
                        if name == "s5" and k == 6:
                            sp.wait_ge(mod_sum, 7)
                            sp.wait_ge(s5_stored, 32)
                            sp.dma_start(mod[:, 0:2048], s5_store[0]).then_inc(s5_loaded, 16)
                            sp.dma_start(mod[:, 2048:4096], s5_store[1]).then_inc(s5_loaded, 16)
                        if name != "s5" and k == 1:
                            for r in {"lru": ("pre_kv", "pre_ffn11", "post_ffn11"), "kv": ("pre_att", "post_att"),
                                      "att": ("pre_ffn21", "post_ffn21")}[name]:
                                reload_row(r)
            sp.wait_ge(final_ok, 1)
            sp.dma_start(out[0].rearrange("(t p) d -> p t d", p=P), X[:, :, :]).then_inc(out_done, 16)
            sp.wait_ge(out_done, 16)

        @block.tensor
        def _(pe):
            spread = [0]

            def mm3(o, lh, ll, rh, rl, start, stop):
                pe.matmul(o, lh, rh, start=start, stop=False)
                pe.matmul(o, lh, rl, start=False, stop=False)
                return pe.matmul(o, ll, rh, start=False, stop=stop)

            def chunk_ready(c, i=None):
                pe.wait_ge(lo_done, c + 1 if i is None else i * 6 + (c + 1))

            def parts(c, shape):
                return shaped(whi[:, c % SPL, :], shape), shaped(wlo[:, c % SPL, :], shape)

            def columns(c, bank, i=None, src=(xhi, xlo)):
                chunk_ready(c, i)
                wh, wl = parts(c, (8, 256))
                for m in range(2):
                    for k in range(KT):
                        last = mm3(ps[:, bank, m * L:(m + 1) * L], wh[:, k, m * P:(m + 1) * P], wl[:, k, m * P:(m + 1) * P],
                                   src[0][:, k, :], src[1][:, k, :], k == 0, k == KT - 1)
                last.then_inc(w_used, 1)

            def rows_of(c, tile, i=None, first=False, final=False, src=(hhi, hlo)):
                chunk_ready(c, i)
                wh, wl = parts(c, (2, D))
                for tt in range(T):
                    for k in range(2):
                        for n in range(2):
                            last = mm3(ps[:, 2 * tt + n, :], src[0][:, tile + k, tt * P:(tt + 1) * P],
                                       src[1][:, tile + k, tt * P:(tt + 1) * P], wh[:, k, n * 512:(n + 1) * 512],
                                       wl[:, k, n * 512:(n + 1) * 512], first and k == 0, final and k == 1)
                    if final and tt == 0:
                        last.then_inc(acc_half, 1)
                last.then_inc(w_used, 1)

            def project(c, bias=False, src=(hhi, hlo)):
                for j in range(4):
                    rows_of(c + j, 2 * j, first=(j == 0 and not bias), final=(j == 3), src=src)

            def open_acc(name):
                pe.wait_ge(acc_free, 2 * ACC[name])
                if name in BIASED:
                    pe.wait_ge(brow_in, 16 * (BIASED.index(name) + 1))
                for b in range(4):
                    if name in BIASED:
                        last = pe.matmul(ps[:, b, :], ones[0:1, :], brow[0:1, (b % 2) * 512:(b % 2 + 1) * 512], start=True, stop=False)
                    else:
                        pe.matmul(ps[:, b, 0:L], zeros[:, 0:P], zeros, start=True, stop=False)
                        pe.matmul(ps[:, b, L:], zeros[:, 0:P], zeros, start=False, stop=False)
                if name in BIASED:
                    last.then_inc(acc_open, 1)

            def turn(name):
                if name == "mlp0":
                    pe.wait_ge(modb_out, 12)
                for tt in range(T):
                    pe.wait_ge(h_ready, 2 * XTS[name] + tt + 1)
                    for hf in range(2):
                        for j in range(4):
                            k = 4 * hf + j
                            last = pe.transpose(ps[:, 4 + 2 * tt + hf, j * P:(j + 1) * P], H[:, tt, k * P:(k + 1) * P], ident[:, :])
                        last.then_inc(xt_ps, 1)

            def input_ready(name):
                pe.wait_ge(xt_ok, 4 * (XTS[name] + 1))

            def spread_mod(acc, banks, third_count=None, s=mod_sum):
                if third_count is not None:
                    pe.wait_ge(s, third_count)
                for b, half_row in zip(banks, acc):
                    pe.matmul(ps[:, b, :], ones[:, :], half_row, start=True, stop=True).then_inc(modb_ps, 1)
                    spread[0] += 1

            def halves(ap, n):
                return [ap[:, 512 * q:512 * (q + 1)] for q in range(n)]

            def mlp(name):
                h, c = HID0[name], FIRST[name]
                open_acc(name)
                turn(name)
                input_ready(name)
                columns(c, 4)
                for a, b in mlp_runs(name):
                    with pe.Fori(a, b) as i:
                        for k in range(3):
                            columns(c + 1 + 2 * k, 4 + (k + 1) % 3, i)
                            pe.wait_ge(hid_ok, i * 3 + (h + k + 1))
                            rows_of(c + 2 + 2 * k, 2 * k, i)
                    if a == 0 and name == "mlp0":
                        pe.wait_ge(m1_sum, 2)
                        spread_mod(halves(modacc, 3), (5, 6, 7), 4)
                        pe.wait_ge(modb_out, 15)
                        spread_mod(halves(modacc, 6)[3:], (5, 6, 7))
                        pe.wait_ge(modb_out, 18)
                pe.wait_ge(hid_ok, h + 16)
                rows_of(c + 31, 0, final=True)

            def ffn(name):
                h, c = HID0[name], FIRST[name]
                open_acc(name)
                turn(name)
                input_ready(name)
                columns(c, 4)
                columns(c + 1, 6)
                with pe.Fori(0, 5) as i:
                    for k in range(2):
                        columns(c + 2 + 3 * k, 4 + (k + 1) % 2, i)
                        columns(c + 3 + 3 * k, 6 + (k + 1) % 2, i)
                        pe.wait_ge(hid_ok, i * 2 + (h + k + 1))
                        rows_of(c + 4 + 3 * k, 2 * k, i)
                pe.wait_ge(hid_ok, h + 11)
                rows_of(c + 32, 0, final=True)


            def mla():
                turn("mla")
                input_ready("mla")
                for c in range(2):
                    chunk_ready(c)
                    wh, wl = parts(c, (4, ZW))
                    for tt in range(T):
                        for k in range(4):
                            kt = 4 * c + k
                            last = mm3(ps[:, tt, 0:ZW], xhi[:, kt, tt * P:(tt + 1) * P], xlo[:, kt, tt * P:(tt + 1) * P],
                                       wh[:, k, :], wl[:, k, :], kt == 0, kt == KT - 1)
                    last.then_inc(w_used, 1)
                s5_matrices()
                for tt in range(T):
                    pe.wait_ge(zn_ok, tt + 1)
                    for j in range(4):
                        last = pe.transpose(ps[:, 4 + j // 2, (j % 2) * L + tt * P:(j % 2) * L + (tt + 1) * P],
                                            zn[:, tt, j * P:(j + 1) * P], ident[:, :])
                last.then_inc(zt_ps, 1)
                pe.wait_ge(s5t_ok, 8)
                chunk_ready(2)
                pe.wait_ge(zx_ok, 1)
                wh, wl = (w[:, 2 % SPL, :].rearrange("p (h n) -> p h n", h=HEADS) for w in (whi, wlo))
                for h in range(HEADS):
                    last = mm3(ps[:, h // 2, (h % 2) * L:(h % 2 + 1) * L], wh[:, h, 0:P], wl[:, h, 0:P], xhi[:, 2, :], xlo[:, 2, :],
                               True, True)
                    if h % 2:
                        last.then_inc(k_ps, 1)
                pe.wait_ge(zx_ok, 2)
                for tt in range(T):
                    for n in range(2):
                        last = mm3(ps[:, 4 + 2 * tt + n, :], xhi[:, 2, tt * P:(tt + 1) * P], xlo[:, 2, tt * P:(tt + 1) * P],
                                   wh[:, 4 * n:4 * n + 4, P:2 * P], wl[:, 4 * n:4 * n + 4, P:2 * P], True, True)
                    if tt == 0:
                        last.then_inc(v_ps, 1)
                last.then_inc(w_used, 1)
                for g in range(2):
                    chunk_ready(3 + g)
                    pe.wait_ge(k_ok, 4)
                    if g:
                        pe.wait_ge(q_ok, 2)
                        pe.wait_ge(qp_ok, 1)
                    wh, wl = (w[:, (3 + g) % SPL, 0:1536].rearrange("p (k h n) -> p k h n", k=2, h=4) for w in (whi, wlo))
                    for h in range(4):
                        for k in range(2):
                            last = mm3(ps[:, h // 2, (h % 2) * L:(h % 2 + 1) * L], wh[:, k, h, 0:P], wl[:, k, h, 0:P],
                                       xhi[:, k, :], xlo[:, k, :], k == 0, k == 1)
                        if h % 2:
                            last.then_inc(q_ps, 1)
                    for tt in range(T):
                        for k in range(2):
                            last = mm3(ps[:, 2, tt * L:(tt + 1) * L], xhi[:, k, tt * P:(tt + 1) * P], xlo[:, k, tt * P:(tt + 1) * P],
                                       wh[:, k, :, P:P + ROPE], wl[:, k, :, P:P + ROPE], k == 0, k == 1)
                    last.then_inc(w_used, 1)
                    pe.wait_ge(qp_ok, g + 1)
                    if g:
                        pe.wait_ge(qt_ok, 1)
                    for r in range(2):
                        for tt in range(T):
                            last = pe.transpose(ps[:, 3, r * L + tt * P:r * L + (tt + 1) * P], qp_tok[:, tt, r * P:(r + 1) * P], ident[:, :])
                    last.then_inc(qt_ps, 1)
                pe.wait_ge(q_ok, 4)
                pe.wait_ge(qt_ok, 2)
                pe.wait_ge(v_ok, 2)
                attention(0, qT, kT, V, True)
                rows_of(5, 0, first=True)
                rows_of(6, 2)
                pe.wait_ge(modb_out, 8)
                spread_mod(halves(modacc, 4)[2:], (6, 7), 2)
                rows_of(7, 4)
                rows_of(8, 6, final=True)
                pe.wait_ge(modb_out, 10)
                spread_mod(halves(modacc, 6)[4:], (6, 7), 1, m1_sum)

            def s5_matrices():
                pe.wait_ge(s5p_pool, 3)
                for r in range(2):
                    for q, b in enumerate((2, 3, 6, 7)):
                        if r:
                            pe.wait_ge(s5t_ok, q + 1)
                        for j in range(4):
                            m, ri = (4 * q + j) // 2, j % 2
                            blk = b_dg[:, m, ri, :, :] if r == 0 else c_pad[:, m, ri, :]
                            last = pe.transpose(ps[:, b, j * P:(j + 1) * P], blk, ident[:, :])
                        last.then_inc(s5p_ps, 1)

            def attention_spreads(i):
                if i == 1:
                    spread_mod(halves(G[:, 0, :], 2), (6, 7), 2, mod0_sum)
                if i == 6:
                    pe.wait_ge(modb_out, 6)
                    spread_mod(halves(modacc, 2), (6, 7), 1)

            def attention(n, q, k, v, rotary):
                for i in range(HEADS + 2):
                    if i < HEADS:
                        h, e = i, HEADS * n + i
                        if e >= 2:
                            pe.wait_ge(sm_ok, e - 1)
                        for lo, hi, tt, keys in ((0, P, 0, P), (P, 3 * P, 1, L)):
                            last = pe.matmul(ps[:, h % 2, lo:hi], q[:, h, tt * P:(tt + 1) * P], k[:, h, 0:keys], start=True, stop=not rotary)
                            if rotary:
                                a = 64 * (h % 2)
                                last = pe.matmul(ps[:, h % 2, lo:hi], qpT[a:a + 64, h // 2, tt * P:(tt + 1) * P], kpT[a:a + 64, 0:keys],
                                                 start=False, stop=True)
                        last.then_inc(s_ps, 1)
                    if 1 <= i <= HEADS:
                        h, e = i - 1, HEADS * n + i - 1
                        pe.wait_ge(p_ok, e + 1)
                        if e >= 2:
                            pe.wait_ge(pt_ok, e - 1)
                        for j in range(3):
                            last = pe.transpose(ps[:, 2 + h % 2, j * P:(j + 1) * P], (sm, sm2)[n][:, h % 2, j * P:(j + 1) * P], ident[:, :])
                        last.then_inc(pt_ps, 1)
                    if i >= 2:
                        h, e = i - 2, HEADS * n + i - 2
                        pe.wait_ge(pt_ok, e + 1)
                        if e >= 2:
                            pe.wait_ge(o_ok, e - 1)
                        pp = (pt, pt2)[n][:, h % 2, :]
                        pe.matmul(ps[:, 4 + h % 2, 0:L], v[:, 0, h * P:(h + 1) * P], pp[:, 0:L], start=True, stop=False)
                        pe.matmul(ps[:, 4 + h % 2, P:L], v[:, 1, h * P:(h + 1) * P], pp[:, L:3 * P], start=False, stop=True).then_inc(o_ps, 1)
                    if n == 0:
                        attention_spreads(i)
                pe.wait_ge(o_ok, HEADS * (n + 1))

            def s5():
                c = FIRST["s5"]
                turn("s5")
                pe.wait_ge(acc_free, 2 * ACC["s5"])
                pe.wait_ge(mod_sum, 6)
                spread_mod(halves(modacc, 4), (0, 1, 2, 3))
                input_ready("s5")
                for j in range(4):
                    columns(c + j, 4 + j)
                pe.wait_ge(modb_out, 22)
                pe.wait_ge(mod_sum, 7)
                spread_mod(halves(modacc, 6)[4:], (0, 1))
                pe.wait_ge(modb_out, 24)
                pe.wait_ge(u_ok, 4)
                pe.wait_ge(s5_loaded, 32)
                for i in range(-1, PAIRS + 1):
                    j = i + 1
                    if j < PAIRS:
                        m, a = j // 4, 32 * (j % 4)
                        if j >= 2:
                            pe.wait_ge(bu_rot, j - 1)
                        for r in range(2):
                            last = pe.matmul(ps[:, j % 2, r * L:(r + 1) * L], s5B[a:a + 32, m, r, :], uT[a:a + 32, m, :], start=True, stop=True)
                        last.then_inc(bu_ps, 1)
                    if 0 <= i < PAIRS:
                        pe.wait_ge(bu_rot, i + 1)
                        s = i % 2
                        pe.matmul(ps[:, 4 + s, :], ident[:, :], rot_a[:, s, :], start=True, stop=False)
                        pe.matmul(ps[:, 4 + s, :], ident[:, :], rot_b[:, s, :], start=False, stop=True).then_inc(w_ps, 1)
                    if i >= 1:
                        e = i - 1
                        m, a = e // 4, 32 * (e % 4)
                        pe.wait_ge(x_rot, e + 1)
                        if e % 4 == 0 and m >= 2:
                            pe.wait_ge(y_ok, m - 1)
                        s = e % 2
                        for q, (r, x) in enumerate(((0, xa[:, s, 0:L]), (0, xb[:, s, 0:L]), (1, xa[:, s, L:]), (1, xb[:, s, L:]))):
                            last = pe.matmul(ps[a:a + 32, 2 + m % 2, 0:L], s5C[:, m, r, a:a + 32], x, start=(q == 0), stop=(q == 3))
                        last.then_inc(x_used, 1)
                pe.wait_ge(g_ok, 2)
                for j in range(4):
                    columns(c + 4 + j, 4 + j)
                for j in range(4):
                    if j == 0:
                        pe.wait_ge(y_ok, KT)
                    pe.wait_ge(zz_lo, j + 1)
                    rows_of(c + 8 + j, 2 * j, first=(j == 0), final=(j == 3))

            def lru():
                c = FIRST["lru"]
                open_acc("lru")
                turn("lru")
                input_ready("lru")
                for j in range(8):
                    if j >= 4:
                        pe.wait_ge(lp_ok, j - 3)
                    columns(c + j, 4 + j % 4)
                chunk_ready(c + 9)
                rh, rl = parts(c + 8, (8, L))
                ih, il = parts(c + 9, (8, L))
                for m in range(KT):
                    h, j = m // 2, m % 2
                    pe.wait_ge(xc_ok, m // 4 + 1)
                    pe.wait_ge(lp_ok, 5 + min(m, 3)) if m < 4 else pe.wait_ge(lg_ok, m - 3)
                    for g, (wh, wl) in enumerate(((rh, rl), (ih, il))):
                        for k in range(2):
                            last = mm3(ps[:, 4 + m % 4, g * L:(g + 1) * L], wh[:, 2 * h + k, j * P:(j + 1) * P],
                                       wl[:, 2 * h + k, j * P:(j + 1) * P], xhi[:, 2 * h + k, :], xlo[:, 2 * h + k, :], k == 0, k == 1)
                    if m < KT - 1:
                        last.then_inc(lg_ps, 1)
                last.then_inc(w_used, 2)
                for j in range(4):
                    pe.wait_ge(hg_lo, j // 2 + 1)
                    rows_of(c + 10 + j, 2 * j, final=(j == 3))

            def kv():
                c = FIRST["kv"]
                turn("kv")
                pe.wait_ge(acc_free, 2 * ACC["kv"])
                input_ready("kv")
                for j in range(4):
                    columns(c + j, 4 + j)
                project(c + 4, src=(xhi, xlo))

            def att():
                c = FIRST["att"]
                turn("att")
                pe.wait_ge(acc_free, 2 * ACC["att"])
                input_ready("att")
                for j in range(4):
                    columns(c + j, 4 + j)
                pe.wait_ge(q_ok, 8)
                attention(1, qT2, kT2, V2, False)
                project(c + 4)

            pe.wait_ge(const_ok, 1)
            pe.wait_ge(s5_in, 16 * 21)
            pe.wait_ge(s5p_pool, 1)
            for k in range(3):
                last = pe.transpose(ps[:, k, 0:PAIRS], a_rows[:, k, :], ident[0:PAIRS, 0:PAIRS])
            last.then_inc(s5p_ps, 1)
            pe.wait_ge(mod0_sum, 1)
            spread_mod(halves(GA[:, :], 2) + halves(BA[:, :], 2), (4, 5, 6, 7))
            pe.wait_ge(modb_out, 4)
            run = {"mla": mla, "s5": s5, "lru": lru, "kv": kv, "att": att}
            for name in phases:
                run[name]() if name in run else (mlp if name in MLPS else ffn)(name)

        @block.scalar
        def _(act):
            steps = Steps(act, act_step)
            spread = [0]

            def hi(c, i=None):
                if i is None and c >= TOTAL:
                    return
                act.wait_ge(raw_in[c % RAW], 16 * (c // RAW + 1) if i is None else i * 32 + 16 * (c // RAW + 1))
                if c >= SPL:
                    act.wait_ge(w_used, c - SPL + 1 if i is None else i * 6 + (c - SPL + 1))
                n = width.get(c, CH) if i is None else CH
                act.activation(whi[:, c % SPL, 0:n], raw[:, c % RAW, 0:n], ACT.Copy).then_inc(hi_done, 1)

            def acc_wait(name, tt):
                if tt == 0:
                    act.wait_ge(acc_half, ACC[name] + 1)
                else:
                    act.wait_ge(w_used, FIRST[name] + dict(PHASES)[name])

            def turned(name):
                for tt in range(T):
                    for hf in range(2):
                        act.wait_ge(xt_ps, 4 * XTS[name] + 2 * tt + hf + 1)
                        act.activation(xhi[:, 4 * hf:4 * hf + 4, tt * P:(tt + 1) * P],
                                       ps[:, 4 + 2 * tt + hf, :].rearrange("p (k n) -> p k n", k=4), ACT.Copy).then_inc(xhi_ok, 1)
                if name != "mla":
                    hi(FIRST[name] + 2)

            def despread(dsts):
                for dst, b, add in dsts:
                    spread[0] += 1
                    act.wait_ge(modb_ps, spread[0])
                    act.activation(dst, ps[:, b, :], ACT.Copy, bias=add).then_inc(modb_out, 1)

            def half_rows(ap, banks, add):
                return [(ap[:, 512 * q:512 * (q + 1)], b, add) for q, b in enumerate(banks)]

            def squares(name, tt):
                acc_wait(name, tt)
                steps.did(act.activation(H[:, tt, :], ps[:, 2 * tt:2 * tt + 2, :].rearrange("p b n -> p (b n)"), ACT.Square,
                                         accum_out=ssq[:, tt:tt + 1]))
                steps.settle()
                w, e = (4.0, eps_rms4) if name in FFNS else (1.0, eps_rms)
                mean_root(tt, ssq[:, tt:tt + 1], w / D, e).then_inc(sq_done, 1)

            def mean_root(k, src, scale, bias):
                act.activation(val[:, k:k + 1], src, ACT.Identity, scale=scale, bias=bias)
                return act.activation(root[:, k:k + 1], src, ACT.Sqrt, scale=scale, bias=bias)

            def warm_sqrt():
                steps.did(act.activation(root[:, 6:7], eps_ln, ACT.Sqrt))
                steps.settle()

            def ln_roots(name):
                k = ("mla", "mlp0", "s5", "mlp1").index(name)
                warm_sqrt()
                for tt in range(T):
                    act.wait_ge(var_ok, 2 * k + tt + 1)
                    mean_root(tt, mv[:, 2 * tt + 1:2 * tt + 2], 1.0, eps_ln).then_inc(root_ok, 1)

            def rms_glue(name, norm=True):
                warm_sqrt()
                for tt in range(T):
                    squares(name, tt)
                if norm:
                    norm_squares()

            def norm_squares():
                for tt in range(T):
                    xs[0] += 1
                    act.wait_ge(x_new, xs[0])
                    steps.did(act.activation(Y[:, tt, :], X[:, tt, :], ACT.Square, accum_out=ssq[:, 2 + tt:3 + tt]))
                    steps.settle()
                    mean_root(2 + tt, ssq[:, 2 + tt:3 + tt], 1 / D, eps_rms).then_inc(sq_done, 1)

            xs = [0]

            def mlp(name):
                l, h, c = MLPS.index(name), HID0[name], FIRST[name]
                turned(name)
                if l == 0:
                    act.wait_ge(small2_in, 16 * 13)

                def hidden(k, i=None):
                    n = c + 2 * k + (0 if k else 1)
                    act.wait_ge(w_used, n if i is None else i * 6 + n)
                    s = k % 3
                    for m in range(2):
                        b = b1c[:, 32 * l + 2 * k + m:32 * l + 2 * k + m + 1] if i is None else b1c[:, bass.ds(i * 6 + (32 * l + 2 * k + m), 1)]
                        steps.did(act.activation(TMP[:, 512 * s + m * L:512 * s + (m + 1) * L], ps[:, 4 + s, m * L:(m + 1) * L],
                                                 ACT.Relu, bias=b))
                    steps.settle()
                    act.activation(hhi[:, 2 * s:2 * s + 2, :].rearrange("p k l -> p (k l)"), TMP[:, 512 * s:512 * (s + 1)],
                                   ACT.Square).then_inc(hid_hi, 1)

                for a, b in mlp_runs(name):
                    with act.Fori(a, b) as i:
                        steps.loop(i, a, 6)
                        for k in range(3):
                            hidden(k, i)
                            hi(c + 3 + 2 * k, i)
                            hi(c + 4 + 2 * k, i)
                    steps.end(b - a)
                    if a == 0 and name == "mlp0":
                        despread(half_rows(B[:, :], (5, 6), 0.0) + half_rows(A[:, :], (7,), 1.0))
                        despread([(A[:, 512:1024], 5, 1.0)] + half_rows(G[:, 0, :], (6, 7), 1.0))
                hidden(15)
                hi(c + 33)

            def ffn(name):
                h, c = HID0[name], FIRST[name]
                s0 = h - HID0["ffn10"]
                turned(name)

                def gate(k, i=None):
                    act.wait_ge(w_used, c + 3 * k + 1 if i is None else i * 6 + (c + 3 * k + 1))
                    act.activation(TMP[:, 512 * (k % 2):512 * (k % 2 + 1)], ps[:, 4 + k % 2, :], ACT.Silu).then_inc(act1, 1)

                def hidden(k, i=None):
                    act.wait_ge(prod, s0 + k + 1 if i is None else i * 2 + (s0 + k + 1))
                    s = k % 2
                    act.activation(hhi[:, 2 * s:2 * s + 2, :].rearrange("p k l -> p (k l)"), TMP[:, 1024 + 512 * s:1536 + 512 * s],
                                   ACT.Copy).then_inc(hid_hi, 1)

                with act.Fori(0, 5) as i:
                    for k in range(2):
                        gate(k, i)
                        hi(c + 3 + 3 * k, i)
                        hidden(k, i)
                        hi(c + 4 + 3 * k, i)
                        hi(c + 5 + 3 * k, i)
                gate(10)
                hidden(10)
                hi(c + 33)
                hi(c + 34)

            def rope_table():
                act.wait_ge(rope_r, 1)
                rr = AR[:, 0:64].rearrange("p (t n) -> p t n", t=T)
                hh = AR[:, 64:128].rearrange("p (t n) -> p t n", t=T)
                act.activation(rope[:, 1, :, :], rr, ACT.Sin)
                steps.did(act.activation(hh, rr, ACT.Sin, scale=0.5))
                steps.settle()
                steps.did(act.activation(hh, hh, ACT.Square))
                steps.settle()
                act.activation(rope[:, 0, :, :], hh, ACT.Copy, scale=-2.0, bias=1.0).then_inc(rope_tab, 1)

            def s5_matrices():
                for q in range(8):
                    act.wait_ge(s5p_ps, q + 2)
                    stage = s5_stage if q < 4 else H.rearrange("p t d -> p (t d)").rearrange("p (m r n) -> p m r n", m=KT, r=2)
                    st = stage[:, 2 * (q % 4):2 * (q % 4) + 2]
                    src = ps[:, (2, 3, 6, 7)[q % 4], :].rearrange("p (m r n) -> p m r n", m=2, r=2)
                    act.activation(st[:, :, 0, :], src[:, :, 0, :], ACT.Copy)
                    act.activation(st[:, :, 1, :], src[:, :, 1, :], ACT.Copy, scale=1.0 if q < 4 else -1.0).then_inc(s5t_ok, 1)
                    if q % 4 == 3:
                        act.wait_ge(s5t_ok, q + 1)
                        act.dma_start(s5_store[q // 4], stage.rearrange("p m r n -> p (m r n)")).then_inc(s5_stored, 16)

            def mla():
                turned("mla")
                hi(2)
                hi(3)
                for tt in range(T):
                    act.wait_ge(w_used, 2)
                    act.activation(qpT[:, tt, 0:QL], ps[:, tt, 0:QL], ACT.Square, accum_out=ssq[:, 2 * tt:2 * tt + 1])
                    steps.did(act.activation(qpT[:, 2 + tt, 0:KVL], ps[:, tt, QL:QL + KVL], ACT.Square, accum_out=ssq[:, 2 * tt + 1:2 * tt + 2]))
                    steps.settle()
                    mean_root(2 * tt, ssq[:, 2 * tt:2 * tt + 1], 1 / QL, eps_rms)
                    mean_root(2 * tt + 1, ssq[:, 2 * tt + 1:2 * tt + 2], 1 / KVL, eps_rms).then_inc(z_sq, 1)
                s5_matrices()
                act.wait_ge(zt_ps, 1)
                act.activation(xhi[:, 2, :], ps[:, 5, 0:L], ACT.Copy)
                act.activation(kpT, ps[:, 5, L:2 * L], ACT.Copy).then_inc(zhi_ok, 1)
                act.activation(xhi[:, 0:2, :].rearrange("p k l -> p (k l)"), ps[:, 4, :], ACT.Copy).then_inc(zhi_ok, 1)
                hi(4)
                for b in range(4):
                    act.wait_ge(k_ps, b + 1)
                    act.activation(kT[:, 2 * b:2 * b + 2, :].rearrange("p h l -> p (h l)"), ps[:, b, :], ACT.Copy).then_inc(k_ok, 1)
                hi(5)
                for g in range(2):
                    for b in range(2):
                        act.wait_ge(q_ps, 2 * g + b + 1)
                        if g == 0 and b == 0:
                            act.wait_ge(mod0_sum, 2)
                        act.activation(qT[:, 4 * g + 2 * b:4 * g + 2 * b + 2, :].rearrange("p h l -> p (h l)"), ps[:, b, :], ACT.Copy).then_inc(q_ok, 1)
                    hi(6 + g)
                    act.wait_ge(qt_ps, g + 1)
                    act.activation(qpT[:, 2 * g:2 * g + 2, :].rearrange("p r l -> p (r l)"), ps[:, 3, :], ACT.Copy).then_inc(qt_ok, 1)
                attention(0)

                def fetch(n):
                    m, q = late[n // 4]
                    if n == 7:
                        act.wait_ge(m1_sum, 1)
                    elif n >= 4:
                        act.wait_ge(m1_used, n - 3)
                    act.dma_start(m0[n % 4], mod_w[m].rearrange("(k p) n -> p k n", p=P)[:, 2 * (n % 4):2 * (n % 4) + 2, D * q:D * (q + 1)]).then_inc(m0_in[n % 4], 16)

                act.wait_ge(m1_clear, 1)
                for m, q in late:
                    act.dma_start(modacc[0:1, D * q:D * (q + 1)], mod_b[m][D * q:D * (q + 1)].rearrange("(o n) -> o n", o=1)).then_inc(m1_bias, 16)
                for n in range(4):
                    fetch(n)
                hi(8)
                for n in range(4, 8):
                    fetch(n)
                    if n == 5:
                        hi(9)
                despread(half_rows(A[:, :], (6, 7), 1.0))
                hi(10)
                softplus()

            def attention(n):
                sms, pts = (sm, sm2)[n], (pt, pt2)[n]
                for i in range(HEADS + 2):
                    if i < HEADS:
                        h, e = i, HEADS * n + i
                        act.wait_ge(mx_ok, e + 1)
                        for tt, (lo, up) in enumerate(((0, P), (P, 3 * P))):
                            last = act.activation(sms[:, h % 2, lo:up], sms[:, h % 2, lo:up], ACT.Exp, bias=attm[:, 2 * (h % 2) + tt:2 * (h % 2) + tt + 1],
                                                  accum_out=atts[:, 2 * (h % 2) + tt:2 * (h % 2) + tt + 1])
                        last.then_inc(exp_ok, 1)
                    if 1 <= i <= HEADS:
                        h, e = i - 1, HEADS * n + i - 1
                        act.wait_ge(pt_ps, e + 1)
                        if e >= 2:
                            act.wait_ge(o_ps, e - 1)
                        act.activation(pts[:, h % 2, :], ps[:, 2 + h % 2, 0:3 * P], ACT.Copy).then_inc(pt_ok, 1)
                    if i >= 2:
                        h, e = i - 2, HEADS * n + i - 2
                        act.wait_ge(o_ps, e + 1)
                        act.activation(hhi[:, h, :], ps[:, 4 + h % 2, 0:L], ACT.Copy).then_inc(o_hi, 1)
                    if n == 0 and i in (2, 7):
                        dst, add = {2: (G[:, 0, :], 1.0), 7: (B[:, :], 0.0)}[i]
                        despread(half_rows(dst, (6, 7), add))

            def s5():
                c = FIRST["s5"]
                turned("s5")
                despread(half_rows(B[:, :], (0, 1), 0.0) + half_rows(A[:, :], (2, 3), 1.0))
                for j in range(4):
                    act.wait_ge(w_used, c + j + 1)
                    act.activation(uT[:, 2 * j:2 * j + 2, :].rearrange("p k l -> p (k l)"), ps[:, 4 + j, :], ACT.Copy).then_inc(u_ok, 1)
                    hi(c + 3 + j)
                despread(half_rows(G[:, 1, :], (0, 1), 1.0))
                for i in range(PAIRS):
                    s = i % 3
                    act.wait_ge(phase_r, i + 1)
                    if i >= 3:
                        act.wait_ge(x_rot, i - 2)
                    act.activation(tabs[:, s, 1, :], ph[:, i % 2, 0, :], ACT.Sin, scale=TWO_PI * (1 - 2.0 ** -22))
                    if i:
                        act.wait_ge(table_ok, i)
                    steps.did(act.activation(half, ph[:, i % 2, 0, :], ACT.Sin, scale=math.pi))
                    steps.settle()
                    steps.did(act.activation(half, half, ACT.Square))
                    steps.settle()
                    act.activation(tabs[:, s, 0, :], half, ACT.Copy, scale=-2.0, bias=1.0).then_inc(table_ok, 1)
                yf = Y.rearrange("p t d -> p (t d)")
                gx = xhi[:, :, :].rearrange("p k l -> p (k l)")
                for q in range(2):
                    act.wait_ge(y_ok, 4 * q + 4)
                    act.activation(yf[:, 1024 * q:1024 * (q + 1)], yf[:, 1024 * q:1024 * (q + 1)], ACT.Gelu_apprx_tanh).then_inc(g_act, 1)
                    act.wait_ge(g_act, q + 1)
                    act.activation(gx[:, 1024 * q:1024 * (q + 1)], yf[:, 1024 * q:1024 * (q + 1)], ACT.Copy).then_inc(g_hi, 1)
                for j in range(4):
                    act.wait_ge(w_used, c + 4 + j + 1)
                    if j >= 2:
                        act.wait_ge(zz_ok, j - 1)
                    for m in range(2):
                        last = act.activation(sig[:, j % 2, m * L:(m + 1) * L], ps[:, 4 + j, m * L:(m + 1) * L], ACT.Sigmoid,
                                              bias=bglu[:, 2 * j + m:2 * j + m + 1])
                    last.then_inc(sig_ok, 1)
                    hi(c + 7 + j)
                    act.wait_ge(zz_ok, j + 1)
                    act.activation(hhi[:, 2 * j:2 * j + 2, :].rearrange("p k l -> p (k l)"), zz[:, j % 2, :], ACT.Copy).then_inc(zz_hi, 1)
                for j in range(3):
                    hi(c + 11 + j)

            def lru():
                c = FIRST["lru"]
                turned("lru")
                for j in range(4):
                    act.wait_ge(w_used, c + j + 1)
                    for m in range(2):
                        last = act.activation(xbp[:, 2 * j + m, 3:], ps[:, 4 + j, m * L:(m + 1) * L], ACT.Identity,
                                              bias=lru_bin[:, 2 * j + m:2 * j + m + 1])
                    last.then_inc(lp_ok, 1)
                    hi(c + 3 + j)
                for j in range(4, 8):
                    act.wait_ge(w_used, c + j + 1)
                    if j == 7:
                        for q in range(2):
                            act.wait_ge(conv_ok, q + 1)
                            act.activation(xhi[:, 4 * q:4 * q + 4, :], xcT[:, 4 * q:4 * q + 4, :], ACT.Copy).then_inc(xc_hi, 1)
                    for m in range(2):
                        last = act.activation(gyT[:, 2 * (j - 4) + m, :], ps[:, j, m * L:(m + 1) * L], ACT.Gelu_apprx_tanh,
                                              bias=lru_bin[:, 2 * j + m:2 * j + m + 1])
                    last.then_inc(lp_ok, 1)
                    hi(c + 3 + j)
                def gates(m):
                    if m < KT - 1:
                        act.wait_ge(lg_ps, m + 1)
                    else:
                        act.wait_ge(w_used, c + 10)
                    act.activation(rT[:, m, :], ps[:, 4 + m % 4, 0:L], ACT.Sigmoid, bias=lru_br[:, m:m + 1])
                    act.activation(iT[:, m, :], ps[:, 4 + m % 4, L:2 * L], ACT.Sigmoid, bias=lru_bi[:, m:m + 1]).then_inc(lg_ok, 1)

                for q in range(2):
                    for m in range(4 * q, 4 * q + 4):
                        gates(m)
                    act.wait_ge(lg_ok, 4 * q + 4)
                    for m in range(4 * q, 4 * q + 4):
                        act.activation(aT[:, m, :], rT[:, m, :], ACT.Exp, scale=lam_n[:, m:m + 1])
                        last = act.activation(tT[:, m, :], rT[:, m, :], ACT.Tanh, scale=lam_p[:, m:m + 1])
                    last.then_inc(la_ok, 1)
                for q in range(2):
                    act.wait_ge(m2_ok, q + 1)
                    act.activation(tT[:, 4 * q:4 * q + 4, :], tT[:, 4 * q:4 * q + 4, :], ACT.Sqrt).then_inc(mult_ok, 1)
                hi(c + 11)
                for q in range(2):
                    act.wait_ge(hg_ok, q + 1)
                    act.activation(hhi[:, 4 * q:4 * q + 4, :], aT[:, 4 * q:4 * q + 4, :], ACT.Copy).then_inc(hg_hi, 1)
                for j in range(4):
                    hi(c + 12 + j)

            def softplus():
                act.wait_ge(lam_ok, 1)
                steps.did(act.activation(lam_p, lam_n, ACT.Exp, scale=-1.0))
                steps.settle()
                act.activation(lam_p, lam_p, ACT.Ln, bias=1.0).then_inc(lam_exp, 1)

            def kv():
                c = FIRST["kv"]
                turned("kv")
                for j in range(4):
                    act.wait_ge(w_used, c + j + 1)
                    act.activation(kT2[:, 2 * j:2 * j + 2, :].rearrange("p k l -> p (k l)"), ps[:, 4 + j, :], ACT.Copy).then_inc(k_ok, 1)
                    hi(c + 3 + j)
                for j in range(3):
                    hi(c + 7 + j)

            def att():
                c = FIRST["att"]
                turned("att")
                for j in range(4):
                    act.wait_ge(w_used, c + j + 1)
                    act.activation(qT2[:, 2 * j:2 * j + 2, :].rearrange("p k l -> p (k l)"), ps[:, 4 + j, :], ACT.Copy).then_inc(q_ok, 1)
                    hi(c + 3 + j)
                attention(1)
                for j in range(3):
                    hi(c + 7 + j)

            act.wait_ge(c_in, 16)
            act.activation(csil, craw, ACT.Silu).then_inc(csil_ok, 1)
            for k, src in enumerate((t["ssm_a_re"][0], t["ssm_a_im"][0])):
                act.dma_start(a_rows[:, k, :], src.rearrange("(q g) p -> q (g p)", g=2)).then_inc(s5_in, 16)
            act.dma_start(ldt_rows, t["ssm_log_dt"][0].rearrange("(q g) -> q g", g=2)).then_inc(s5_in, 16)
            for r, src in enumerate((t["ssm_b_re"][0], t["ssm_b_im"][0])):
                act.dma_start(b_in[:, r, :, :], src.rearrange("(q g) p c -> (g p) q c", g=2)).then_inc(s5_in, 16)
            act.wait_ge(const_ok, 1)
            for r, src in enumerate((t["ssm_c_re"][0], t["ssm_c_im"][0])):
                v = src.rearrange("(m i g) c p -> i g c m p", m=KT, i=4)
                for i in range(4):
                    for g in range(2):
                        a = 32 * i + 16 * g
                        act.dma_start(c_pad[a:a + 16, :, r, 64 * g:64 * g + 64], v[i, g]).then_inc(s5_in, 16)
            act.wait_ge(s5p_ps, 1)
            for k in range(3):
                last = act.activation(g0v[:, k, :], ps[:, k, 0:PAIRS], ACT.Copy)
            last.then_inc(s5p_act, 1)
            act.wait_ge(s5p_act, 1)
            act.activation(g0v[:, 2, :], g0v[:, 2, :], ACT.Exp).then_inc(s5p_act, 1)
            act.wait_ge(s5p_pool, S5P_ANGLE)
            act.activation(rho, g0v[:, 3, :], ACT.Exp).then_inc(s5p_act, 1)
            act.activation(g0v[:, 6, :], g0v[:, 5, :], ACT.Sin)
            act.activation(g0v[:, 7, :], g0v[:, 5, :], ACT.Sin, scale=0.5).then_inc(s5p_act, 1)
            act.wait_ge(s5p_act, 4)
            act.activation(g0v[:, 7, :], g0v[:, 7, :], ACT.Square).then_inc(s5p_act, 1)
            act.wait_ge(s5p_act, 5)
            act.activation(g0v[:, 7, :], g0v[:, 7, :], ACT.Copy, scale=-2.0, bias=1.0).then_inc(s5p_act, 1)
            hi(0)
            despread(half_rows(B[:, :], (4, 5), 0.0) + half_rows(A[:, :], (6, 7), 1.0))
            rope_table()
            hi(1)
            run = {"mla": mla, "s5": s5, "lru": lru, "kv": kv, "att": att}
            for name in phases:
                if name in run:
                    run[name]()
                else:
                    (mlp if name in MLPS else ffn)(name)
                if name in ("ffn10", "lru", "ffn20", "ffn11", "att", "ffn21"):
                    rms_glue(name, name != "ffn21")
                if name in ("mla", "mlp0", "s5", "mlp1"):
                    ln_roots(name)
                if name == "mla":
                    despread(half_rows(G[:, 1, :], (6, 7), 1.0))
                if name == "mlp1":
                    norm_squares()
            act.wait_ge(s5_stored, 32)


        @block.vector
        def _(dve):
            steps = Steps(dve, dve_step)
            spare = small[0:1, 511:512]
            sq, xn = [0], [0]

            def do(ins):
                steps.did(ins)
                steps.settle()

            def lo(c, i=None):
                if i is None and c >= TOTAL:
                    return
                dve.wait_ge(hi_done, c + 1 if i is None else i * 6 + (c + 1))
                n = width.get(c, CH) if i is None else CH
                dve.tensor_tensor(wlo[:, c % SPL, 0:n], raw[:, c % RAW, 0:n], whi[:, c % SPL, 0:n].bitcast(F32),
                                  ALU.subtract).then_inc(lo_done, 1)

            def rest(dst, src, hi_part):
                return dve.tensor_tensor(dst, src, hi_part.bitcast(F32), ALU.subtract)

            def rsqrt(k, n=1):
                c = slice(k, k + n)
                y, tmp = recip[:, 0:n], newton[:, 0:n]
                do(dve.reciprocal(y, root[:, c]))
                do(dve.tensor_tensor(tmp, y, y, ALU.mult))
                do(dve.scalar_tensor_tensor(tmp, tmp, -0.5, val[:, c], ALU.mult, ALU.mult))
                do(dve.scalar_tensor_tensor(rsq[:, c], tmp, 1.5, y, ALU.add, ALU.mult))

            def acc_wait(name, tt):
                if tt == 0:
                    dve.wait_ge(acc_half, ACC[name] + 1)
                else:
                    dve.wait_ge(w_used, FIRST[name] + dict(PHASES)[name])

            def acc_tile(tt):
                return ps[:, 2 * tt:2 * tt + 2, :].rearrange("p b n -> p (b n)")

            def turned(name):
                for tt in range(T):
                    for hf in range(2):
                        dve.wait_ge(xhi_ok, 4 * XTS[name] + 2 * tt + hf + 1)
                        rest(xlo[:, 4 * hf:4 * hf + 4, tt * P:(tt + 1) * P],
                             ps[:, 4 + 2 * tt + hf, :].rearrange("p (k n) -> p k n", k=4),
                             xhi[:, 4 * hf:4 * hf + 4, tt * P:(tt + 1) * P]).then_inc(xt_ok, 1)
                if name != "mla":
                    lo(FIRST[name] + 2)

            def row_read(name, s, n):
                dve.wait_ge(s, n)
                dve.memset(spare, 0.0).then_inc(row_used, 1)
                dve.wait_ge(row_used, ROW_INDEX[name] - ROW_FIRST + 1)

            def normed(name, nxt):
                pre = "pre_" + nxt
                for tt in range(T):
                    if name is not None:
                        sq[0] += 1
                        dve.wait_ge(sq_done, sq[0])
                        rsqrt(2 + tt)
                    if tt == 0:
                        row_wait(dve, pre)
                    dve.scalar_tensor_tensor(H[:, tt, :], X[:, tt, :], rsq[:, 2 + tt:3 + tt], row(pre), ALU.mult, ALU.mult).then_inc(h_ready, 1)
                row_read(pre, h_ready, 2 * XTS[nxt] + 2)

            def ln_glue(name):
                k = {"mla": 1, "mlp0": 2, "s5": 3, "mlp1": 4}[name]
                for tt in range(T):
                    acc_wait(name, tt)
                    if tt == 0:
                        dve.wait_ge(modb_out, (6, 12, 18, 24)[k - 1])
                        if k == 1:
                            dve.wait_ge(x_scaled, 1)
                        else:
                            dve.wait_ge(res_ok, 2 * (k - 1))
                    dve.tensor_tensor(Y[:, tt, :], acc_tile(tt), G[:, (k - 1) % 2, :], ALU.mult).then_inc(acc_free, 1)
                    dve.wait_ge(acc_free, 2 * ACC[name] + tt + 1)
                    do(dve.tensor_tensor(Y[:, tt, :], Y[:, tt, :], X[:, tt, :], ALU.add))
                    for n in range(2):
                        steps.did(dve.bn_stats(stats[:, 12 * tt + 6 * n:12 * tt + 6 * n + 6], Y[:, tt, n * 512:(n + 1) * 512]))
                    steps.settle()
                    dve.bn_aggr(mv[:, 2 * tt:2 * tt + 2], stats[:, 12 * tt:12 * tt + 12]).then_inc(var_ok, 1)
                for tt in range(T):
                    dve.wait_ge(root_ok, 2 * (k - 1) + tt + 1)
                    rsqrt(tt)
                    dve.scalar_tensor_tensor(nmr[:, tt:tt + 1], mv[:, 2 * tt:2 * tt + 1], -1.0, rsq[:, tt:tt + 1], ALU.mult, ALU.mult).then_inc(ln_stats, 1)
                    if tt == 0:
                        if k < 4:
                            dve.wait_ge(vec_done, k)
                        else:
                            row_wait(dve, "lg4")
                            row_wait(dve, "lb4")
                    do(dve.scalar_tensor_tensor(H[:, tt, :], Y[:, tt, :], mv[:, 2 * tt:2 * tt + 1], A[:, :], ALU.subtract, ALU.mult))
                    dst, s = (H, h_ready) if k < 4 else (X, x_new)
                    dve.scalar_tensor_tensor(dst[:, tt, :], H[:, tt, :], rsq[:, tt:tt + 1], B[:, :], ALU.mult, ALU.add).then_inc(s, 1)
                if k < 4:
                    dve.wait_ge(h_ready, 2 * XTS[name] + 4)
                else:
                    xn[0] += 2
                    dve.wait_ge(x_new, xn[0])
                dve.memset(spare, 0.0).then_inc(glue_done, 1)
                dve.wait_ge(glue_done, k + 1)
                if k == 4:
                    normed(name, "ffn10")

            def rms_glue(name, nxt):
                post = "post_" + name
                for tt in range(T):
                    sq[0] += 1
                    dve.wait_ge(sq_done, sq[0])
                    rsqrt(tt)
                    if tt == 0:
                        row_wait(dve, post)
                    dve.scalar_tensor_tensor(Y[:, tt, :], acc_tile(tt), rsq[:, tt:tt + 1], row(post), ALU.mult, ALU.mult).then_inc(acc_free, 1)
                    dve.wait_ge(acc_free, 2 * ACC[name] + tt + 1)
                    dve.tensor_tensor(X[:, tt, :], X[:, tt, :], Y[:, tt, :], ALU.add).then_inc(x_new, 1)
                row_read(post, acc_free, 2 * ACC[name] + 2)
                xn[0] += 2
                dve.wait_ge(x_new, xn[0])
                if nxt is not None:
                    normed(name, nxt)

            def mlp(name):
                h, c = HID0[name], FIRST[name]
                turned(name)

                def hidden(k, i=None):
                    dve.wait_ge(hid_hi, h + k + 1 if i is None else i * 3 + (h + k + 1))
                    s = k % 3
                    r = TMP[:, 512 * s:512 * (s + 1)]
                    if k:
                        dve.wait_ge(hid_ok, h + k if i is None else i * 3 + (h + k))
                    do(dve.tensor_tensor(TMP[:, 1536:2048], r, r, ALU.mult))
                    rest(hlo[:, 2 * s:2 * s + 2, :].rearrange("p k l -> p (k l)"), TMP[:, 1536:2048],
                         hhi[:, 2 * s:2 * s + 2, :].rearrange("p k l -> p (k l)")).then_inc(hid_ok, 1)

                for a, b in mlp_runs(name):
                    with dve.Fori(a, b) as i:
                        steps.loop(i, a, 3)
                        for k in range(3):
                            hidden(k, i)
                            lo(c + 3 + 2 * k, i)
                            lo(c + 4 + 2 * k, i)
                    steps.end(b - a)
                hidden(15)
                lo(c + 33)

            def ffn(name):
                h, c = HID0[name], FIRST[name]
                s0 = h - HID0["ffn10"]
                turned(name)

                def product(k, i=None):
                    dve.wait_ge(act1, s0 + k + 1 if i is None else i * 2 + (s0 + k + 1))
                    n = c + 3 * k + (1 if k else 2)
                    dve.wait_ge(w_used, n if i is None else i * 6 + n)
                    s = k % 2
                    dve.tensor_tensor(TMP[:, 1024 + 512 * s:1536 + 512 * s], TMP[:, 512 * s:512 * (s + 1)], ps[:, 6 + s, :],
                                      ALU.mult).then_inc(prod, 1)

                def hidden(k, i=None):
                    dve.wait_ge(hid_hi, h + k + 1 if i is None else i * 2 + (h + k + 1))
                    s = k % 2
                    rest(hlo[:, 2 * s:2 * s + 2, :].rearrange("p k l -> p (k l)"), TMP[:, 1024 + 512 * s:1536 + 512 * s],
                         hhi[:, 2 * s:2 * s + 2, :].rearrange("p k l -> p (k l)")).then_inc(hid_ok, 1)

                with dve.Fori(0, 5) as i:
                    for k in range(2):
                        lo(c + 3 + 3 * k, i)
                        product(k, i)
                        hidden(k, i)
                        lo(c + 4 + 3 * k, i)
                        lo(c + 5 + 3 * k, i)
                product(10)
                hidden(10)
                lo(c + 33)
                lo(c + 34)

            def table(k, tt, heads):
                return rope[:, k, tt, :].rearrange("p (h x n) -> p h x n", h=1, x=1).to_broadcast([P, heads, 2, 32])

            def rotate(dsts, src, tt, heads):
                n = heads * ROPE
                a, b = (rt.rearrange("p s n -> p (s n)")[:, q * 256:q * 256 + n].rearrange("p (h x n) -> p h x n", h=heads, x=2) for q in range(2))
                x = src.rearrange("p (h x n) -> p h x n", h=heads, x=2)
                steps.did(dve.tensor_tensor(a, x, table(0, tt, heads), ALU.mult))
                do(dve.tensor_tensor(b, x, table(1, tt, heads), ALU.mult))
                for dst in dsts:
                    d = dst.rearrange("p (h x n) -> p h x n", h=heads, x=2)
                    dve.tensor_tensor(d[:, :, 0, :], a[:, :, 0, :], b[:, :, 1, :], ALU.subtract)
                    last = dve.tensor_tensor(d[:, :, 1, :], b[:, :, 0, :], a[:, :, 1, :], ALU.add)
                return last

            def mla():
                turned("mla")
                lo(2)
                first_gate(0)
                first_gate(1)
                lo(3)
                for tt in range(T):
                    dve.wait_ge(z_sq, tt + 1)
                    rsqrt(2 * tt, 2)
                    dve.scalar_tensor_tensor(zn[:, tt, 0:QL], ps[:, tt, 0:QL], rsq[:, 2 * tt:2 * tt + 1], G[:, 1, 0:QL], ALU.mult, ALU.mult)
                    dve.scalar_tensor_tensor(zn[:, tt, QL:QL + KVL], ps[:, tt, QL:QL + KVL], rsq[:, 2 * tt + 1:2 * tt + 2],
                                             G[:, 1, QL:QL + KVL], ALU.mult, ALU.mult)
                    if tt == 0:
                        dve.wait_ge(rope_tab, 1)
                    rotate([zn[:, tt, 384:448], zn[:, tt, 448:512]], ps[:, tt, QL + KVL:ZW], tt, 1).then_inc(zn_ok, 1)
                    dve.wait_ge(zn_ok, tt + 1)
                dve.wait_ge(zhi_ok, 1)
                rest(xlo[:, 2, :], ps[:, 5, 0:L], xhi[:, 2, :]).then_inc(zx_ok, 1)
                dve.wait_ge(zhi_ok, 2)
                rest(xlo[:, 0:2, :].rearrange("p k l -> p (k l)"), ps[:, 4, :], xhi[:, 0:2, :].rearrange("p k l -> p (k l)")).then_inc(zx_ok, 1)
                first_gate(2)
                lo(4)
                dve.wait_ge(s5_stored, 32)
                for tt in range(T):
                    dve.wait_ge(v_ps, 1) if tt == 0 else dve.wait_ge(w_used, 3)
                    dve.tensor_copy(V[:, tt, :], ps[:, 4 + 2 * tt:6 + 2 * tt, :].rearrange("p b n -> p (b n)")).then_inc(v_ok, 1)
                lo(5)
                first_gate(3)
                for g in range(2):
                    dve.wait_ge(w_used, 4 + g)
                    if g:
                        dve.wait_ge(qt_ps, 1)
                    for tt in range(T):
                        last = rotate([qp_tok[:, tt, :]], ps[:, 2, tt * L:(tt + 1) * L], tt, 4)
                        if tt == 0:
                            do(last)
                    last.then_inc(qp_ok, 1)
                    dve.wait_ge(qp_ok, g + 1)
                    lo(6 + g)
                attention(0)
                dve.wait_ge(s5_stored, 32)
                dve.wait_ge(modb_out, 8)
                dve.memset(modacc[:, 0:D], 0.0)
                dve.memset(modacc[:, 2 * D:], 0.0).then_inc(m1_clear, 1)
                dve.wait_ge(m1_bias, 32)
                for n in range(8):
                    dve.wait_ge(m0_in[n % 4], 16 * (n // 4 + 3))
                    q = late[n // 4][1]
                    last = sum_piece(modacc[:, D * q:D * (q + 1)], m0[n % 4], n % 4)
                    if n % 4 < 3:
                        last.then_inc(m1_used, 1)
                        dve.wait_ge(m1_used, n + 1 - n // 4)
                    else:
                        last.then_inc(m1_sum, 1)
                    if n in (1, 4):
                        lo(8 + n // 4)
                lo(10)
                dve.wait_ge(small2_in, 16 * 13)
                do(dve.tensor_scalar(lam_p, lru_lam, -1.0, None, ALU.mult))
                dve.tensor_tensor(lam_n, lam_p, lru_lam, ALU.max).then_inc(lam_ok, 1)

            def softplus():
                dve.wait_ge(lam_exp, 1)
                do(dve.tensor_scalar(lam_n, lru_lam, -1.0, 0.0, ALU.mult, ALU.max))
                do(dve.tensor_tensor(lam_n, lam_n, lam_p, ALU.add))
                do(dve.tensor_scalar(lam_p, lam_n, 8.0, None, ALU.mult))
                do(dve.tensor_scalar(lam_n, lam_n, -8.0, None, ALU.mult))

            def attention(n):
                sms = (sm, sm2)[n]
                scale = ((NOPE + ROPE) ** -0.5, 128 ** -0.5)[n]
                if n:
                    dve.wait_ge(bias_in, 16)
                for i in range(HEADS + 2):
                    if i < HEADS:
                        h, e = i, HEADS * n + i
                        dve.wait_ge(s_ps, e + 1)
                        if e >= 2:
                            dve.wait_ge(pt_ps, e - 1)
                        s = h % 2
                        bias = relb[:, h, :] if n else mask
                        dve.scalar_tensor_tensor(sms[:, s, 0:P], ps[:, s, 0:P], scale, bias[:, P:2 * P], ALU.mult, ALU.add)
                        dve.scalar_tensor_tensor(sms[:, s, P:3 * P], ps[:, s, P:3 * P], scale, bias[:, 0:L], ALU.mult, ALU.add).then_inc(sm_ok, 1)
                        dve.wait_ge(sm_ok, e + 1)
                        for tt, (a, b) in enumerate(((0, P), (P, 3 * P))):
                            last = dve.tensor_reduce(attm[:, 2 * s + tt:2 * s + tt + 1], sms[:, s, a:b], mybir.AxisListType.X, ALU.max, negate=True)
                        last.then_inc(mx_ok, 1)
                    if 1 <= i <= HEADS:
                        h, e = i - 1, HEADS * n + i - 1
                        s = h % 2
                        dve.wait_ge(exp_ok, e + 1)
                        do(dve.reciprocal(newton[:, 0:2], atts[:, 2 * s:2 * s + 2]))
                        dve.tensor_scalar(sms[:, s, 0:P], sms[:, s, 0:P], newton[:, 0:1], None, ALU.mult)
                        dve.tensor_scalar(sms[:, s, P:3 * P], sms[:, s, P:3 * P], newton[:, 1:2], None, ALU.mult).then_inc(p_ok, 1)
                        dve.wait_ge(p_ok, e + 1)
                    if i >= 2:
                        h, e = i - 2, HEADS * n + i - 2
                        dve.wait_ge(o_hi, e + 1)
                        rest(hlo[:, h, :], ps[:, 4 + h % 2, 0:L], hhi[:, h, :]).then_inc(o_ok, 1)

            def s5():
                c = FIRST["s5"]
                turned("s5")
                for j in range(4):
                    lo(c + 3 + j)
                dve.wait_ge(res_ok, 4)
                dve.wait_ge(u_ok, 4)

                def both(ap):
                    return ap.rearrange("p (k l) -> p k l", k=1).to_broadcast([P, 2, L])

                def out_tile(m):
                    dve.wait_ge(x_used, 4 * m + 4)
                    dve.scalar_tensor_tensor(yT[:, m, :], uT[:, m, :], dskip[:, m:m + 1], ps[:, 2 + m % 2, 0:L], ALU.mult, ALU.add).then_inc(y_ok, 1)

                def phase(i):
                    dve.wait_ge(turn_r, i + 1)
                    r = ph[:, i % 2, 0, :]
                    do(dve.scalar_tensor_tensor(r, iotaf, th_lo[:, i:i + 1], r, ALU.mult, ALU.add))
                    dve.tensor_scalar(r, r, 0.5, -0.5, ALU.min, ALU.max).then_inc(phase_r, 1)

                phase(0)
                phase(1)
                for i in range(PAIRS + 1):
                    if i + 2 < PAIRS:
                        phase(i + 2)
                    if i < PAIRS:
                        s = i % 2
                        dve.wait_ge(bu_ps, i + 1)
                        dve.wait_ge(table_ok, i + 1)
                        cos, sin = tabs[:, i % 3, 0, :], tabs[:, i % 3, 1, :]
                        dve.tensor_tensor(rot_a[:, s, :].rearrange("p (k l) -> p k l", k=2), ps[:, s, :].rearrange("p (k l) -> p k l", k=2), both(cos), ALU.mult)
                        dve.tensor_tensor(rot_b[:, s, 0:L], ps[:, s, L:2 * L], sin, ALU.mult)
                        dve.scalar_tensor_tensor(rot_b[:, s, L:], ps[:, s, 0:L], -1.0, sin, ALU.mult, ALU.mult).then_inc(bu_rot, 1)
                    if i >= 1:
                        e = i - 1
                        s = e % 2
                        dve.wait_ge(w_ps, e + 1)
                        cos, sin = tabs[:, e % 3, 0, :], tabs[:, e % 3, 1, :]
                        for r in range(2):
                            steps.did(dve.tensor_tensor_scan(zst[:, r * L:(r + 1) * L], rho[:, e:e + 1].to_broadcast([P, L]),
                                                             ps[:, 4 + s, r * L:(r + 1) * L], 0.0, ALU.mult, ALU.add))
                        steps.settle()
                        if e >= 2:
                            dve.wait_ge(x_used, e - 1)
                        dve.tensor_tensor(xa[:, s, :].rearrange("p (k l) -> p k l", k=2), zst.rearrange("p (k l) -> p k l", k=2), both(cos), ALU.mult)
                        dve.scalar_tensor_tensor(xb[:, s, 0:L], zst[:, L:], -1.0, sin, ALU.mult, ALU.mult)
                        dve.tensor_tensor(xb[:, s, L:], zst[:, 0:L], sin, ALU.mult).then_inc(x_rot, 1)
                        dve.wait_ge(x_rot, e + 1)
                        if e % 4 == 0 and e:
                            out_tile(e // 4 - 1)
                out_tile(KT - 1)
                for q in range(2):
                    dve.wait_ge(g_hi, q + 1)
                    rest(xlo[:, 4 * q:4 * q + 4, :], yT[:, 4 * q:4 * q + 4, :], xhi[:, 4 * q:4 * q + 4, :]).then_inc(g_ok, 1)
                for j in range(4):
                    dve.wait_ge(sig_ok, j + 1)
                    if j >= 2:
                        dve.wait_ge(zz_lo, j - 1)
                    dve.tensor_tensor(zz[:, j % 2, :], yT[:, 2 * j:2 * j + 2, :].rearrange("p k l -> p (k l)"), sig[:, j % 2, :], ALU.mult).then_inc(zz_ok, 1)
                    lo(c + 7 + j)
                    dve.wait_ge(zz_hi, j + 1)
                    rest(hlo[:, 2 * j:2 * j + 2, :].rearrange("p k l -> p (k l)"), zz[:, j % 2, :],
                         hhi[:, 2 * j:2 * j + 2, :].rearrange("p k l -> p (k l)")).then_inc(zz_lo, 1)
                for j in range(3):
                    lo(c + 11 + j)

            def lru():
                c = FIRST["lru"]
                turned("lru")
                do(dve.memset(xbp[:, :, 0:3], 0.0))
                for j in range(4):
                    dve.wait_ge(lp_ok, j + 1)
                    tiles = (2 * j, 2 * j + 1)
                    for m in tiles:
                        steps.did(dve.tensor_scalar(xcT[:, m, :], xbp[:, m, 3:3 + L], lru_conv[:, 24 + m:25 + m], lru_cb[:, m:m + 1], ALU.mult, ALU.add))
                    for tap in range(3):
                        steps.settle()
                        for m in tiles:
                            ins = dve.scalar_tensor_tensor(xcT[:, m, :], xbp[:, m, tap:tap + L], lru_conv[:, 8 * tap + m:8 * tap + m + 1],
                                                           xcT[:, m, :], ALU.mult, ALU.add)
                            if tap == 2 and m % 4 == 3:
                                ins.then_inc(conv_ok, 1)
                            else:
                                steps.did(ins)
                    lo(c + 3 + j)
                for j in range(4, 7):
                    lo(c + 3 + j)
                for q in range(2):
                    dve.wait_ge(xc_hi, q + 1)
                    rest(xlo[:, 4 * q:4 * q + 4, :], xcT[:, 4 * q:4 * q + 4, :], xhi[:, 4 * q:4 * q + 4, :]).then_inc(xc_ok, 1)
                lo(c + 10)
                hf = lambda ap, q: ap[:, 4 * q:4 * q + 4, :]
                sq_a = work[:, 4096:6144].rearrange("p (m l) -> p m l", m=KT)

                def gated_rest(q):
                    dve.wait_ge(hg_hi, q + 1)
                    rest(hf(hlo, q), hf(aT, q), hf(hhi, q)).then_inc(hg_lo, 1)

                for q in range(2):
                    dve.wait_ge(lg_ok, 4 * q + 4)
                    do(dve.tensor_tensor(hf(iT, q), hf(iT, q), hf(xcT, q), ALU.mult))
                    dve.wait_ge(la_ok, q + 1)
                    do(dve.tensor_tensor(hf(sq_a, q), hf(aT, q), hf(aT, q), ALU.mult))
                    dve.scalar_tensor_tensor(hf(tT, q), hf(sq_a, q), 1.0, hf(tT, q), ALU.add, ALU.mult).then_inc(m2_ok, 1)
                for q in range(2):
                    dve.wait_ge(mult_ok, q + 1)
                    do(dve.tensor_tensor(hf(tT, q), hf(tT, q), hf(iT, q), ALU.mult))
                    for m in range(4 * q, 4 * q + 4):
                        steps.did(dve.tensor_tensor_scan(rT[:, m, :], aT[:, m, :], tT[:, m, :], 0.0, ALU.mult, ALU.add))
                    steps.settle()
                    if q:
                        gated_rest(0)
                    dve.tensor_tensor(hf(aT, q), hf(rT, q), hf(gyT, q), ALU.mult).then_inc(hg_ok, 1)
                gated_rest(1)
                lo(c + 11)
                lo(c + 12)
                for j in range(3):
                    lo(c + 13 + j)

            def kv():
                c = FIRST["kv"]
                turned("kv")
                normed(None, "ffn11")
                for j in range(7):
                    lo(c + 3 + j)
                for tt in range(T):
                    acc_wait("kv", tt)
                    dve.tensor_copy(V2[:, tt, :], acc_tile(tt)).then_inc(acc_free, 1)

            def att():
                c = FIRST["att"]
                turned("att")
                for j in range(4):
                    lo(c + 3 + j)
                attention(1)
                for j in range(3):
                    lo(c + 7 + j)

            acc0 = (GA[:, :], BA[:, :], G[:, 0, :])
            dve.memset(G[:, 0, :], 0.0)
            dve.memset(GA[:, :], 0.0)
            dve.memset(BA[:, :], 0.0).then_inc(acc0_clear, 1)
            dve.wait_ge(csil_ok, 1)
            dve.wait_ge(modb0_in, 48)
            def sum_piece(acc, w, n):
                do(dve.scalar_tensor_tensor(acc, w[:, 0, :], csil[:, 2 * n:2 * n + 1], acc, ALU.mult, ALU.add))
                return dve.scalar_tensor_tensor(acc, w[:, 1, :], csil[:, 2 * n + 1:2 * n + 2], acc, ALU.mult, ALU.add)

            def first_gate(n):
                dve.wait_ge(m0_gate, 16 * max(n + 1, 2))
                last = sum_piece(G[:, 0, :], m0[0 if n == 1 else 2], n)
                if n < 3:
                    last.then_inc(m0_used, 1)
                    dve.wait_ge(m0_used, n + 8)
                else:
                    last.then_inc(mod0_sum, 1)

            for n in range(8):
                dve.wait_ge(m0_in[n % 4], 16 * (n // 4 + 1))
                last = sum_piece(acc0[n // 4], m0[n % 4], n % 4)
                if n < 7:
                    last.then_inc(m0_used, 1)
                    dve.wait_ge(m0_used, n + 1)
                else:
                    last.then_inc(mod0_sum, 1)
            dve.wait_ge(s5p_pool, S5P_ANGLE)
            dve.reciprocal(g0v[:, 8, :], g0v[:, 8, :]).then_inc(s5p_dve, 1)
            lo(0)
            dve.wait_ge(small_in, 64)
            do(dve.tensor_copy(posf, posi.bitcast(I32)))
            ang, turns, red = AR[:, 128:192], AR[:, 192:256], AR[:, 0:64]
            for tt in range(T):
                steps.did(dve.tensor_scalar(ang[:, 32 * tt:32 * tt + 32], invf, posf[:, tt:tt + 1], None, ALU.mult))
            steps.settle()
            do(dve.tensor_scalar(turns, ang, 1 / TWO_PI, MAGIC, ALU.mult, ALU.add))
            do(dve.tensor_scalar(turns, turns, -MAGIC, None, ALU.add))
            do(dve.scalar_tensor_tensor(red, turns, -PI_A, ang, ALU.mult, ALU.add))
            do(dve.scalar_tensor_tensor(red, turns, -PI_B, red, ALU.mult, ALU.add))
            do(dve.scalar_tensor_tensor(red, turns, -PI_C, red, ALU.mult, ALU.add))
            dve.tensor_scalar(red, red, 3.1415925, -3.1415925, ALU.min, ALU.max).then_inc(rope_r, 1)
            dve.wait_ge(x_in, 16)
            dve.wait_ge(modb_out, 4)
            for tt in range(T):
                do(dve.tensor_tensor(H[:, tt, :], X[:, tt, :], A[:, :], ALU.mult))
                dve.tensor_tensor(H[:, tt, :], H[:, tt, :], B[:, :], ALU.add).then_inc(h_ready, 1)
            dve.wait_ge(h_ready, 2)
            dve.memset(spare, 0.0).then_inc(glue_done, 1)
            dve.wait_ge(glue_done, 1)
            lo(1)

            following = {"ffn10": "lru", "lru": "ffn20", "ffn20": "kv", "ffn11": "att", "att": "ffn21", "ffn21": None}
            run = {"mla": mla, "s5": s5, "lru": lru, "kv": kv, "att": att}
            for name in phases:
                if name in run:
                    run[name]()
                else:
                    (mlp if name in MLPS else ffn)(name)
                if name in ("mla", "mlp0", "s5", "mlp1"):
                    ln_glue(name)
                if name == "mla":
                    softplus()
                if name in following:
                    rms_glue(name, following[name])
            dve.memset(spare, 0.0).then_inc(final_ok, 1)

        @block.gpsimd
        def _(pool):
            steps = Steps(pool, pool_step)
            TT, TS = pool.tensor_tensor, pool.tensor_scalar

            def do(ins):
                steps.did(ins)
                steps.settle()

            def axpy(x, a, y, tmp, op=ALU.add):
                do(TS(tmp, x, a, 0.0, ALU.mult, ALU.add))
                return lambda dst: TT(dst, tmp, y, op)

            steps.did(pool.memset(ones[:, :], 1.0))
            for e, value in ((eps_ln, 1e-5), (eps_rms, 1e-6), (eps_rms4, 4e-6)):
                steps.did(pool.memset(e, value))
            steps.did(pool.memset(ident[:, :], 0.0))
            steps.did(pool.memset(mask[:, :], 0.0))
            steps.did(pool.memset(mod[:, 1024:5120], 0.0))
            steps.settle()
            steps.did(pool.affine_select(out=ident[:, :], in_=ident[:, :], compare_op=ALU.not_equal, fill=1.0, base=0,
                                         pattern=[[-1, P]], channel_multiplier=1))
            pool.affine_select(out=mask[:, P:], in_=mask[:, P:], compare_op=ALU.is_ge, fill=NEG, base=0,
                               pattern=[[-1, P]], channel_multiplier=1).then_inc(const_ok, 1)

            v = lambda k: g0v[:, k, :]
            pool.wait_ge(s5_in, 16 * 21)
            pool.tensor_copy(a_rows[:, 2, :].rearrange("q (g p) -> q g p", g=2),
                             ldt_rows.rearrange("q (g o) -> q g o", o=1).to_broadcast([PAIRS, 2, 64])).then_inc(s5p_pool, 1)
            pool.wait_ge(s5p_act, 2)
            steps.did(TT(v(3), v(0), v(2), ALU.mult))
            steps.did(TT(v(4), v(1), v(2), ALU.mult))
            steps.did(TT(v(8), v(0), v(0), ALU.mult))
            do(TT(v(9), v(1), v(1), ALU.mult))
            steps.did(TT(v(8), v(8), v(9), ALU.add))
            do(TS(v(10), v(4), 1 / TWO_PI, MAGIC, ALU.mult, ALU.add))
            do(TS(v(10), v(10), -MAGIC, 1.0, ALU.add, ALU.mult))
            do(axpy(v(10), -PI_A, v(4), v(11))(v(5)))
            do(axpy(v(10), -PI_B, v(5), v(11))(v(5)))
            do(axpy(v(10), -PI_C, v(5), v(11))(v(5)))
            TS(v(5), v(5), 3.1415925, -3.1415925, ALU.min, ALU.max).then_inc(s5p_pool, 1)
            pool.wait_ge(s5p_pool, S5P_ANGLE)
            do(TS(th, v(5), 1 / TWO_PI, 0.0, ALU.mult, ALU.add))
            do(TS(th_hi, th, 192.0, 1.0, ALU.add, ALU.mult))
            do(TS(th_hi, th_hi, -192.0, 1.0, ALU.add, ALU.mult))
            do(axpy(th_hi, -PI_A, v(5), v(11))(th_lo))
            do(axpy(th_hi, -(PI_B + PI_C), th_lo, v(11))(th_lo))
            do(TS(th_lo, th_lo, 1 / TWO_PI, 0.0, ALU.mult, ALU.add))
            pool.wait_ge(s5p_act, 6)
            pool.wait_ge(s5p_dve, 1)
            steps.did(TT(v(9), rho, v(7), ALU.mult))
            do(TT(v(10), rho, v(6), ALU.mult))
            do(TS(v(9), v(9), -1.0, 1.0, ALU.add, ALU.mult))
            steps.did(TT(v(11), v(9), v(0), ALU.mult))
            steps.did(TT(v(12), v(10), v(1), ALU.mult))
            steps.did(TT(v(13), v(10), v(0), ALU.mult))
            do(TT(v(14), v(9), v(1), ALU.mult))
            steps.did(TT(v(11), v(11), v(12), ALU.add))
            do(TT(v(13), v(13), v(14), ALU.subtract))
            steps.did(TT(v(11), v(11), v(8), ALU.mult))
            do(TT(v(13), v(13), v(8), ALU.mult))
            wide = lambda k: v(k).rearrange("p (q o) -> p q o", o=1).to_broadcast([P, PAIRS, 16])
            for r, (c0, c1, op) in enumerate(((11, 13, ALU.subtract), (13, 11, ALU.add))):
                steps.did(TT(bu1, b_in[:, 0], wide(c0), ALU.mult))
                do(TT(bu2, b_in[:, 1], wide(c1), ALU.mult))
                for g in range(2):
                    q = slice(64 * g, 64 * g + 64)
                    last = TT(b_dg[q, :, r, :, 16 * g:16 * g + 16], bu1[q].rearrange("p (m i) c -> p m i c", i=4),
                              bu2[q].rearrange("p (m i) c -> p m i c", i=4), op)
                    if r and g:
                        last.then_inc(s5p_pool, 1)
                    else:
                        do(last)

            pieces = [(m, q, kk) for m in range(1, 4) for q in range(3) if (m, q) not in late for kk in range(4)]
            index = {p: n for n, p in enumerate(pieces)}

            def fetch(n):
                m, q, kk = pieces[n]
                pool.dma_start(modw[:, n % 2, :].rearrange("p (k n) -> p k n", k=2),
                               mod_w[m].rearrange("(k p) n -> p k n", p=P)[:, 2 * kk:2 * kk + 2, D * q:D * (q + 1)]).then_inc(modw_in[n % 2], 16)

            def third(m, q, ahead):
                acc = modacc[:, D * q:D * (q + 1)]
                if m >= 2:
                    pool.wait_ge(modb_out, (8 if m == 2 else 14) + 2 * q)
                do(pool.memset(acc, 0.0))
                pool.dma_start(acc[0:1, :], mod_b[m][D * q:D * (q + 1)].rearrange("(o n) -> o n", o=1)).then_inc(modb_in, 16)
                thirds[0] += 1
                pool.wait_ge(modb_in, 16 * thirds[0])
                for kk in range(4):
                    n = index[(m, q, kk)]
                    if n + 1 < len(pieces) and (kk < 3 or ahead):
                        fetch(n + 1)
                    pool.wait_ge(modw_in[n % 2], 16 * (n // 2 + 1))
                    for k in range(2):
                        w = modw[:, n % 2, D * k:D * (k + 1)]
                        last = axpy(w, csil[:, 2 * kk + k:2 * kk + k + 1], acc, w)(acc)
                        if kk == 3 and k == 1:
                            last.then_inc(mod_sum, 1)
                            pool.wait_ge(mod_sum, thirds[0])
                        else:
                            do(last)

            thirds = [0]

            def vectors(k):
                pool.wait_ge(modb_out, (10, 18, 24)[k - 1])
                row_wait(pool, f"lg{k}")
                row_wait(pool, f"lb{k}")
                if k == 3:
                    pool.wait_ge(x_rot, PAIRS)
                tmp = modacc[:, D:2 * D]
                steps.did(TT(tmp, BA[:, :], A[:, :], ALU.mult))
                steps.settle()
                steps.did(TT(B[:, :], B[:, :], tmp, ALU.add))
                steps.did(TT(A[:, :], A[:, :], GA[:, :], ALU.mult))
                steps.settle()
                steps.did(TS(GA[:, :], GA[:, :], ALPHA, 0.0, ALU.mult, ALU.add))
                steps.settle()
                TS(BA[:, :], BA[:, :], ALPHA, 0.0, ALU.mult, ALU.add).then_inc(vec_done, 1)
                pool.wait_ge(vec_done, k)

            def residual(k):
                for tt in range(T):
                    pool.wait_ge(ln_stats, 2 * (k - 1) + tt + 1)
                    do(TS(X[:, tt, :], Y[:, tt, :], rsq[:, tt:tt + 1], nmr[:, tt:tt + 1], ALU.mult, ALU.add))
                    do(TT(X[:, tt, :], X[:, tt, :], GA[:, :], ALU.mult))
                    TT(X[:, tt, :], X[:, tt, :], BA[:, :], ALU.add).then_inc(res_ok, 1)

            def s5_phases():
                pool.wait_ge(modb_out, 24)
                count = ph[:, 0, 0, :].bitcast(I32)
                do(pool.iota(count, pattern=[[1, L]], base=0, channel_multiplier=0))
                do(pool.tensor_copy(iotaf, count))
                for i in range(PAIRS):
                    s = i % 2
                    if i >= 2:
                        pool.wait_ge(table_ok, i - 1)
                    r, k = ph[:, s, 0, :], ph[:, s, 1, :]
                    do(TS(k, iotaf, th[:, i:i + 1], MAGIC, ALU.mult, ALU.add))
                    do(TS(k, k, -MAGIC, 1.0, ALU.add, ALU.mult))
                    axpy(iotaf, th_hi[:, i:i + 1], k, r, ALU.subtract)(r).then_inc(turn_r, 1)

            def relative_bias():
                pool.wait_ge(x_rot, PAIRS)
                pool.dma_start(rel, t["rel_bias_2"]).then_inc(rel_in, 16)
                pool.wait_ge(rel_in, 16)
                b = buckets()[::-1]
                cuts = [0] + [m for m in range(1, L) if b[m] != b[m - 1]] + [L]
                for m0, m1 in zip(cuts, cuts[1:]):
                    steps.did(pool.tensor_copy(vrev[:, m0:m1], rel[:, int(b[m0]):int(b[m0]) + 1].to_broadcast([HEADS, m1 - m0])))
                steps.settle()
                pool.memset(vrev[:, L:], NEG).then_inc(vrev_ok, 1)
                pool.wait_ge(vrev_ok, 1)
                pool.dma_start(bias_store[:, 0:P * 385].rearrange("h (q m) -> h q m", m=385)[:, :, 0:384],
                               vrev.rearrange("h (o m) -> h o m", o=1).to_broadcast([HEADS, P, 384])).then_inc(bias_stored, 16)
                pool.wait_ge(bias_stored, 16)

            def load_bias():
                pool.wait_ge(hg_lo, 2)
                src = bias_store[:, P - 1:P - 1 + P * 384].rearrange("h (q m) -> q h m", m=384)[:, :, 0:L]
                pool.dma_start(relb, src).then_inc(bias_in, 16)

            pool.wait_ge(s5t_ok, 8)
            pool.wait_ge(s5_stored, 32)
            pool.wait_ge(csil_ok, 1)
            pool.wait_ge(glue_done, 1)
            TS(X[:, :, :].rearrange("p t d -> p (t d)"), X[:, :, :].rearrange("p t d -> p (t d)"), ALPHA, 0.0, ALU.mult, ALU.add).then_inc(x_scaled, 1)
            fetch(0)
            third(1, 0, True)
            third(1, 1, True)
            vectors(1)
            third(2, 1, True)
            residual(1)
            third(2, 2, True)
            third(3, 0, True)
            vectors(2)
            third(3, 1, True)
            third(3, 2, False)
            residual(2)
            s5_phases()
            vectors(3)
            residual(3)
            relative_bias()
            load_bias()


def kernel(**inputs):
    import concourse.bacc as bacc
    from concourse.bass_utils import run_bass_kernel_spmd

    nc = bacc.Bacc("TRN2", target_bir_lowering=False, num_devices=1)
    arrays = {name: np.ascontiguousarray(a) for name, a in inputs.items()}
    arrays["inv_freq"] = (10000.0 ** (-np.arange(0, ROPE, 2, dtype=np.float32) / ROPE)).astype(np.float32)
    arrays = {f"in_{name}": a for name, a in arrays.items()}
    t = {name[3:]: nc.dram_tensor(name, a.shape, mybir.dt.from_np(a.dtype), kind="ExternalInput").ap() for name, a in arrays.items()}
    out = nc.dram_tensor("out", (1, L, D), F32, kind="ExternalOutput").ap()
    build_program(nc, t, out)
    return run_bass_kernel_spmd(nc, [arrays], core_ids=[0]).results[0]["out"]
```
